# Optimizing a Trainium2 kernel written in Bass

```python
import math
import jax, jax.numpy as jnp
from jax import lax
import numpy as np

D_MODEL = 1024
BATCH = 1
SEQ = 256
DEPTH = 2

CHUNK = 64
N_MIXERS = 2
N_HEADS = 16
HEAD_DIM = D_MODEL // N_HEADS
IDX_HEADS = 8
IDX_DIM = 64
TOPK_MAX = 256
Q_BLOCK = 128
ATTN_SPLITS = (D_MODEL, 2 * D_MODEL, 3 * D_MODEL,
               3 * D_MODEL + IDX_HEADS * IDX_DIM,
               3 * D_MODEL + IDX_HEADS * IDX_DIM + IDX_DIM)
ATTN_PROJ = 3 * D_MODEL + IDX_HEADS * IDX_DIM + IDX_DIM + IDX_HEADS
SSM_WIDTH = D_MODEL
SSM_GROUP = 16
SSM_GROUPS = SSM_WIDTH // SSM_GROUP
SSM_STATE = 64
SSM_GROUP_BLOCK = 16
D_FF = 2816
CONV_WIDTH = 3
EPS = 1e-6

kernel_name = 'hybrid_dsa_s5_convffn_adaln'

def rms_norm(x, g):
    x32 = x.astype(jnp.float32)
    y = x32 * lax.rsqrt(jnp.mean(x32 * x32, axis=-1, keepdims=True) + EPS)
    return (y * g.astype(jnp.float32)).astype(x.dtype)

def modulate(h, shift, scale):
    return h * (1.0 + scale[:, None, :]) + shift[:, None, :]

def alibi_slopes(n_heads):
    return 2.0 ** (-8.0 * jnp.arange(1, n_heads + 1, dtype=jnp.float32) / n_heads)

def dsa_attention(h, w_in, w_out):
    bsz, seq, _ = h.shape
    proj = h @ w_in
    q, k, v, qi, ki, wi = jnp.split(proj, ATTN_SPLITS, axis=-1)
    q = q.reshape(bsz, seq, N_HEADS, HEAD_DIM)
    k = k.reshape(bsz, seq, N_HEADS, HEAD_DIM)
    v = v.reshape(bsz, seq, N_HEADS, HEAD_DIM)
    qi = qi.reshape(bsz, seq, IDX_HEADS, IDX_DIM)
    wi = wi * (IDX_HEADS ** -0.5)
    n_keep = min(TOPK_MAX, seq // 4)
    n_blk = seq // Q_BLOCK
    pos = jnp.arange(seq)
    key_chunk = pos // CHUNK
    slopes = alibi_slopes(N_HEADS)

    def to_blocks(a):
        return jnp.moveaxis(a.reshape(bsz, n_blk, Q_BLOCK, *a.shape[2:]), 1, 0)

    def one_block(args):
        qb, qib, wb, tb = args
        logits = jnp.einsum('bqhd,bsd->bqhs', qib, ki) * (IDX_DIM ** -0.5)
        score = jnp.einsum('bqh,bqhs->bqs', wb, jax.nn.relu(logits)).astype(jnp.float32)
        q_chunk = tb // CHUNK
        admissible = key_chunk[None, :] <= q_chunk[:, None]
        score = jnp.where(admissible[None], score, -jnp.inf)
        _, idx = lax.top_k(score, n_keep)
        kg = jax.vmap(lambda kk, ii: kk[ii])(k, idx)
        vg = jax.vmap(lambda vv, ii: vv[ii])(v, idx)
        s_att = jnp.einsum('bqhd,bqkhd->bhqk', qb, kg).astype(jnp.float32) * (HEAD_DIM ** -0.5)
        dist = jnp.abs(tb[None, :, None] - idx).astype(jnp.float32)
        s_att = s_att - slopes[None, :, None, None] * dist[:, None]
        valid = (idx // CHUNK) <= q_chunk[None, :, None]
        s_att = jnp.where(valid[:, None], s_att, -jnp.inf)
        p = jax.nn.softmax(s_att, axis=-1).astype(vg.dtype)
        return jnp.einsum('bhqk,bqkhd->bqhd', p, vg)

    out = lax.map(one_block, (to_blocks(q), to_blocks(qi), to_blocks(wi),
                              pos.reshape(n_blk, Q_BLOCK)))
    out = jnp.moveaxis(out, 0, 1).reshape(bsz, seq, D_MODEL)
    return out @ w_out

def _complex_affine_combine(e1, e2):
    a1r, a1i, b1r, b1i = e1
    a2r, a2i, b2r, b2i = e2
    ar = a2r * a1r - a2i * a1i
    ai = a2r * a1i + a2i * a1r
    br = a2r * b1r - a2i * b1i + b2r
    bi = a2r * b1i + a2i * b1r + b2i
    return (ar, ai, br, bi)

def _s5_group_block(args):
    u, lam_re, lam_im, log_dt, b_re, b_im, c_re, c_im, d_skip = args
    dt = jnp.exp(log_dt)[:, None]
    mag = jnp.exp(lam_re * dt)
    a_re = mag * jnp.cos(lam_im * dt)
    a_im = mag * jnp.sin(lam_im * dt)
    den = lam_re * lam_re + lam_im * lam_im
    coef_re = ((a_re - 1.0) * lam_re + a_im * lam_im) / den
    coef_im = (a_im * lam_re - (a_re - 1.0) * lam_im) / den
    bb_re = coef_re[..., None] * b_re - coef_im[..., None] * b_im
    bb_im = coef_re[..., None] * b_im + coef_im[..., None] * b_re
    bu_re = jnp.einsum('bsgc,gpc->bsgp', u, bb_re)
    bu_im = jnp.einsum('bsgc,gpc->bsgp', u, bb_im)
    a_re_t = jnp.broadcast_to(a_re, bu_re.shape)
    a_im_t = jnp.broadcast_to(a_im, bu_im.shape)
    _, _, h_re, h_im = lax.associative_scan(
        _complex_affine_combine, (a_re_t, a_im_t, bu_re, bu_im), axis=1)
    y = (jnp.einsum('bsgp,gcp->bsgc', h_re, c_re)
         - jnp.einsum('bsgp,gcp->bsgc', h_im, c_im)
         + d_skip * u)
    return y

def s5_layer(h, w_in, lam_re, lam_im, log_dt, b_re, b_im, c_re, c_im, d_skip, w_glu):
    bsz, seq, _ = h.shape
    n_gb = SSM_GROUPS // SSM_GROUP_BLOCK
    u = (h @ w_in).astype(jnp.float32).reshape(bsz, seq, n_gb, SSM_GROUP_BLOCK, SSM_GROUP)
    u = jnp.moveaxis(u, 2, 0)

    def grp(p):
        return p.astype(jnp.float32).reshape(n_gb, SSM_GROUP_BLOCK, *p.shape[1:])

    y = lax.map(_s5_group_block, (u, grp(lam_re), grp(lam_im), grp(log_dt), grp(b_re),
                                   grp(b_im), grp(c_re), grp(c_im), grp(d_skip)))
    y = jnp.moveaxis(y, 0, 2).reshape(bsz, seq, SSM_WIDTH)
    y = jax.nn.gelu(y).astype(h.dtype)
    val, gate = jnp.split(y @ w_glu, 2, axis=-1)
    return val * jax.nn.sigmoid(gate)

def conv_ffn(h, w_up, conv_w, conv_b, w_down):
    z = h @ w_up
    n_ch = z.shape[-1]
    z = lax.conv_general_dilated(
        z, conv_w[:, None, :].astype(z.dtype), window_strides=(1,),
        padding=[(CONV_WIDTH - 1, 0)], dimension_numbers=('NWC', 'WIO', 'NWC'),
        feature_group_count=n_ch) + conv_b
    val, gate = jnp.split(z, 2, axis=-1)
    return (jax.nn.silu(gate) * val) @ w_down

def setup_inputs(seed: int = 0) -> dict:
    key = jax.random.key(seed)
    ks = jax.random.split(key, 24)
    f32 = jnp.float32
    n_attn = (DEPTH + 1) // 2
    n_ssm = DEPTH // 2
    G, P, GS = SSM_GROUPS, SSM_STATE, SSM_GROUP

    def nrm(k, shape, std):
        return std * jax.random.normal(k, shape, f32)

    lam_im_base = math.pi * jnp.arange(P, dtype=f32)
    return {
        'x': nrm(ks[0], (BATCH, SEQ, D_MODEL), 1.0),
        'c': nrm(ks[1], (BATCH, D_MODEL), 1.0),
        'mod_w': nrm(ks[2], (DEPTH, D_MODEL, 6 * D_MODEL), 0.5 * D_MODEL ** -0.5),
        'mod_b': nrm(ks[3], (DEPTH, 6 * D_MODEL), 0.02),
        'norm_mix_g': 1.0 + nrm(ks[4], (DEPTH, D_MODEL), 0.02),
        'norm_ffn_g': 1.0 + nrm(ks[5], (DEPTH, D_MODEL), 0.02),
        'attn_w_in': nrm(ks[6], (n_attn, D_MODEL, ATTN_PROJ), D_MODEL ** -0.5),
        'attn_w_out': nrm(ks[7], (n_attn, D_MODEL, D_MODEL), D_MODEL ** -0.5),
        'ssm_w_in': nrm(ks[8], (n_ssm, D_MODEL, SSM_WIDTH), D_MODEL ** -0.5),
        'ssm_lam_re': -0.5 + nrm(ks[9], (n_ssm, G, P), 0.01),
        'ssm_lam_im': lam_im_base + nrm(ks[10], (n_ssm, G, P), 0.01),
        'ssm_log_dt': jax.random.uniform(ks[11], (n_ssm, G), f32,
                                         minval=math.log(1e-3), maxval=math.log(1e-1)),
        'ssm_b_re': nrm(ks[12], (n_ssm, G, P, GS), (2.0 * GS) ** -0.5),
        'ssm_b_im': nrm(ks[13], (n_ssm, G, P, GS), (2.0 * GS) ** -0.5),
        'ssm_c_re': nrm(ks[14], (n_ssm, G, GS, P), 0.5),
        'ssm_c_im': nrm(ks[15], (n_ssm, G, GS, P), 0.5),
        'ssm_d': nrm(ks[16], (n_ssm, G, GS), 1.0),
        'ssm_w_glu': nrm(ks[17], (n_ssm, SSM_WIDTH, 2 * D_MODEL), SSM_WIDTH ** -0.5),
        'ffn_w_up': nrm(ks[18], (DEPTH, D_MODEL, 2 * D_FF), D_MODEL ** -0.5),
        'ffn_conv_w': nrm(ks[19], (DEPTH, CONV_WIDTH, 2 * D_FF), CONV_WIDTH ** -0.5),
        'ffn_conv_b': nrm(ks[20], (DEPTH, 2 * D_FF), 0.02),
        'ffn_w_down': nrm(ks[21], (DEPTH, D_FF, D_MODEL), D_FF ** -0.5),
        'final_g': 1.0 + nrm(ks[22], (D_MODEL,), 0.02),
    }

def reference(x, c, mod_w, mod_b, norm_mix_g, norm_ffn_g, attn_w_in, attn_w_out,
              ssm_w_in, ssm_lam_re, ssm_lam_im, ssm_log_dt, ssm_b_re, ssm_b_im,
              ssm_c_re, ssm_c_im, ssm_d, ssm_w_glu, ffn_w_up, ffn_conv_w, ffn_conv_b,
              ffn_w_down, final_g):
    cond = jax.nn.silu(c)
    for i in range(DEPTH):
        mod = cond @ mod_w[i] + mod_b[i]
        sh1, sc1, g1, sh2, sc2, g2 = jnp.split(mod, 6, axis=-1)
        h = modulate(rms_norm(x, norm_mix_g[i]), sh1, sc1)
        j = i // N_MIXERS
        if i % N_MIXERS == 0:
            y = dsa_attention(h, attn_w_in[j], attn_w_out[j])
        else:
            y = s5_layer(h, ssm_w_in[j], ssm_lam_re[j], ssm_lam_im[j], ssm_log_dt[j],
                         ssm_b_re[j], ssm_b_im[j], ssm_c_re[j], ssm_c_im[j], ssm_d[j],
                         ssm_w_glu[j])
        x = x + g1[:, None, :] * y
        h = modulate(rms_norm(x, norm_ffn_g[i]), sh2, sc2)
        x = x + g2[:, None, :] * conv_ffn(h, ffn_w_up[i], ffn_conv_w[i], ffn_conv_b[i],
                                          ffn_w_down[i])
    return rms_norm(x, final_g)


_drawn_inputs = setup_inputs


def setup_inputs(seed=0):
    import zlib

    import numpy as np

    out = dict(_drawn_inputs(seed))
    spreads = {}
    factors = {'norm_mix_g': 2.717,
     'norm_ffn_g': 6.643,
     'ssm_lam_re': 200.0,
     'ffn_conv_b': 7.192,
     'final_g': 24.568,
     'ssm_lam_im': 64.0,
     'ssm_log_dt': 64.0,
     'ssm_b_re': 64.0,
     'ssm_b_im': 64.0,
     'ssm_c_re': 64.0,
     'ssm_c_im': 64.0}
    for name, (base, spread) in spreads.items():
        noise = np.random.default_rng([zlib.crc32(name.encode()), seed]).standard_normal(out[name].shape)
        drawn = base * np.exp(spread * noise) if base else spread * noise
        out[name] = __import__('jax').numpy.asarray(drawn.astype(out[name].dtype))
    for name, factor in factors.items():
        out[name] = (out[name] * factor).astype(out[name].dtype)
    return out
```

```python
from contextlib import ExitStack

import numpy as np

import concourse.bass as bass
from concourse import mybir
from concourse.bass import ds

F32 = mybir.dt.float32
F32R = mybir.dt.float32r
ALU = mybir.AluOpType
ACT = mybir.ActivationFunctionType
AX = mybir.AxisListType

P = 128
D = 1024
KT = D // P
T = 256
HEADS, HD = 16, 64
PAIRS = HEADS // 2
IH = 8
KEEP = T // 4
FF = 2816
FT = FF // P
EPS = 1e-6

RAW, SPL = 6, 3
N_IN = 30
N_OUT = KT
N_FFN = 3 * FT
N_SIN = KT
N_GLU = 2 * KT
W_IN = 0
W_OUT = W_IN + N_IN
W_FFN0 = W_OUT + N_OUT
W_SIN = W_FFN0 + N_FFN
W_GLU = W_SIN + N_SIN
W_FFN1 = W_GLU + N_GLU
N_SLOTS = W_FFN1 + N_FFN
S_KI, S_WI, S_QI, S_Q, S_K, S_V = 0, 1, 2, 6, 14, 22

CH = 6 * D // 512
MS = 4

LCH = 4
NJ = T // LCH
PR = 32
TWO_PI = 6.283185307179586
ROUND = 12582912.0
C1, C2 = 6.28125, 0.0019350051879882812
C3 = TWO_PI - C1 - C2

NEG = -3.0e38
TAKEN = -3.3e38
MASKED = -1.0e30

PRM = ["lr", "li", "ldt", "dt", "th", "mag", "sin", "cos", "are", "aim", "cre", "cim", "rho", "frac",
       "t0", "t1", "t2", "t3"]
PRM_IN = 3


def build(nc, t):
    with ExitStack() as ctx:
        def sb(name, shape, dt=F32):
            return ctx.enter_context(nc.sbuf_tensor(name, shape, dt))

        def sem(name):
            return ctx.enter_context(nc.semaphore(name))

        x = sb("x", [P, KT, T])
        hh = sb("hh", [P, KT, T], F32R)
        hl = sb("hl", [P, KT, T], F32R)
        raw = sb("raw", [P, RAW, 1024])
        whi = sb("whi", [P, SPL, 1024], F32R)
        wlo = sb("wlo", [P, SPL, 1024], F32R)
        mraw = sb("mraw", [P, MS, 1024])
        gm = sb("gm", [P, 512])
        tmp8 = sb("tmp8", [P, KT * T])
        ffn = sb("ffn", [P, KT * T])
        ah = sb("ah", [P, 2, T], F32R)
        al = sb("al", [P, 2, T], F32R)
        arena = sb("arena", [P, 22528])
        ident = sb("ident", [P, P])
        ones = sb("ones", [P, P])
        craw = sb("craw", [P, KT])
        cond = sb("cond", [P, KT])
        prm = sb("prm", [P, len(PRM), PR])
        conv = sb("conv", [P, 2, 4, 2 * FT])
        modc = sb("modc", [P, 2 * 48])
        modb = sb("modb", [P, 2 * 48])
        gains = sb("gains", [P, 5, KT])
        amul = sb("amul", [P, 4, KT])
        dcol = sb("dcol", [P, KT])
        rstd = sb("rstd", [P, T])
        jrow = sb("jrow", [P, NJ])
        slope = sb("slope", [P, HEADS])
        epsc = sb("epsc", [P, 1])
        zrow = sb("zrow", [1, 512], mybir.dt.bfloat16)

        tmp = tmp8[:].rearrange("p (k t) -> p k t", k=KT)

        def carve(cursor, n):
            a = arena[:, cursor[0]:cursor[0] + n]
            cursor[0] += n
            return a

        cur = [0]
        qkv = carve(cur, N_IN * T).rearrange("p (n t) -> p n t", n=N_IN)
        stage = carve(cur, 2 * 3 * T).rearrange("p (a n t) -> p a n t", a=2, n=3)
        rbuf = carve(cur, 8 * T).rearrange("p (b h t) -> p b h t", b=4, h=2)
        scr = carve(cur, 384)
        msk = carve(cur, 384)
        ndist = carve(cur, 384)
        bm = carve(cur, 4 * 384).rearrange("p (a e t) -> p a e t", a=2, e=2)
        sp = carve(cur, 4 * 384).rearrange("p (a e t) -> p a e t", a=2, e=2)
        pt = carve(cur, 4 * 384).rearrange("p (a e t) -> p a e t", a=2, e=2)
        vsb = carve(cur, 2 * T).rearrange("p (a k d) -> p a k d", a=2, k=2)
        max8 = carve(cur, 16).rearrange("p (q n) -> p q n", q=2)
        wit = carve(cur, 16).rearrange("p (q n) -> p q n", q=2)
        nmx = carve(cur, 8).rearrange("p (a n) -> p a n", a=2)
        rs = carve(cur, 8).rearrange("p (a n) -> p a n", a=2)
        ri = carve(cur, 8).rearrange("p (a n) -> p a n", a=2)
        cur = [0]
        bpow = carve(cur, 8192).rearrange("p (r n l c) -> p r n l c", r=2, n=PR, l=LCH)
        cpow = carve(cur, 8192).rearrange("p (k r n) -> p k r n", k=4, r=2)
        tab = carve(cur, 4096)
        tpool = carve(cur, 2048)
        t1, t2 = tpool[:, 0:1024], tpool[:, 1024:2048]
        rot1 = tpool[:, 0:512].rearrange("p (r q j) -> p r q j", r=2, q=4)
        rot2 = tpool[:, 512:1024].rearrange("p (r q j) -> p r q j", r=2, q=4)
        hst = tpool[:, 1024:1536].rearrange("p (r q j) -> p r q j", r=2, q=4)
        yv = tpool[:, 1536:2048].rearrange("p (a t) -> p a t", a=2)
        yg = ffn[:].rearrange("p (m t) -> p m t", m=KT)
        kbd = mraw[:].rearrange("p a (m l n) -> p (a m) l n", m=2, l=LCH)
        tcos, tsin = tab[:, 0:2048], tab[:, 2048:4096]
        tcos_v = tcos.rearrange("p (n j) -> p n j", j=NJ)
        tsin_v = tsin.rearrange("p (n j) -> p n j", j=NJ)
        va = tmp8[:, 0:512].rearrange("p (q r j) -> p q r j", q=4, r=2)
        vb = tmp8[:, 512:1024].rearrange("p (q r j) -> p q r j", q=4, r=2)
        ust = tmp8[:, 1024:1536].rearrange("p (a q j) -> p a q j", a=2, q=4)
        g2 = tmp8[:, 1536:2048].rearrange("p (r q j) -> p r q j", r=2, q=4)
        bpow_r = bpow.rearrange("p r n l c -> p r (n l c)")
        u = ffn[:].rearrange("p (m j l) -> p m j l", m=KT, l=LCH)
        cb = ffn[:, 0:1024].rearrange("p (a e t) -> p a e t", a=2, e=2)
        sg = ffn[:, 1024:1536].rearrange("p (a t) -> p a t", a=2)
        ab = ffn[:, 1536:2048].rearrange("p (a t) -> p a t", a=2)

        qkv_f = arena[:, 0:N_IN * T]
        hh_f = hh[:].rearrange("p k t -> p (k t)")
        hl_f = hl[:].rearrange("p k t -> p (k t)")

        def pr(name):
            return prm[:, PRM.index(name), :]

        acc = ctx.enter_context(nc.psum_tensor("acc", [P, 4, 512], F32))
        up = ctx.enter_context(nc.psum_tensor("up", [P, 2, 512], F32))
        gv = ctx.enter_context(nc.psum_tensor("gv", [P, 512], F32))
        misc = ctx.enter_context(nc.psum_tensor("misc", [P, 512], F32))

        cond_in = sem("cond_in")
        small_in = sem("small_in")
        x_in = sem("x_in")
        w_loaded = [sem(f"w_loaded{j}") for j in range(RAW)]
        m_loaded = [sem(f"m_loaded{j}") for j in range(MS)]
        hi_ready, lo_ready, slot_used = sem("hi_ready"), sem("lo_ready"), sem("slot_used")
        mod_used = sem("mod_used")
        gm_ready = sem("gm_ready")
        cols_done = sem("cols_done")
        mod_col = sem("mod_col")
        amul_ready = sem("amul_ready")
        set_up = sem("set_up")
        cond_ready = sem("cond_ready")
        prm_v, prm_a = sem("prm_v"), sem("prm_a")
        x_upd = sem("x_upd")
        sq_ready, ssum, rt_ready, rstd_ready, hp_ready = (
            sem("sq_ready"), sem("ssum"), sem("rt_ready"), sem("rstd_ready"), sem("hp_ready"))
        act_hi, act_lo = sem("act_hi"), sem("act_lo")
        qkv_ready = sem("qkv_ready")
        idx_done, idx_relu, idx_acc = sem("idx_done"), sem("idx_relu"), sem("idx_acc")
        wit_ready = sem("wit_ready")
        sel = sem("sel")
        stage_ready, s_done, v_ready, bias_ready, sp_ready, mx_ready = (
            sem("stage_ready"), sem("s_done"), sem("v_ready"), sem("bias_ready"), sem("sp_ready"), sem("mx_ready"))
        exp_done, ri_ready, p_ready, tr_done, tr_out, pv_done = (
            sem("exp_done"), sem("ri_ready"), sem("p_ready"), sem("tr_done"), sem("tr_out"), sem("pv_done"))
        tap, conv_s, sg_ready, am, a_hi, a_lo = (
            sem("tap"), sem("conv_s"), sem("sg_ready"), sem("am"), sem("a_hi"), sem("a_lo"))
        ssm_in = sem("ssm_in")
        pw = sem("pw")
        k_done, k_out = sem("k_done"), sem("k_out")
        bt_done, bt_act, bt_dve = sem("bt_done"), sem("bt_act"), sem("bt_dve")
        kz = sem("kz")
        st_done, st_ready = sem("st_done"), sem("st_ready")
        tab_ready = sem("tab_ready")
        u_ready = sem("u_ready")
        v_done, v_read, g_ready, g2_ready, rot_s, h_ready = (
            sem("v_done"), sem("v_read"), sem("g_ready"), sem("g2_ready"), sem("rot_s"), sem("h_ready"))
        y_done, yv_ready, yg_ready = sem("y_done"), sem("yv_ready"), sem("yg_ready")
        sig_ready, glu_s = sem("sig_ready"), sem("glu_s")
        fin_ready, out_done = sem("fin_ready"), sem("out_done")

        N_SMALL = 11
        N_SSM = 4

        block = ctx.enter_context(nc.Block())

        @block.sync
        def _(sp_):
            def load_w(n, i=0, free=True):
                if free:
                    sp_.wait_ge(lo_ready, n + RAW * i - RAW + 1)
                sp_.dma_start(raw[:, n % RAW, :], t["w"][n + RAW * i, :, :]).then_inc(w_loaded[n % RAW], 16)

            def load_m(c, i=0):
                for s in range(MS):
                    if not (isinstance(c, int) and isinstance(i, int) and c + i == 0):
                        sp_.wait_ge(mod_used, (c + i - 1) * MS + s + 1)
                    sp_.dma_start(mraw[:, s, :], t["mw"][(c + i) * MS + s, :, :]).then_inc(m_loaded[s], 16)

            sp_.dma_start(craw[:], t["cond"]).then_inc(cond_in, 16)
            sp_.dma_start(modb[:], t["modb"]).then_inc(small_in, 16)
            load_m(0)
            for k in range(0, KT, 2):
                sp_.dma_start(x[:, k:k + 2, :], t["x"][:, k:k + 2, :]).then_inc(x_in, 16)
            load_m(1)
            for dst, name in ((ident[:], "ident"), (ones[:], "ones"), (prm[:, 0:PRM_IN, :], "prm"),
                              (conv[:], "conv"), (gains[:], "gains"), (dcol[:], "dcol"), (jrow[:], "jrow"),
                              (slope[:], "slope"), (epsc[:], "epsc"), (ndist, "ndist")):
                sp_.dma_start(dst, t[name]).then_inc(small_in, 16)
            load_m(2)
            load_m(3)
            for n in range(RAW):
                load_w(n, free=False)
            load_m(4)
            with sp_.Fori(0, 4) as i:
                for n in range(RAW, 2 * RAW):
                    load_w(n, i)
            for n in range(W_OUT, W_OUT + RAW):
                load_w(n)
            with sp_.Fori(0, 7) as i:
                load_m(5, i)
            load_w(W_OUT + 6)
            load_w(W_OUT + 7)
            for n in range(W_FFN0, W_FFN0 + RAW):
                load_w(n)
            load_m(CH)
            with sp_.Fori(0, 9) as i:
                for n in range(W_FFN0 + RAW, W_FFN0 + 2 * RAW):
                    load_w(n, i)
                load_m(CH + 1, i)
            for n in range(W_FFN0 + 10 * RAW, W_FFN0 + 11 * RAW):
                load_w(n)
            load_m(2 * CH - 2)
            for n in range(W_SIN, W_SIN + 3):
                load_w(n)
            load_m(2 * CH - 1)
            first = W_SIN + 3
            loops = (N_SLOTS - first) // RAW
            with sp_.Fori(0, loops) as i:
                for n in range(first, first + RAW):
                    load_w(n, i)
            for n in range(first + RAW * loops, N_SLOTS):
                load_w(n)
            for m in range(KT):
                sp_.wait_ge(fin_ready, m + 1)
                sp_.dma_start(t["out"][:, m, :], tmp[:, m, :]).then_inc(out_done, 16)
            sp_.wait_ge(out_done, 16 * KT)

        @block.tensor
        def _(pe):
            def three(out, n, cols, xh, xl, first, last, skip=False):
                w_h, w_l = whi[:, n % SPL, cols:cols + P], wlo[:, n % SPL, cols:cols + P]
                pe.matmul(out, w_h, xh, start=first, stop=False, skip_group_check=skip)
                pe.matmul(out, w_h, xl, start=False, stop=False, skip_group_check=skip)
                return pe.matmul(out, w_l, xh, start=False, stop=last, skip_group_check=skip)

            def project(out, n, i=0, phase=None):
                pe.wait_ge(lo_ready, n + RAW * i + 1)
                for k in range(KT):
                    if phase is not None:
                        pe.wait_ge(act_lo, KT * phase + k + 1)
                    mm = three(out, n, k * P, hh[:, k, :], hl[:, k, :], k == 0, k == KT - 1)
                mm.then_inc(slot_used, 1)

            def gemv(c, i=0):
                if not (isinstance(i, int) and c + i == 0):
                    pe.wait_ge(gm_ready, c + i)
                for s in range(MS):
                    pe.wait_ge(m_loaded[s], 16 * (c + i + 1))
                    for kk in range(2):
                        k = 2 * s + kk
                        j = k % 4
                        mm = pe.matmul(gv[32 * j:32 * j + 1, :], cond[:, k:k + 1], mraw[:, s, kk * 512:kk * 512 + 512],
                                       start=(k < 4), stop=(k >= 4))
                    mm.then_inc(mod_used, 1)

            def columns(c, i=0):
                pe.wait_ge(gm_ready, c + i + 1)
                if not (isinstance(i, int) and c + i == 0):
                    pe.wait_ge(mod_col, c + i)
                for q in range(4):
                    mm = pe.matmul(misc[:, q:q + 1], gm[:, q * P:(q + 1) * P], ones[:, 0:1], start=True, stop=True)
                mm.then_inc(cols_done, 1)

            def sum_squares(norm, chunks):
                if chunks:
                    pe.wait_ge(mod_col, chunks)
                for k in range(KT):
                    pe.wait_ge(sq_ready, KT * norm + k + 1)
                    mm = pe.matmul(misc[:, 256:512], ones[:], tmp[:, k, :], start=(k == 0), stop=(k == KT - 1))
                mm.then_inc(ssum, 1)

            pe.wait_ge(set_up, 2)
            pe.wait_ge(cond_ready, 1)
            gemv(0)
            pe.wait_ge(small_in, 16 * N_SMALL)
            for c in range(1, 4):
                gemv(c)
                columns(c - 1)
            columns(3)
            sum_squares(0, 4)

            for n in range(RAW):
                if n >= 2:
                    pe.wait_ge(qkv_ready, n - 1)
                project(up[:, n % 2, 0:T], n, phase=0 if n == 0 else None)
            pe.wait_ge(qkv_ready, RAW)
            pe.wait_ge(rt_ready, 1)
            for qt in range(2):
                mm = pe.transpose(misc[:, qt * P:(qt + 1) * P], qkv[:, S_WI, qt * P:(qt + 1) * P], ident[:])
            mm.then_inc(idx_done, 1)
            for step, (qt, keys) in enumerate(((1, T), (0, P))):
                if step:
                    pe.wait_ge(idx_relu, 1)
                for h in range(IH):
                    r = HD * (h % 2)
                    mm = pe.matmul(acc[:, h % 4, (h // 4) * T:(h // 4) * T + keys],
                                   qkv[r:r + HD, S_QI + h // 2, qt * P:(qt + 1) * P], qkv[r:r + HD, S_KI, 0:keys],
                                   start=True, stop=True)
                mm.then_inc(idx_done, 1)
            with pe.Fori(1, N_IN // RAW) as i:
                for n in range(RAW):
                    pe.wait_ge(qkv_ready, n - 1 + RAW * i)
                    project(up[:, n % 2, 0:T], n, i)

            pe.wait_ge(wit_ready, 1)
            pe.wait_ge(idx_relu, 2)
            pe.wait_ge(qkv_ready, N_IN)
            with pe.Fori(0, PAIRS // 2) as i:
                def scores(a):
                    pe.wait_ge(stage_ready, 3 * (2 * i + a + 1))
                    pe.wait_ge(act_lo, KT + 2 * i + a - 1)
                    for e in range(2):
                        r = HD * e
                        pe.matmul(acc[:, 2 * a + e, 0:T], stage[r:r + HD, a, 0, P:T], stage[r:r + HD, a, 1, :],
                                  start=True, stop=True)
                        pe.matmul(acc[:, 2 * a + e, T:T + P], stage[r:r + HD, a, 0, 0:P], stage[r:r + HD, a, 1, 0:P],
                                  start=True, stop=True)
                    for kt in range(2):
                        mm = pe.transpose(acc[:, 2 * a + kt, 384:512], stage[:, a, 2, kt * P:(kt + 1) * P], ident[:])
                    mm.then_inc(s_done, 1)

                def turn(a):
                    pe.wait_ge(p_ready, 4 * (2 * i + a + 1))
                    if a:
                        pe.wait_ge(tr_out, 2 * i + 1)
                    for e in range(2):
                        for b, src in ((0, T), (1, 0), (2, P)):
                            mm = pe.transpose(up[:, e, b * P:(b + 1) * P], sp[:, a, e, src:src + P], ident[:])
                    mm.then_inc(tr_done, 1)

                def values(a):
                    pe.wait_ge(tr_out, 2 * i + a + 1)
                    for e in range(2):
                        o = acc[HD * e:HD * e + HD, 2 * a, :]
                        pe.matmul(o[:, 0:T], vsb[:, a, 0, HD * e:HD * e + HD], pt[:, a, e, 0:T], start=True, stop=False)
                        mm = pe.matmul(o[:, P:T], vsb[:, a, 1, HD * e:HD * e + HD], pt[:, a, e, T:T + P],
                                       start=False, stop=True)
                    mm.then_inc(pv_done, 1)

                scores(0)
                scores(1)
                gemv(4, 2 * i)
                turn(0)
                columns(4, 2 * i)
                gemv(5, 2 * i)
                turn(1)
                values(0)
                columns(5, 2 * i)
                values(1)

            for m in range(KT):
                if m >= 4:
                    pe.wait_ge(x_upd, m - 3)
                project(acc[:, (m + 1) % 4, 0:T], W_OUT + m, phase=1 if m == 0 else None)
            sum_squares(1, CH)

            def ffn_phase(layer, base, phase):
                def up_step(par, n_v, i=0, phase=None):
                    project(up[:, par, 0:T], n_v, i, phase)
                    project(up[:, par, T:2 * T], n_v + 1, i)

                def down_step(par, n, i, s, last=False):
                    pe.wait_ge(lo_ready, n + RAW * i + 1)
                    pe.wait_ge(a_lo, FT * layer + s + 1)
                    for m in range(KT):
                        mm = three(acc[:, m // 2, (m % 2) * T:(m % 2 + 1) * T], n, m * P, ah[:, par, :], al[:, par, :],
                                   False, last, skip=True)
                    mm.then_inc(slot_used, 1)

                up_step(0, base, phase=phase)
                up_step(1, base + 2)
                for b in range(4):
                    pe.matmul(acc[:, b, :], zrow[:, 0:P], zrow[:], start=True, stop=True, skip_group_check=True)
                with pe.Fori(0, 10) as i:
                    if layer == 0:
                        gemv(CH, i)
                    for h in range(2):
                        n = base + 4 + 3 * h
                        down_step(h, n, i, 2 * i + h)
                        pe.wait_ge(conv_s, 4 * (FT * layer + 2 * i + h + 1))
                        up_step(h, n + 1, i)
                        if layer == 0 and h == 0:
                            columns(CH, i)
                if layer == 0:
                    gemv(2 * CH - 2)
                down_step(0, base + 64, 0, 20)
                if layer == 0:
                    columns(2 * CH - 2)
                down_step(1, base + 65, 0, 21, last=True)
                if layer == 0:
                    gemv(2 * CH - 1)
                    columns(2 * CH - 1)

            ffn_phase(0, W_FFN0, 2)
            sum_squares(2, 2 * CH)
            pe.wait_ge(pw, PW_TAB)
            for mt in range(KT):
                for q in range(4):
                    pair = mt * 4 + q
                    for r in range(2):
                        mm = pe.matmul(up[32 * q:32 * q + 32, mt // 4, (mt % 4) * P:(mt % 4 + 1) * P],
                                       bpow[:, r, pair, LCH - 1, :], cpow[:, :, r, pair * 32:pair * 32 + 32],
                                       start=(r == 0), stop=(r == 1))
            mm.then_inc(k_done, 1)
            pe.wait_ge(mod_col, 2 * CH)
            pe.wait_ge(rt_ready, 3)

            def transpose_b(mt):
                if mt:
                    pe.wait_ge(bt_act, mt)
                    pe.wait_ge(bt_dve, mt)
                for r, bank in ((0, gv), (1, misc)):
                    for q in range(4):
                        mm = pe.transpose(bank[:, q * P:(q + 1) * P], bpow_r[:, r, (4 * mt + q) * P:(4 * mt + q + 1) * P],
                                          ident[:])
                mm.then_inc(bt_done, 1)

            def stack_u(mt):
                pe.wait_ge(u_ready, mt + 1)
                for q in range(4):
                    for l in range(LCH):
                        mm = pe.matmul(acc[32 * l:32 * l + 32, mt % 2, T + q * NJ:T + (q + 1) * NJ],
                                       ident[:, 32 * q:32 * q + 32], u[:, mt, :, l], start=True, stop=True)
                mm.then_inc(st_done, 1)

            def inject(mt):
                pe.wait_ge(bt_act, mt + 1)
                pe.wait_ge(bt_dve, mt + 1)
                pe.wait_ge(st_ready, mt + 1)
                if mt >= 2:
                    pe.wait_ge(v_read, 2 * mt - 2)
                for r in range(2):
                    for q in range(4):
                        c = (4 * mt + q) * P
                        mm = pe.matmul(acc[:, 2 + mt % 2, (2 * q + r) * NJ:(2 * q + r + 1) * NJ],
                                       bpow_r[:, r, c:c + P], ust[:, mt % 2, q, :], start=True, stop=True)
                mm.then_inc(v_done, 1)

            def lags(mt):
                if mt == 0:
                    pe.wait_ge(k_out, 4)
                if mt >= 2:
                    pe.wait_ge(yv_ready, mt - 1)
                y = up[:, mt % 2, 0:T].rearrange("p (j l) -> p j l", l=LCH)
                for lag in range(LCH):
                    pe.matmul(y[:, :, lag:LCH], kbd[:, mt, lag, :], u[:, mt, :, 0:LCH - lag],
                              start=(lag == 0), stop=False, skip_group_check=True)

            def emit(mt):
                if mt == 0:
                    pe.wait_ge(pw, PW_ALL)
                pe.wait_ge(h_ready, 2 * (mt + 1))
                y = up[:, mt % 2, 0:T].rearrange("p (j l) -> p j l", l=LCH)
                for l in range(LCH):
                    for r in range(2):
                        for q in range(4):
                            pair = mt * 4 + q
                            mm = pe.matmul(y[32 * q:32 * q + 32, :, l], cpow[:, (l + 1) % 4, r, pair * 32:pair * 32 + 32],
                                           hst[:, r, q, :], start=False, stop=(l == LCH - 1 and r == 1),
                                           skip_group_check=True)
                mm.then_inc(y_done, 1)

            for m in range(KT + 2):
                if m < KT:
                    if m >= 2:
                        pe.wait_ge(st_ready, m - 1)
                    project(acc[:, m % 2, 0:T], W_SIN + m, phase=3 if m == 0 else None)
                    transpose_b(m)
                if 1 <= m <= KT:
                    inject(m - 1)
                    lags(m - 1)
                if m >= 2:
                    emit(m - 2)
                if m < KT:
                    stack_u(m)

            for m in range(KT):
                for g in range(2):
                    if m >= 2:
                        pe.wait_ge(glu_s, m - 1)
                    project(acc[:, 2 * (m % 2) + g, 0:T], W_GLU + 2 * m + g, phase=4 if m == 0 and g == 0 else None)
            sum_squares(3, 2 * CH)
            ffn_phase(1, W_FFN1, 5)
            sum_squares(4, 2 * CH)

        @block.scalar
        def _(act):
            def split_hi(n, i=0, ring=True):
                act.wait_ge(w_loaded[n % RAW], 16 * (n // RAW + 1 + i))
                if ring:
                    act.wait_ge(slot_used, n + RAW * i - SPL + 1)
                act.activation(whi[:, n % SPL, :], raw[:, n % RAW, :], ACT.Copy).then_inc(hi_ready, 1)

            def row_out(c, i=0):
                act.wait_ge(mod_used, MS * (c + i + 1))
                if not (isinstance(i, int) and c + i == 0):
                    act.wait_ge(cols_done, c + i)
                act.activation(gm[:], gv[:], ACT.Copy).then_inc(gm_ready, 1)

            def square(norm, k):
                if norm == 0:
                    if k % 2 == 0:
                        act.wait_ge(x_in, 64)
                else:
                    act.wait_ge(x_upd, KT * (norm - 1) + k + 1)
                act.activation(tmp[:, k, :], x[:, k, :], ACT.Square).then_inc(sq_ready, 1)

            def root(norm):
                act.wait_ge(ssum, norm + 1)
                act.activation(rstd[:], misc[:, 256:512], ACT.Sqrt, scale=1.0 / D, bias=epsc[:, 0:1]).then_inc(rt_ready, 1)

            def norm_hi(norm, phase, sh):
                for k in range(KT):
                    act.wait_ge(hp_ready, KT * norm + k + 1)
                    act.activation(hh[:, k, :], tmp[:, k, :], ACT.Identity, bias=modc[:, sh + k:sh + k + 1]).then_inc(act_hi, 1)

            act.wait_ge(cond_in, 16)
            act.activation(cond[:], craw[:], ACT.Silu).then_inc(cond_ready, 1)
            row_out(0)
            row_out(1)
            row_out(2)
            for k in range(KT):
                square(0, k)
            row_out(3)
            for n in range(SPL):
                split_hi(n, ring=False)
            act.wait_ge(small_in, 16 * N_SMALL)
            root(0)
            norm_hi(0, 0, 0)

            for n in range(RAW):
                act.wait_ge(slot_used, n + 1)
                act.activation(qkv[:, n, :], up[:, n % 2, 0:T], ACT.Copy).then_inc(qkv_ready, 1)
                split_hi(n + SPL)
            for step, keys in enumerate((T, P)):
                act.wait_ge(idx_done, step + 2)
                if step:
                    act.wait_ge(idx_acc, 8)
                act.activation(rbuf[:, :, :, 0:keys], acc[:].rearrange("p b (h t) -> p b h t", h=2)[:, :, :, 0:keys],
                               ACT.Relu, scale=HD ** -0.5).then_inc(idx_relu, 1)
            act.activation(pr("dt"), pr("ldt"), ACT.Exp).then_inc(prm_a, 1)
            act.wait_ge(prm_v, 1)
            act.activation(pr("mag"), pr("t0"), ACT.Exp).then_inc(prm_a, 1)
            act.wait_ge(prm_v, PRM_SIN)
            act.activation(pr("sin"), pr("t2"), ACT.Sin).then_inc(prm_a, 1)
            act.activation(pr("cos"), pr("t3"), ACT.Sin).then_inc(prm_a, 1)
            with act.Fori(1, N_IN // RAW) as i:
                for n in range(RAW):
                    act.wait_ge(slot_used, n + RAW * i + 1)
                    act.activation(qkv_f[:, ds((n + RAW * i) * T, T)], up[:, n % 2, 0:T], ACT.Copy).then_inc(qkv_ready, 1)
                    split_hi(n + SPL, i)

            with act.Fori(0, PAIRS // 2) as i:
                for a in range(2):
                    act.wait_ge(mx_ready, 2 * (2 * i + a + 1))
                    for e in range(2):
                        act.activation(sp[:, a, e, 0:T], sp[:, a, e, 0:T], ACT.Exp, bias=nmx[:, a, e:e + 1],
                                       accum_out=rs[:, a, e:e + 1]).then_inc(exp_done, 1)
                        act.activation(sp[:, a, e, T:T + P], sp[:, a, e, T:T + P], ACT.Exp,
                                       bias=nmx[:, a, 2 + e:3 + e], accum_out=rs[:, a, 2 + e:3 + e]).then_inc(exp_done, 1)

                def turned(a):
                    act.wait_ge(tr_done, 2 * i + a + 1)
                    act.activation(pt[:, a, :, :], up[:, :, 0:384], ACT.Copy).then_inc(tr_out, 1)

                def out_hi(a):
                    act.wait_ge(pv_done, 2 * i + a + 1)
                    act.activation(hh_f[:, ds((2 * i + a) * T, T)], acc[:, 2 * a, 0:T], ACT.Copy).then_inc(act_hi, 1)

                row_out(4, 2 * i)
                turned(0)
                row_out(5, 2 * i)
                turned(1)
                out_hi(0)
                out_hi(1)

            for m in range(KT):
                split_hi(W_OUT + m + SPL)
                square(1, m)
            root(1)
            norm_hi(1, 2, 24)

            def ffn_phase(layer, base):
                def chain_a(par, s, need):
                    act.wait_ge(slot_used, need)
                    for e in range(2):
                        act.activation(cb[:, par, e, :], up[:, par, e * T:(e + 1) * T], ACT.Identity,
                                       scale=conv[:, layer, 2, ds(s + e * FT, 1)],
                                       bias=conv[:, layer, 3, ds(s + e * FT, 1)]).then_inc(tap, 1)

                def chain_b(par, s, cnt, down_used=None):
                    act.wait_ge(conv_s, 4 * (cnt + 1))
                    act.activation(sg[:, par, :], cb[:, par, 1, :], ACT.Silu).then_inc(sg_ready, 1)
                    act.wait_ge(am, cnt + 1)
                    if down_used is not None:
                        act.wait_ge(slot_used, down_used)
                    act.activation(ah[:, par, :], ab[:, par, :], ACT.Copy).then_inc(a_hi, 1)

                off = FT * layer
                chain_a(0, 0, base + 2)
                split_hi(base + 3)
                chain_b(0, 0, off)
                split_hi(base + 4)
                split_hi(base + 5)
                with act.Fori(0, 10) as i:
                    for h in range(2):
                        par = 1 - h
                        chain_a(par, 2 * i + 1 + h, base + 4 + 3 * h + RAW * i)
                        if layer == 0 and h == 0:
                            row_out(CH, i)
                        split_hi(base + 6 + 3 * h, i)
                        chain_b(par, 2 * i + 1 + h, off + 2 * i + 1 + h, base + 2 + 3 * h + RAW * i)
                        split_hi(base + 7 + 3 * h, i)
                        split_hi(base + 8 + 3 * h, i)
                chain_a(1, FT - 1, base + 64)
                if layer == 0:
                    row_out(2 * CH - 2)
                chain_b(1, FT - 1, off + FT - 1, base + 62)
                if layer == 0:
                    act.wait_ge(pw, PW_TAB)
                    act.activation(tab, tab, ACT.Sin, scale=TWO_PI * (1 - 2 ** -23)).then_inc(tab_ready, 1)
                    row_out(2 * CH - 1)

            ffn_phase(0, W_FFN0)
            for n in range(SPL):
                split_hi(W_SIN + n)
            for k in range(KT):
                square(2, k)
            root(2)
            norm_hi(2, 3, 48)
            act.wait_ge(k_done, 1)
            act.wait_ge(kz, 1)
            for q in (1, 3):
                rows = slice(32 * q, 32 * q + 32)
                act.activation(kbd[rows, :, :, 32 * q:32 * q + 32],
                               up[rows, :, :].rearrange("p b (m l n) -> p (b m) l n", m=4, l=LCH),
                               ACT.Copy).then_inc(k_out, 1)

            def gelu(mt):
                act.wait_ge(yv_ready, mt + 1)
                act.activation(yg[:, mt, :], yv[:, mt % 2, :], ACT.Gelu_apprx_tanh).then_inc(yg_ready, 1)

            def hi(mt):
                act.wait_ge(yg_ready, mt + 1)
                act.activation(hh[:, mt, :], yg[:, mt, :], ACT.Copy).then_inc(act_hi, 1)

            for m in range(KT + 2):
                if m < KT:
                    act.wait_ge(slot_used, W_SIN + m + 1)
                    act.activation(ffn[:, m * T:(m + 1) * T], acc[:, m % 2, 0:T], ACT.Copy).then_inc(u_ready, 1)
                    split_hi(W_SIN + m + SPL)
                    act.wait_ge(bt_done, m + 1)
                    act.activation(bpow_r[:, 0, m * 512:(m + 1) * 512], gv[:], ACT.Copy).then_inc(bt_act, 1)
                    act.wait_ge(st_done, m + 1)
                    if m >= 2:
                        act.wait_ge(v_done, m - 1)
                    act.activation(ust[:, m % 2, :, :].rearrange("p q j -> p (q j)"), acc[:, m % 2, T:2 * T],
                                   ACT.Copy).then_inc(st_ready, 1)
                if m >= 2:
                    gelu(m - 2)
                if m == KT:
                    act.wait_ge(slot_used, W_GLU)
                    for mt in range(KT - 1):
                        hi(mt)
            hi(KT - 1)

            for m in range(KT):
                split_hi(W_GLU + 2 * m + SPL)
                act.wait_ge(slot_used, W_GLU + 2 * m + 2)
                if m >= 2:
                    act.wait_ge(glu_s, m - 1)
                act.activation(sg[:, m % 2, :], acc[:, 2 * (m % 2) + 1, 0:T], ACT.Sigmoid).then_inc(sig_ready, 1)
                split_hi(W_GLU + 2 * m + 1 + SPL)
                if m:
                    square(3, m - 1)
            square(3, KT - 1)
            root(3)
            norm_hi(3, 5, 48 + 24)
            ffn_phase(1, W_FFN1)
            for k in range(KT):
                square(4, k)
            root(4)

        @block.vector
        def _(dve):
            def split_lo(n, i=0):
                dve.wait_ge(hi_ready, n + RAW * i + 1)
                dve.tensor_tensor(wlo[:, n % SPL, :], raw[:, n % RAW, :], whi[:, n % SPL, :].bitcast(F32),
                                  ALU.subtract).then_inc(lo_ready, 1)

            def col_out(c, i=0):
                dve.wait_ge(cols_done, c + i + 1)
                dve.tensor_tensor(modc[:, ds(4 * (c + i), 4)], misc[:, 0:4], modb[:, ds(4 * (c + i), 4)],
                                  ALU.add).then_inc(mod_col, 1)

            def scale_columns(norm, sc):
                dve.wait_ge(mod_col, (sc + 8) // 4)
                dve.scalar_tensor_tensor(amul[:, norm, :], modc[:, sc:sc + KT], 1.0, gains[:, norm, :],
                                         ALU.add, ALU.mult).then_inc(amul_ready, 1)

            def normalise(norm):
                dve.wait_ge(rt_ready, norm + 1)
                dve.reciprocal(rstd[:], rstd[:]).then_inc(rstd_ready, 1)
                dve.wait_ge(rstd_ready, norm + 1)

            def norm_out(norm, phase, sh):
                normalise(norm)
                dve.wait_ge(amul_ready, norm + 1)

                def scaled(k):
                    dve.scalar_tensor_tensor(tmp[:, k, :], x[:, k, :], amul[:, norm, k:k + 1], rstd[:],
                                             ALU.mult, ALU.mult).then_inc(hp_ready, 1)

                def low(k):
                    dve.wait_ge(act_hi, KT * phase + k + 1)
                    dve.scalar_tensor_tensor(hl[:, k, :], tmp[:, k, :], modc[:, sh + k:sh + k + 1],
                                             hh[:, k, :].bitcast(F32), ALU.add, ALU.subtract).then_inc(act_lo, 1)

                scaled(0)
                scaled(1)
                for k in range(KT):
                    low(k)
                    if k + 2 < KT:
                        scaled(k + 2)

            dve.memset(gv[:], 0.0).then_inc(set_up, 1)
            dve.memset(zrow[:], 0.0).then_inc(set_up, 1)
            dve.wait_ge(small_in, 16 * N_SMALL)
            for c in range(4):
                col_out(c)
            scale_columns(0, 8)
            for n in range(SPL):
                split_lo(n)
            norm_out(0, 0, 0)

            for n in range(RAW):
                split_lo(n + SPL)
            dve.wait_ge(idx_done, 1)
            dve.tensor_scalar(wit, misc[:, 0:T].rearrange("p (q n) -> p q n", q=2)[:, :, 0:IH], float(IH) ** -0.5, None,
                              ALU.mult).then_inc(wit_ready, 1)
            dve.wait_ge(wit_ready, 1)
            for step, (qt, keys, off) in enumerate(((1, T, 0), (0, P, T))):
                dve.wait_ge(idx_relu, step + 1)
                for h in range(IH):
                    r = rbuf[:, h % 4, h // 4, 0:keys]
                    out = scr[:, off:off + keys]
                    if h == 0:
                        dve.tensor_scalar(out, r, wit[:, qt, h:h + 1], None, ALU.mult).then_inc(idx_acc, 1)
                    else:
                        dve.wait_ge(idx_acc, step * 8 + h)
                        dve.scalar_tensor_tensor(out, r, wit[:, qt, h:h + 1], out, ALU.mult, ALU.add).then_inc(idx_acc, 1)
            dve.wait_ge(idx_acc, 16)
            dve.memset(scr[0:64, 192:256], NEG).then_inc(sel, 1)
            dve.memset(scr[0:64, T + 64:T + P], NEG).then_inc(sel, 1)
            np_ = [0]

            def step(ins):
                ins.then_inc(prm_v, 1)
                np_[0] += 1
                dve.wait_ge(prm_v, np_[0])

            dve.wait_ge(prm_a, 1)
            step(dve.tensor_tensor(pr("t0"), pr("lr"), pr("dt"), ALU.mult))
            step(dve.tensor_tensor(pr("th"), pr("li"), pr("dt"), ALU.mult))
            for dst, quarter in (("t2", 0.0), ("t3", 0.25)):
                step(dve.tensor_scalar(pr("t1"), pr("th"), 1.0 / TWO_PI, quarter, ALU.mult, ALU.add))
                step(dve.tensor_scalar(pr("t1"), pr("t1"), ROUND, -ROUND, ALU.add, ALU.add))
                step(dve.scalar_tensor_tensor(pr(dst), pr("t1"), -C1, pr("th"), ALU.mult, ALU.add))
                step(dve.scalar_tensor_tensor(pr(dst), pr("t1"), -C2, pr(dst), ALU.mult, ALU.add))
                if quarter:
                    step(dve.tensor_scalar(pr("t1"), pr("t1"), -C3, TWO_PI / 4, ALU.mult, ALU.add))
                    step(dve.tensor_tensor(pr(dst), pr(dst), pr("t1"), ALU.add))
                else:
                    step(dve.scalar_tensor_tensor(pr(dst), pr("t1"), -C3, pr(dst), ALU.mult, ALU.add))
            pi_f = 3.1415925
            step(dve.tensor_scalar(pr("frac"), pr("t2"), LCH / TWO_PI, None, ALU.mult))
            step(dve.tensor_scalar(pr("t1"), pr("frac"), ROUND, -ROUND, ALU.add, ALU.add))
            step(dve.tensor_tensor(pr("frac"), pr("frac"), pr("t1"), ALU.subtract))
            step(dve.tensor_scalar(pr("t2"), pr("t2"), pi_f, -pi_f, ALU.min, ALU.max))
            step(dve.tensor_scalar(pr("t3"), pr("t3"), pi_f, -pi_f, ALU.min, ALU.max))
            dve.wait_ge(prm_a, 4)
            step(dve.tensor_tensor(pr("are"), pr("mag"), pr("cos"), ALU.mult))
            step(dve.tensor_tensor(pr("aim"), pr("mag"), pr("sin"), ALU.mult))
            step(dve.tensor_tensor(pr("t0"), pr("mag"), pr("mag"), ALU.mult))
            step(dve.tensor_tensor(pr("rho"), pr("t0"), pr("t0"), ALU.mult))
            step(dve.tensor_tensor(pr("t0"), pr("lr"), pr("lr"), ALU.mult))
            step(dve.tensor_tensor(pr("t1"), pr("li"), pr("li"), ALU.mult))
            step(dve.tensor_tensor(pr("t0"), pr("t0"), pr("t1"), ALU.add))
            step(dve.reciprocal(pr("t3"), pr("t0")))
            step(dve.tensor_scalar(pr("t2"), pr("are"), -1.0, None, ALU.add))
            step(dve.tensor_tensor(pr("t0"), pr("t2"), pr("lr"), ALU.mult))
            step(dve.tensor_tensor(pr("t1"), pr("aim"), pr("li"), ALU.mult))
            step(dve.tensor_tensor(pr("t0"), pr("t0"), pr("t1"), ALU.add))
            step(dve.tensor_tensor(pr("cre"), pr("t0"), pr("t3"), ALU.mult))
            step(dve.tensor_tensor(pr("t0"), pr("aim"), pr("lr"), ALU.mult))
            step(dve.tensor_tensor(pr("t1"), pr("t2"), pr("li"), ALU.mult))
            step(dve.tensor_tensor(pr("t0"), pr("t0"), pr("t1"), ALU.subtract))
            step(dve.tensor_tensor(pr("cim"), pr("t0"), pr("t3"), ALU.mult))

            dve.wait_ge(sel, 2)
            with dve.Fori(1, N_IN // RAW) as i:
                for n in range(RAW):
                    if n in (1, 2, 4, 5):
                        dve.wait_ge(sel, 2 + 8 * (i - 1) + 2 * (n - n // 3 - 1))
                    split_lo(n + SPL, i)
                    for qt, off, keys in ((0, 0, T), (1, T, P)):
                        sc = scr[:, off:off + keys]
                        if n in (1, 4):
                            dve.max(max8[:, qt, :], sc).then_inc(sel, 1)
                        if n in (2, 5):
                            dve.match_replace(sc, max8[:, qt, :], sc, TAKEN).then_inc(sel, 1)
            dve.wait_ge(sel, 34)
            dve.tensor_scalar(msk, scr, TAKEN, MASKED, ALU.not_equal, ALU.mult).then_inc(sel, 1)
            dve.wait_ge(sel, 35)

            with dve.Fori(0, PAIRS // 2) as i:
                for a in range(2):
                    dve.wait_ge(s_done, 2 * i + a + 1)
                    dve.tensor_copy(vsb[:, a, :, :], acc[:, 2 * a:2 * a + 2, 384:512]).then_inc(v_ready, 1)
                    for e in range(2):
                        dve.scalar_tensor_tensor(bm[:, a, e, :], ndist, slope[:, ds(4 * i + 2 * a + e, 1)], msk,
                                                 ALU.mult, ALU.add).then_inc(bias_ready, 1)
                    for e in range(2):
                        dve.wait_ge(bias_ready, 4 * i + 2 * a + e + 1)
                        dve.scalar_tensor_tensor(sp[:, a, e, :], acc[:, 2 * a + e, 0:384], HD ** -0.5, bm[:, a, e, :],
                                                 ALU.mult, ALU.add).then_inc(sp_ready, 1)
                    dve.wait_ge(sp_ready, 4 * i + 2 * a + 2)
                    dve.tensor_reduce(nmx[:, a, 0:2], sp[:, a, :, 0:T], AX.X, ALU.max, negate=True).then_inc(mx_ready, 1)
                    dve.tensor_reduce(nmx[:, a, 2:4], sp[:, a, :, T:T + P], AX.X, ALU.max, negate=True).then_inc(mx_ready, 1)
                for a in range(2):
                    dve.wait_ge(exp_done, 4 * (2 * i + a + 1))
                    dve.reciprocal(ri[:, a, :], rs[:, a, :]).then_inc(ri_ready, 1)
                    dve.wait_ge(ri_ready, 2 * i + a + 1)
                    for e in range(2):
                        dve.tensor_scalar(sp[:, a, e, 0:T], sp[:, a, e, 0:T], ri[:, a, e:e + 1], None,
                                          ALU.mult).then_inc(p_ready, 1)
                        dve.tensor_scalar(sp[:, a, e, T:T + P], sp[:, a, e, T:T + P], ri[:, a, 2 + e:3 + e], None,
                                          ALU.mult).then_inc(p_ready, 1)
                col_out(4, 2 * i)
                for a in range(2):
                    if a == 1:
                        col_out(5, 2 * i)
                    dve.wait_ge(act_hi, KT + 2 * i + a + 1)
                    dve.tensor_tensor(hl_f[:, ds((2 * i + a) * T, T)], acc[:, 2 * a, 0:T],
                                      hh_f[:, ds((2 * i + a) * T, T)].bitcast(F32), ALU.subtract).then_inc(act_lo, 1)
            scale_columns(1, 32)
            dve.wait_ge(mod_col, CH)

            def residual(psum, k, gate):
                dve.scalar_tensor_tensor(x[:, k, :], psum, modc[:, gate + k:gate + k + 1], x[:, k, :],
                                         ALU.mult, ALU.add).then_inc(x_upd, 1)

            for m in range(KT):
                split_lo(W_OUT + m + SPL)
                dve.wait_ge(slot_used, W_OUT + m + 1)
                residual(acc[:, (m + 1) % 4, 0:T], m, 16)
            norm_out(1, 2, 24)

            def ffn_phase(layer, base):
                def conv_rest(par, s, cnt):
                    dve.wait_ge(tap, 2 * (cnt + 1))
                    for back in range(2):
                        for e in range(2):
                            if back:
                                dve.wait_ge(conv_s, 4 * cnt + e + 1)
                            w = conv[:, layer, 1 - back, ds(s + e * FT, 1)]
                            dve.scalar_tensor_tensor(cb[:, par, e, 1 + back:T], up[:, par, e * T:e * T + T - 1 - back], w,
                                                     cb[:, par, e, 1 + back:T], ALU.mult, ALU.add).then_inc(conv_s, 1)

                def gate(par, cnt):
                    dve.wait_ge(sg_ready, cnt + 1)
                    dve.tensor_tensor(ab[:, par, :], sg[:, par, :], cb[:, par, 0, :], ALU.mult).then_inc(am, 1)

                def low(par, cnt):
                    dve.wait_ge(a_hi, cnt + 1)
                    dve.tensor_tensor(al[:, par, :], ab[:, par, :], ah[:, par, :].bitcast(F32),
                                      ALU.subtract).then_inc(a_lo, 1)

                off = FT * layer
                conv_rest(0, 0, off)
                split_lo(base + 3)
                gate(0, off)
                low(0, off)
                split_lo(base + 4)
                split_lo(base + 5)
                with dve.Fori(0, 10) as i:
                    for h in range(2):
                        par = 1 - h
                        cnt = off + 2 * i + 1 + h
                        conv_rest(par, 2 * i + 1 + h, cnt)
                        split_lo(base + 6 + 3 * h, i)
                        gate(par, cnt)
                        low(par, cnt)
                        if layer == 0 and h == 1:
                            col_out(CH, i)
                        split_lo(base + 7 + 3 * h, i)
                        split_lo(base + 8 + 3 * h, i)
                conv_rest(1, FT - 1, off + FT - 1)
                gate(1, off + FT - 1)
                low(1, off + FT - 1)
                if layer == 0:
                    col_out(2 * CH - 2)
                dve.wait_ge(slot_used, base + N_FFN)
                for k in range(KT):
                    residual(acc[:, k // 2, (k % 2) * T:(k % 2 + 1) * T], k, 48 * layer + 40)

            ffn_phase(0, W_FFN0)
            col_out(2 * CH - 1)
            scale_columns(2, 48 + 8)
            scale_columns(3, 48 + 32)
            for n in range(SPL):
                split_lo(W_SIN + n)
            norm_out(2, 3, 48)
            dve.wait_ge(k_done, 1)
            dve.wait_ge(kz, 1)
            for q in (0, 2):
                rows = slice(32 * q, 32 * q + 32)
                dve.tensor_copy(kbd[rows, :, :, 32 * q:32 * q + 32],
                                up[rows, :, :].rearrange("p b (m l n) -> p (b m) l n", m=4, l=LCH)).then_inc(k_out, 1)

            dve.wait_ge(tab_ready, 1)

            def turn_in(mt):
                dve.wait_ge(v_done, mt + 1)
                if mt:
                    dve.wait_ge(g2_ready, 8 * mt)
                pairs = slice(4 * mt, 4 * mt + 4)
                v = acc[:, 2 + mt % 2, :].rearrange("p (q r j) -> p q r j", q=4, r=2)
                shape = [P, 4, 2, NJ]
                dve.tensor_tensor(va, v, tcos_v[:, pairs, :].unsqueeze(2).broadcast_to(shape), ALU.mult).then_inc(v_read, 1)
                dve.tensor_tensor(vb, v, tsin_v[:, pairs, :].unsqueeze(2).broadcast_to(shape), ALU.mult).then_inc(v_read, 1)
                dve.wait_ge(v_read, 2 * mt + 2)
                dve.tensor_tensor(va[:, :, 0, :], va[:, :, 0, :], vb[:, :, 1, :], ALU.add).then_inc(g_ready, 1)
                dve.tensor_tensor(va[:, :, 1, :], va[:, :, 1, :], vb[:, :, 0, :], ALU.subtract).then_inc(g_ready, 1)
                dve.wait_ge(g_ready, 2 * mt + 2)
                if mt:
                    dve.wait_ge(rot_s, 2 * mt)
                for q in range(4):
                    for r in range(2):
                        p_ = 4 * mt + q
                        dve.tensor_tensor_scan(g2[:, r, q, :],
                                               prm[:, PRM.index("rho"), p_:p_ + 1].broadcast_to([P, NJ]),
                                               va[:, q, r, :], 0.0, ALU.mult, ALU.add).then_inc(g2_ready, 1)

            def skip(mt):
                dve.wait_ge(y_done, mt + 1)
                if mt >= 2:
                    dve.wait_ge(yg_ready, mt - 1)
                dve.scalar_tensor_tensor(yv[:, mt % 2, :], ffn[:, mt * T:(mt + 1) * T], dcol[:, mt:mt + 1],
                                         up[:, mt % 2, 0:T], ALU.mult, ALU.add).then_inc(yv_ready, 1)

            def low(mt):
                dve.wait_ge(act_hi, 4 * KT + mt + 1)
                dve.tensor_tensor(hl[:, mt, :], yg[:, mt, :], hh[:, mt, :].bitcast(F32),
                                  ALU.subtract).then_inc(act_lo, 1)

            for m in range(KT + 2):
                if m < KT:
                    split_lo(W_SIN + m + SPL)
                    dve.wait_ge(bt_done, m + 1)
                    dve.tensor_copy(bpow_r[:, 1, m * 512:(m + 1) * 512], misc[:]).then_inc(bt_dve, 1)
                if 1 <= m <= KT:
                    turn_in(m - 1)
                if m >= 2:
                    skip(m - 2)
            for mt in range(KT):
                low(mt)

            for m in range(KT):
                split_lo(W_GLU + 2 * m + SPL)
                dve.wait_ge(sig_ready, m + 1)
                dve.tensor_tensor(ab[:, m % 2, :], sg[:, m % 2, :], acc[:, 2 * (m % 2), 0:T], ALU.mult).then_inc(glu_s, 1)
                split_lo(W_GLU + 2 * m + 1 + SPL)
                dve.wait_ge(glu_s, m + 1)
                dve.scalar_tensor_tensor(x[:, m, :], ab[:, m % 2, :], modc[:, 64 + m:65 + m], x[:, m, :],
                                         ALU.mult, ALU.add).then_inc(x_upd, 1)
            norm_out(3, 5, 48 + 24)
            ffn_phase(1, W_FFN1)
            normalise(4)
            for k in range(KT):
                dve.scalar_tensor_tensor(tmp[:, k, :], x[:, k, :], gains[:, 4, k:k + 1], rstd[:],
                                         ALU.mult, ALU.mult).then_inc(fin_ready, 1)

        @block.gpsimd
        def _(pool):
            pool.wait_ge(qkv_ready, N_IN)
            for a in range(2):
                for j, s in enumerate((S_Q, S_K, S_V)):
                    pool.tensor_copy(stage[:, a, j, :], qkv[:, s + a, :]).then_inc(stage_ready, 1)
            with pool.Fori(1, PAIRS // 2) as i:
                for a in range(2):
                    pool.wait_ge(s_done, 2 * i + a - 1)
                    for j, s in enumerate((S_Q, S_K, S_V)):
                        pool.tensor_copy(stage[:, a, j, :], qkv_f[:, ds((s + a + 2 * i) * T, T)]).then_inc(stage_ready, 1)

            cnt = [0]

            def step(ins):
                ins.then_inc(pw, 1)
                cnt[0] += 1
                pool.wait_ge(pw, cnt[0])

            def wide(name):
                return pr(name).unsqueeze(2).broadcast_to([P, PR, 32])

            def w3(a):
                return a.rearrange("p (n c) -> p n c", c=32)

            def b_at(k):
                return bpow[:, :, :, LCH - 1 - k, :]

            def c_at(k):
                return cpow[:, k].rearrange("p r (n c) -> p r n c", c=32)

            def times(dst, src, re, im, minus_im):
                ops = (ALU.subtract, ALU.add) if not minus_im else (ALU.add, ALU.subtract)
                step(pool.tensor_tensor(w3(t1), src[:, 0], wide(re), ALU.mult))
                step(pool.tensor_tensor(w3(t2), src[:, 1], wide(im), ALU.mult))
                step(pool.tensor_tensor(dst[:, 0], w3(t1), w3(t2), ops[0]))
                step(pool.tensor_tensor(w3(t1), src[:, 1], wide(re), ALU.mult))
                step(pool.tensor_tensor(w3(t2), src[:, 0], wide(im), ALU.mult))
                step(pool.tensor_tensor(dst[:, 1], w3(t1), w3(t2), ops[1]))

            pool.wait_ge(act_lo, 16)
            for ri_, name in ((0, "b_re"), (1, "b_im")):
                pool.dma_start(tab[:, ri_ * 1024:ri_ * 1024 + 1024], t[name]).then_inc(ssm_in, 16)
            for ri_, name in ((0, "c_re"), (1, "c_im")):
                pool.dma_start(cpow[:, 0, ri_, :], t[name]).then_inc(ssm_in, 16)
            pool.wait_ge(prm_v, PRM_STEPS)
            pool.wait_ge(ssm_in, 16 * N_SSM)
            times(b_at(0), tab[:, 0:2048].rearrange("p (r n c) -> p r n c", r=2, c=32), "cre", "cim", False)
            for k in range(3):
                times(b_at(k + 1), b_at(k), "are", "aim", False)
            step(pool.tensor_scalar(cpow[:, 0, 1, :], cpow[:, 0, 1, :], -1.0, None, ALU.mult))
            for k in range(3):
                times(c_at(k + 1), c_at(k), "are", "aim", True)
            ang = tpool.rearrange("p (n j) -> p n j", j=NJ)
            shape = [P, PR, NJ]
            step(pool.tensor_tensor(ang, pr("frac").unsqueeze(2).broadcast_to(shape),
                                    jrow[:].unsqueeze(1).broadcast_to(shape), ALU.mult))
            step(pool.tensor_scalar(tsin, tpool, ROUND, -ROUND, ALU.add, ALU.add))
            step(pool.tensor_tensor(tsin, tpool, tsin, ALU.subtract))
            step(pool.tensor_scalar(tpool, tpool, 0.25, None, ALU.add))
            step(pool.tensor_scalar(tcos, tpool, ROUND, -ROUND, ALU.add, ALU.add))
            step(pool.tensor_tensor(tcos, tpool, tcos, ALU.subtract))
            assert cnt[0] == PW_TAB
            pool.wait_ge(mod_used, 2 * CH * MS)
            pool.memset(mraw[:].rearrange("p a b -> p (a b)"), 0.0).then_inc(kz, 1)
            pool.wait_ge(k_done, 1)
            times(c_at(0), c_at(3), "are", "aim", True)
            assert cnt[0] == PW_ALL
            step(pool.memset(hst[:, :, :, 0:1], 0.0))
            pool.wait_ge(tab_ready, 1)
            for mt in range(KT):
                pool.wait_ge(g2_ready, 8 * (mt + 1))
                pairs = slice(4 * mt, 4 * mt + 4)
                sh4 = [P, 2, 4, NJ]
                pool.tensor_tensor(rot1, g2, tcos_v[:, pairs, :].unsqueeze(1).broadcast_to(sh4), ALU.mult).then_inc(rot_s, 1)
                pool.tensor_tensor(rot2, g2, tsin_v[:, pairs, :].unsqueeze(1).broadcast_to(sh4), ALU.mult).then_inc(rot_s, 1)
                pool.wait_ge(rot_s, 2 * mt + 2)
                if mt:
                    pool.wait_ge(y_done, mt)
                pool.tensor_tensor(hst[:, 0, :, 1:NJ], rot1[:, 0, :, 0:NJ - 1], rot2[:, 1, :, 0:NJ - 1],
                                   ALU.subtract).then_inc(h_ready, 1)
                pool.tensor_tensor(hst[:, 1, :, 1:NJ], rot1[:, 1, :, 0:NJ - 1], rot2[:, 0, :, 0:NJ - 1],
                                   ALU.add).then_inc(h_ready, 1)
                pool.wait_ge(h_ready, 2 * mt + 2)


PRM_SIN = 18
PRM_STEPS = 35
PW_TAB = 4 * 6 + 1 + 3 * 6 + 6
PW_ALL = PW_TAB + 6


def _weights(a):
    k, m = a.shape
    return a.reshape(k // P, P, m // P, P).transpose(2, 1, 0, 3).reshape(m // P, P, k * P // P)


def _ffn_weights(up, down):
    u, d = _weights(up), down.reshape(FT, P, D)
    order = [u[0], u[FT], u[1], u[FT + 1]]
    for s in range(2, FT):
        order += [d[s - 2], u[s], u[FT + s]]
    return order + [d[FT - 2], d[FT - 1]]


def _columns(a):
    a = a.reshape(*a.shape[:-1], a.shape[-1] // P, P)
    return np.moveaxis(a, -1, 0)


def _pairs(a):
    return a.reshape(PR, 2, 64).transpose(1, 2, 0).reshape(P, PR)


def _blocks(a):
    out = np.zeros((2, 64, PR, 2, 16), a.dtype)
    v = a.reshape(PR, 2, 64, 16)
    for g in range(2):
        out[g, :, :, g, :] = v[:, g].transpose(1, 0, 2)
    return out.reshape(P, 1024)


def layout(i):
    f = np.float32
    w_in = i["attn_w_in"][0]
    qi0 = 3 * D
    ki0 = qi0 + IH * HD
    ki, wi = w_in[:, ki0:ki0 + HD], w_in[:, ki0 + HD:]
    w_first = np.concatenate([ki, ki, wi, np.zeros((D, P - IH), f), w_in[:, qi0:ki0], w_in[:, 0:qi0]], axis=1)
    glu = _weights(i["ssm_w_glu"][0])
    glu = glu.reshape(2, KT, P, D).transpose(1, 0, 2, 3).reshape(N_GLU, P, D)
    stream = [*_weights(w_first), *_weights(i["attn_w_out"][0]),
              *_ffn_weights(i["ffn_w_up"][0], i["ffn_w_down"][0]), *_weights(i["ssm_w_in"][0]), *glu,
              *_ffn_weights(i["ffn_w_up"][1], i["ffn_w_down"][1])]
    mw = i["mod_w"].reshape(2, MS, 2, P, CH, 512).transpose(0, 4, 1, 3, 2, 5).reshape(2 * CH * MS, P, 1024)
    q = np.arange(P)[:, None]
    ndist = -np.abs(np.concatenate([q + P - np.arange(T)[None], q - np.arange(P)[None]], axis=1)).astype(f)
    conv = np.concatenate([i["ffn_conv_w"], i["ffn_conv_b"][:, None]], axis=1)
    slopes = (2.0 ** (-8.0 * np.arange(1, HEADS + 1, dtype=f) / HEADS)).astype(f)
    return {
        "w": np.stack(stream),
        "mw": mw,
        "x": i["x"][0].T.reshape(KT, P, T).transpose(1, 0, 2),
        "cond": _columns(i["c"][0]),
        "modb": _columns(i["mod_b"]).reshape(P, 96),
        "ident": np.eye(P, dtype=f),
        "ones": np.ones((P, P), f),
        "prm": np.stack([_pairs(i["ssm_lam_re"][0]), _pairs(i["ssm_lam_im"][0]),
                         _pairs(np.repeat(i["ssm_log_dt"][0][:, None], 64, axis=1))], axis=1),
        "conv": _columns(conv),
        "gains": _columns(np.stack([i["norm_mix_g"][0], i["norm_ffn_g"][0], i["norm_mix_g"][1], i["norm_ffn_g"][1],
                                    i["final_g"]])),
        "dcol": _columns(i["ssm_d"][0].reshape(D)),
        "jrow": np.repeat(np.arange(NJ, dtype=f)[None], P, axis=0),
        "slope": np.repeat(slopes[None], P, axis=0),
        "epsc": np.full((P, 1), EPS, f),
        "ndist": ndist,
        "b_re": _blocks(i["ssm_b_re"][0]),
        "b_im": _blocks(i["ssm_b_im"][0]),
        "c_re": _blocks(i["ssm_c_re"][0].transpose(0, 2, 1)),
        "c_im": _blocks(i["ssm_c_im"][0].transpose(0, 2, 1)),
    }


def kernel(**inputs):
    import concourse.bacc as bacc
    from concourse.bass_utils import run_bass_kernel_spmd

    nc = bacc.Bacc("TRN2", target_bir_lowering=False, num_devices=1)
    given = {k: np.asarray(v) for k, v in inputs.items()}
    arrays, tensors = {}, {}
    for name, a in layout(given).items():
        a = np.ascontiguousarray(a)
        arrays[f"in_{name}"] = a
        tensors[name] = nc.dram_tensor(f"in_{name}", a.shape, mybir.dt.from_np(a.dtype), kind="ExternalInput").ap()
    tensors["out"] = nc.dram_tensor("out_0", (P, KT, T), F32, kind="ExternalOutput").ap()
    build(nc, tensors)
    r = run_bass_kernel_spmd(nc, [arrays], core_ids=[0])
    y = r.results[0]["out_0"]
    return np.ascontiguousarray(y.transpose(1, 0, 2).reshape(D, T).T).reshape(1, T, D)
```

```python
from contextlib import ExitStack

import numpy as np

import concourse.bass as bass
from concourse import mybir
from concourse.bass import ds

F32 = mybir.dt.float32
F32R = mybir.dt.float32r
ALU = mybir.AluOpType
ACT = mybir.ActivationFunctionType
AX = mybir.AxisListType

P = 128
D = 1024
KT = D // P
T = 256
HEADS, HD = 16, 64
PAIRS = HEADS // 2
IH = 8
KEEP = T // 4
FF = 2816
FT = FF // P
EPS = 1e-6

RAW, SPL = 6, 3
N_IN = 30
N_OUT = KT
N_FFN = 3 * FT
N_SIN = KT
N_GLU = 2 * KT
W_IN = 0
W_OUT = W_IN + N_IN
W_FFN0 = W_OUT + N_OUT
W_SIN = W_FFN0 + N_FFN
W_GLU = W_SIN + N_SIN
W_FFN1 = W_GLU + N_GLU
N_SLOTS = W_FFN1 + N_FFN
S_KI, S_WI, S_QI, S_Q, S_K, S_V = 0, 1, 2, 6, 14, 22

CH = 6 * D // 512
MS = 4
C_PROJ, C_ATT, C_FFN = 4, 6, 14

LCH = 4
NJ = T // LCH
PR = 32
TWO_PI = 6.283185307179586
ROUND = 12582912.0
C1, C2 = 6.28125, 0.0019350051879882812
C3 = TWO_PI - C1 - C2

NEG = -3.0e38
TAKEN = -3.3e38
MASKED = -1.0e30

PRM = ["lr", "li", "ldt", "dt", "th", "mag", "sin", "cos", "are", "aim", "cre", "cim", "rho", "frac",
       "t0", "t1", "t2", "t3"]
PRM_IN = 3


def build(nc, t):
    with ExitStack() as ctx:
        def sb(name, shape, dt=F32):
            return ctx.enter_context(nc.sbuf_tensor(name, shape, dt))

        def sem(name):
            return ctx.enter_context(nc.semaphore(name))

        x = sb("x", [P, KT, T])
        hh = sb("hh", [P, KT, T], F32R)
        hl = sb("hl", [P, KT, T], F32R)
        raw = sb("raw", [P, RAW, 1024])
        whi = sb("whi", [P, SPL, 1024], F32R)
        wlo = sb("wlo", [P, SPL, 1024], F32R)
        mraw = sb("mraw", [P, MS, 1024])
        gm = sb("gm", [P, 512])
        tmp8 = sb("tmp8", [P, KT * T])
        ffn = sb("ffn", [P, KT * T])
        ah = sb("ah", [P, 2, T], F32R)
        al = sb("al", [P, 2, T], F32R)
        arena = sb("arena", [P, 22528])
        ident = sb("ident", [P, P])
        ones = sb("ones", [P, P])
        craw = sb("craw", [P, KT])
        cond = sb("cond", [P, KT])
        prm = sb("prm", [P, len(PRM), PR])
        conv = sb("conv", [P, 2, 4, 2 * FT])
        modc = sb("modc", [P, 2 * 48])
        modb = sb("modb", [P, 2 * 48])
        gains = sb("gains", [P, 5, KT])
        amul = sb("amul", [P, 4, KT])
        dcol = sb("dcol", [P, KT])
        rt = sb("rt", [P, 2])
        diag = sb("diag", [P, 2, P])
        jrow = sb("jrow", [P, NJ])
        slope = sb("slope", [P, HEADS])
        epsc = sb("epsc", [P, 1])
        zrow = sb("zrow", [1, 512], mybir.dt.bfloat16)

        tmp = tmp8[:].rearrange("p (k t) -> p k t", k=KT)

        def carve(cursor, n):
            a = arena[:, cursor[0]:cursor[0] + n]
            cursor[0] += n
            return a

        cur = [0]
        qkv = carve(cur, N_IN * T).rearrange("p (n t) -> p n t", n=N_IN)
        stage = carve(cur, 2 * 3 * T).rearrange("p (a n t) -> p a n t", a=2, n=3)
        rbuf = carve(cur, 8 * T).rearrange("p (b h t) -> p b h t", b=4, h=2)
        scr = carve(cur, 384)
        msk = carve(cur, 384)
        bm = carve(cur, 4 * 384).rearrange("p (a e t) -> p a e t", a=2, e=2)
        sp = carve(cur, 4 * 384).rearrange("p (a e t) -> p a e t", a=2, e=2)
        pt = carve(cur, 4 * 384).rearrange("p (a e t) -> p a e t", a=2, e=2)
        vsb = carve(cur, 2 * T).rearrange("p (a k d) -> p a k d", a=2, k=2)
        max8 = carve(cur, 16).rearrange("p (q n) -> p q n", q=2)
        wit = carve(cur, 16).rearrange("p (q n) -> p q n", q=2)
        nmx = carve(cur, 8).rearrange("p (a n) -> p a n", a=2)
        rs = carve(cur, 8).rearrange("p (a n) -> p a n", a=2)
        ri = carve(cur, 8).rearrange("p (a n) -> p a n", a=2)
        ndist = carve(cur, 384)
        ATT_END = cur[0]
        cur = [0]
        bpow = carve(cur, 8192).rearrange("p (r n l c) -> p r n l c", r=2, n=PR, l=LCH)
        cpow = carve(cur, 8192).rearrange("p (k r n) -> p k r n", k=4, r=2)
        tpool = carve(cur, 2048)
        tab = carve(cur, 4096)
        assert ATT_END <= cur[0] - 4096 and cur[0] <= 22528
        t1, t2 = tpool[:, 0:1024], tpool[:, 1024:2048]
        rot1 = tpool[:, 0:512].rearrange("p (r q j) -> p r q j", r=2, q=4)
        rot2 = tpool[:, 512:1024].rearrange("p (r q j) -> p r q j", r=2, q=4)
        hst = tpool[:, 1024:1536].rearrange("p (r q j) -> p r q j", r=2, q=4)
        yv = tpool[:, 1536:2048].rearrange("p (a t) -> p a t", a=2)
        yg = ffn[:].rearrange("p (m t) -> p m t", m=KT)
        kbd = mraw[:].rearrange("p a (m l n) -> p (a m) l n", m=2, l=LCH)
        tcos, tsin = tab[:, 0:2048], tab[:, 2048:4096]
        tcos_v = tcos.rearrange("p (n j) -> p n j", j=NJ)
        tsin_v = tsin.rearrange("p (n j) -> p n j", j=NJ)
        va = tmp8[:, 0:512].rearrange("p (q r j) -> p q r j", q=4, r=2)
        vb = tmp8[:, 512:1024].rearrange("p (q r j) -> p q r j", q=4, r=2)
        ust = tmp8[:, 1024:1536].rearrange("p (a q j) -> p a q j", a=2, q=4)
        g2 = tmp8[:, 1536:2048].rearrange("p (r q j) -> p r q j", r=2, q=4)
        bpow_r = bpow.rearrange("p r n l c -> p r (n l c)")
        u = ffn[:].rearrange("p (m j l) -> p m j l", m=KT, l=LCH)
        cb = ffn[:, 0:1024].rearrange("p (a e t) -> p a e t", a=2, e=2)
        sg = ffn[:, 1024:1536].rearrange("p (a t) -> p a t", a=2)
        ab = ffn[:, 1536:2048].rearrange("p (a t) -> p a t", a=2)

        mslot = ([mraw[:, s, :] for s in range(MS)],
                 [tmp8[:, 0:1024], tmp8[:, 1024:2048], ffn[:, 0:1024], ffn[:, 1024:2048]])
        early = arena[:, 0:3 * MS * 1024].rearrange("p (s n) -> p s n", n=1024)
        qkv_f = arena[:, 0:N_IN * T]
        hh_f = hh[:].rearrange("p k t -> p (k t)")
        hl_f = hl[:].rearrange("p k t -> p (k t)")

        def pr(name):
            return prm[:, PRM.index(name), :]

        acc = ctx.enter_context(nc.psum_tensor("acc", [P, 4, 512], F32))
        up = ctx.enter_context(nc.psum_tensor("up", [P, 2, 512], F32))
        gv = ctx.enter_context(nc.psum_tensor("gv", [P, 512], F32))
        misc = ctx.enter_context(nc.psum_tensor("misc", [P, 512], F32))

        diag_ready, rstd_ready = sem("diag_ready"), sem("rstd_ready")
        fold_done = sem("fold_done")
        cond_in = sem("cond_in")
        prm_in = sem("prm_in")
        early_in = sem("early_in")
        small_in = sem("small_in")
        m_early = [sem(f"m_early{j}") for j in range(3 * MS)]
        sum_row, csum = sem("sum_row"), sem("csum")
        x_in = sem("x_in")
        w_loaded = [sem(f"w_loaded{j}") for j in range(RAW)]
        m_loaded = [sem(f"m_loaded{j}") for j in range(MS)]
        m_odd = [sem(f"m_odd{j}") for j in range(MS)]
        hi_ready, lo_ready, slot_used = sem("hi_ready"), sem("lo_ready"), sem("slot_used")
        mod_used = sem("mod_used")
        gm_ready = sem("gm_ready")
        cols_done = sem("cols_done")
        mod_col = sem("mod_col")
        amul_ready = sem("amul_ready")
        set_up = sem("set_up")
        cond_ready = sem("cond_ready")
        prm_v, prm_a = sem("prm_v"), sem("prm_a")
        x_upd = sem("x_upd")
        sq_ready, ssum, rt_ready, ri_norm, hp_ready = (
            sem("sq_ready"), sem("ssum"), sem("rt_ready"), sem("ri_norm"), sem("hp_ready"))
        act_hi, act_lo = sem("act_hi"), sem("act_lo")
        qkv_ready = sem("qkv_ready")
        idx_done, idx_relu, idx_acc = sem("idx_done"), sem("idx_relu"), sem("idx_acc")
        wit_ready = sem("wit_ready")
        sel = sem("sel")
        stage_ready, s_done, v_ready, bias_ready, sp_ready, mx_ready = (
            sem("stage_ready"), sem("s_done"), sem("v_ready"), sem("bias_ready"), sem("sp_ready"), sem("mx_ready"))
        exp_done, ri_ready, p_ready, tr_done, tr_out, pv_done = (
            sem("exp_done"), sem("ri_ready"), sem("p_ready"), sem("tr_done"), sem("tr_out"), sem("pv_done"))
        tap, conv_s, sg_ready, am, a_hi, a_lo = (
            sem("tap"), sem("conv_s"), sem("sg_ready"), sem("am"), sem("a_hi"), sem("a_lo"))
        ssm_in = sem("ssm_in")
        pw = sem("pw")
        k_done, k_out = sem("k_done"), sem("k_out")
        bt_done, bt_act, bt_dve = sem("bt_done"), sem("bt_act"), sem("bt_dve")
        kz = sem("kz")
        st_done, st_ready = sem("st_done"), sem("st_ready")
        tab_arg, tab_ready = sem("tab_arg"), sem("tab_ready")
        u_ready = sem("u_ready")
        v_done, v_read, g_ready, g2_ready, rot_s, h_ready = (
            sem("v_done"), sem("v_read"), sem("g_ready"), sem("g2_ready"), sem("rot_s"), sem("h_ready"))
        y_done, yv_ready, yg_ready = sem("y_done"), sem("yv_ready"), sem("yg_ready")
        sig_ready, glu_s = sem("sig_ready"), sem("glu_s")
        fin_ready, out_done = sem("fin_ready"), sem("out_done")

        N_PRM, N_EARLY, N_SMALL = 2, 5, 4
        N_SSM = 4

        block = ctx.enter_context(nc.Block())

        @block.sync
        def _(sp_):
            def load_w(n, i=0, free=True):
                if free:
                    sp_.wait_ge(lo_ready, n + RAW * i - RAW + 1)
                sp_.dma_start(raw[:, n % RAW, :], t["w"][n + RAW * i, :, :]).then_inc(w_loaded[n % RAW], 16)

            def load_m(c, i=0):
                for s in range(MS):
                    if not (isinstance(c, int) and isinstance(i, int) and c + i == 0):
                        sp_.wait_ge(mod_used, (c + i - 1) * MS + s + 1)
                    sp_.dma_start(mraw[:, s, :], t["mw"][(c + i) * MS + s, :, :]).then_inc(m_loaded[s], 16)

            sp_.dma_start(craw[:], t["cond"]).then_inc(cond_in, 16)
            for dst, name in ((prm[:, 0:PRM_IN, :], "prm"), (jrow[:], "jrow")):
                sp_.dma_start(dst, t[name]).then_inc(prm_in, 16)
            load_m(0)
            for dst, name in ((modb[:], "modb"), (ones[:], "ones"), (ident[:], "ident"), (gains[:], "gains"),
                              (epsc[:], "epsc")):
                sp_.dma_start(dst, t[name]).then_inc(early_in, 16)
            for k in range(0, KT, 2):
                sp_.dma_start(x[:, k:k + 2, :], t["x"][:, k:k + 2, :]).then_inc(x_in, 16)
            for s in range(3 * MS):
                sp_.dma_start(early[:, s, :], t["mw"][MS + s, :, :]).then_inc(m_early[s], 16)
            for n in range(RAW):
                load_w(n, free=False)
            for dst, name in ((conv[:], "conv"), (dcol[:], "dcol"), (slope[:], "slope"), (ndist, "ndist")):
                sp_.dma_start(dst, t[name]).then_inc(small_in, 16)
            load_m(4)
            with sp_.Fori(0, 4) as i:
                for n in range(RAW, 2 * RAW):
                    load_w(n, i)
            for n in range(W_OUT, W_OUT + RAW):
                load_w(n)

            def load_att(c, i=0):
                for s in range(MS):
                    sp_.wait_ge(mod_used, (c - 2 + 2 * i) * MS + s + 1)
                    sp_.dma_start(mslot[c % 2][s], t["mw"][(c + 2 * i) * MS + s, :, :]).then_inc((m_loaded, m_odd)[c % 2][s], 16)

            with sp_.Fori(0, 3) as i:
                load_att(C_ATT + 2, i)
                load_att(C_ATT + 3, i)
            load_att(C_FFN)
            for n in range(W_OUT + RAW, W_FFN0 + RAW):
                load_w(n)
            with sp_.Fori(0, 9) as i:
                for n in range(W_FFN0 + RAW, W_FFN0 + 2 * RAW):
                    load_w(n, i)
                load_m(C_FFN + 1, i)
            for n in range(W_FFN0 + 10 * RAW, W_FFN0 + 11 * RAW):
                load_w(n)
            for n in range(W_SIN, W_SIN + 3):
                load_w(n)
            first = W_SIN + 3
            loops = (N_SLOTS - first) // RAW
            with sp_.Fori(0, loops) as i:
                for n in range(first, first + RAW):
                    load_w(n, i)
            for n in range(first + RAW * loops, N_SLOTS):
                load_w(n)
            for m in range(KT):
                sp_.wait_ge(fin_ready, m + 1)
                sp_.dma_start(t["out"][:, m, :], tmp[:, m, :]).then_inc(out_done, 16)
            sp_.wait_ge(out_done, 16 * KT)

        @block.tensor
        def _(pe):
            def three(out, n, cols, xh, xl, first, last, skip=False):
                w_h, w_l = whi[:, n % SPL, cols:cols + P], wlo[:, n % SPL, cols:cols + P]
                pe.matmul(out, w_h, xh, start=first, stop=False, skip_group_check=skip)
                pe.matmul(out, w_h, xl, start=False, stop=False, skip_group_check=skip)
                return pe.matmul(out, w_l, xh, start=False, stop=last, skip_group_check=skip)

            def project(out, n, i=0, phase=None):
                pe.wait_ge(lo_ready, n + RAW * i + 1)
                for k in range(KT):
                    if phase is not None:
                        pe.wait_ge(act_lo, KT * phase + k + 1)
                    mm = three(out, n, k * P, hh[:, k, :], hl[:, k, :], k == 0, k == KT - 1)
                mm.then_inc(slot_used, 1)

            def gemv(c, i=0):
                if c:
                    pe.wait_ge(gm_ready, c + i if c >= C_FFN else c + 2 * i)
                for s in range(MS):
                    src = mraw[:, s, :]
                    if c >= C_FFN:
                        pe.wait_ge(m_loaded[s], 16 * (c - C_FFN // 2 + i))
                    elif isinstance(c, int) and c == 0:
                        pe.wait_ge(m_loaded[s], 16)
                    elif c < 4:
                        src = early[:, (c - 1) * MS + s, :]
                        pe.wait_ge(m_early[(c - 1) * MS + s], 16)
                    elif c % 2 == 0:
                        pe.wait_ge(m_loaded[s], 16 * (c // 2 + i))
                    else:
                        src = mslot[1][s]
                        pe.wait_ge(m_odd[s], 16 * ((c - 3) // 2 + i))
                    for kk in range(2):
                        k = 2 * s + kk
                        j = k % 4
                        mm = pe.matmul(gv[32 * j:32 * j + 1, :], cond[:, k:k + 1], src[:, kk * 512:kk * 512 + 512],
                                       start=(k < 4), stop=(k >= 4))
                    mm.then_inc(mod_used, 1)

            def columns(c, i=0):
                pe.wait_ge(gm_ready, c + i + 1)
                if not (isinstance(i, int) and c + i == 0):
                    pe.wait_ge(mod_col, c + i)
                for q in range(4):
                    mm = pe.matmul(misc[:, q:q + 1], gm[:, q * P:(q + 1) * P], ones[:, 0:1], start=True, stop=True)
                mm.then_inc(cols_done, 1)

            def open_bank(bank):
                pe.matmul(bank, zrow[:, 0:P], zrow[:], start=True, stop=True, skip_group_check=True)

            def project_two(outs, n, phase, opened=False):
                pe.wait_ge(lo_ready, n + 2)
                for k in range(KT):
                    pe.wait_ge(act_lo, KT * phase + k + 1)
                    for j in range(2):
                        mm = three(outs[j], n + j, k * P, hh[:, k, :], hl[:, k, :], k == 0 and not opened,
                                   k == KT - 1, skip=True)
                        if k == KT - 1:
                            mm.then_inc(slot_used, 1)

            def norm(n, chunks, spread):
                pe.wait_ge(gm_ready, chunks)
                for k in range(KT):
                    pe.wait_ge(sq_ready, KT * n + k + 1)
                    mm = pe.matmul(gv[32 * (k % 4):32 * (k % 4) + 1, 0:T], ones[:, 0:1], tmp[:, k, :],
                                   start=(k < 4), stop=(k >= 4))
                mm.then_inc(ssum, 1)
                pe.wait_ge(sum_row, n + 1)
                pe.wait_ge(mod_col, chunks)
                for h in range(2):
                    mm = pe.matmul(misc[:, 4 + h:5 + h], gm[:, h * P:(h + 1) * P], ones[:, 0:1], start=True, stop=True)
                mm.then_inc(csum, 1)
                if n:
                    spread_root(n, spread)

            def spread_root(n, spread):
                for h in range(2):
                    pe.wait_ge(diag_ready, 2 * n + h + 1)
                    mm = pe.matmul(spread[:, h * P:(h + 1) * P], ones[:], diag[:, h, :], start=True, stop=True)
                mm.then_inc(rstd_ready, 1)

            pe.wait_ge(set_up, 2)
            pe.wait_ge(cond_ready, 1)
            gemv(0)
            gemv(1)
            pe.wait_ge(early_in, 16 * N_EARLY)
            columns(0)
            columns(1)
            norm(0, 2, None)
            gemv(2)
            spread_root(0, up[:, 0, 0:T])
            gemv(3)
            columns(2)
            columns(3)

            for n in range(RAW):
                if n >= 2:
                    pe.wait_ge(qkv_ready, n - 1)
                if n == 0:
                    project_two((up[:, 0, 0:T], up[:, 1, 0:T]), 0, 0)
                elif n > 1:
                    project(up[:, n % 2, 0:T], n)
                if n == 3:
                    gemv(C_PROJ)
                if n == 4:
                    columns(C_PROJ)
            pe.wait_ge(mod_col, C_PROJ + 1)
            pe.wait_ge(qkv_ready, RAW)
            for qt in range(2):
                mm = pe.transpose(misc[:, qt * P:(qt + 1) * P], qkv[:, S_WI, qt * P:(qt + 1) * P], ident[:])
            mm.then_inc(idx_done, 1)
            for step, (qt, keys) in enumerate(((1, T), (0, P))):
                if step:
                    gemv(C_PROJ + 1)
                    pe.wait_ge(idx_relu, 1)
                for h in range(IH):
                    r = HD * (h % 2)
                    mm = pe.matmul(acc[:, h % 4, (h // 4) * T:(h // 4) * T + keys],
                                   qkv[r:r + HD, S_QI + h // 2, qt * P:(qt + 1) * P], qkv[r:r + HD, S_KI, 0:keys],
                                   start=True, stop=True)
                mm.then_inc(idx_done, 1)
            pe.wait_ge(wit_ready, 1)
            columns(C_PROJ + 1)
            with pe.Fori(1, N_IN // RAW) as i:
                for n in range(RAW):
                    pe.wait_ge(qkv_ready, n - 1 + RAW * i)
                    project(up[:, n % 2, 0:T], n, i)

            pe.wait_ge(idx_relu, 2)
            pe.wait_ge(qkv_ready, N_IN)

            def scores(p, a):
                pe.wait_ge(stage_ready, 3 * (p + 1))
                if not (isinstance(p, int) and p < 2):
                    pe.wait_ge(v_ready, p - 1)
                for e in range(2):
                    r = HD * e
                    pe.matmul(acc[:, 2 * a + e, 0:T], stage[r:r + HD, a, 0, P:T], stage[r:r + HD, a, 1, :],
                              start=True, stop=True)
                    pe.matmul(acc[:, 2 * a + e, T:T + P], stage[r:r + HD, a, 0, 0:P], stage[r:r + HD, a, 1, 0:P],
                              start=True, stop=True)
                for kt in range(2):
                    mm = pe.transpose(acc[:, 2 * a + kt, 384:512], stage[:, a, 2, kt * P:(kt + 1) * P], ident[:])
                mm.then_inc(s_done, 1)

            def turn(p, a):
                pe.wait_ge(p_ready, 4 * (p + 1))
                pe.wait_ge(act_lo, KT + p)
                for e in range(2):
                    for b, src in ((0, T), (1, 0), (2, P)):
                        mm = pe.transpose(up[:, e, b * P:(b + 1) * P], sp[:, a, e, src:src + P], ident[:])
                mm.then_inc(tr_done, 1)

            def values(p, a):
                pe.wait_ge(tr_out, p + 1)
                pe.wait_ge(v_ready, p + 1)
                for e in range(2):
                    rows = slice(HD * e, HD * e + HD)
                    v0, v1 = vsb[:, a, 0, rows], vsb[:, a, 1, rows]
                    pe.matmul(up[rows, 0, 384:512], v0, pt[:, a, e, 0:P], start=True, stop=True)
                    pe.matmul(up[rows, 1, 384:512], v0, pt[:, a, e, P:2 * P], start=True, stop=False)
                    mm = pe.matmul(up[rows, 1, 384:512], v1, pt[:, a, e, 2 * P:3 * P], start=False, stop=True)
                mm.then_inc(pv_done, 1)

            scores(0, 0)
            scores(1, 1)
            turn(0, 0)
            scores(2, 0)
            values(0, 0)
            gemv(C_ATT)
            with pe.Fori(0, 2) as i:
                for h in range(2):
                    turn(2 * i + 1 + h, (1 + h) % 2)
                    scores(2 * i + 3 + h, (1 + h) % 2)
                    values(2 * i + 1 + h, (1 + h) % 2)
                    columns(C_ATT + h, 2 * i)
                    gemv(C_ATT + 1 + h, i)
            for p in range(5, PAIRS):
                turn(p, p % 2)
                if p + 2 < PAIRS:
                    scores(p + 2, p % 2)
                values(p, p % 2)
                columns(C_ATT + p - 1)
                gemv(C_ATT + p)
            columns(C_ATT + PAIRS - 1)

            for m in range(KT):
                if m >= 4:
                    pe.wait_ge(x_upd, m - 3)
                project(acc[:, (m + 1) % 4, 0:T], W_OUT + m, phase=1 if m == 0 else None)
            norm(1, C_FFN, misc[:, T:2 * T])

            def ffn_phase(layer, base, phase):
                def up_step(par, n_v, i=0):
                    project(up[:, par, 0:T], n_v, i)
                    project(up[:, par, T:2 * T], n_v + 1, i)

                def down_step(par, n, i, s, last=False):
                    pe.wait_ge(lo_ready, n + RAW * i + 1)
                    pe.wait_ge(a_lo, FT * layer + s + 1)
                    for m in range(KT):
                        mm = three(acc[:, m // 2, (m % 2) * T:(m % 2 + 1) * T], n, m * P, ah[:, par, :], al[:, par, :],
                                   False, last, skip=True)
                        if last and m % 2 and m < KT - 1:
                            mm.then_inc(fold_done, 1)
                    mm.then_inc(slot_used, 1)

                open_bank(up[:, 0, :])
                project_two((up[:, 0, 0:T], up[:, 0, T:2 * T]), base, phase, opened=True)
                up_step(1, base + 2)
                for b in range(4):
                    open_bank(acc[:, b, :])
                with pe.Fori(0, 10) as i:
                    if layer == 0:
                        gemv(C_FFN, i)
                    for h in range(2):
                        n = base + 4 + 3 * h
                        down_step(h, n, i, 2 * i + h)
                        pe.wait_ge(conv_s, 4 * (FT * layer + 2 * i + h + 1))
                        up_step(h, n + 1, i)
                        if layer == 0 and h == 0:
                            columns(C_FFN, i)
                down_step(0, base + 64, 0, 20)
                down_step(1, base + 65, 0, 21, last=True)

            ffn_phase(0, W_FFN0, 2)
            pe.wait_ge(pw, PW_K)
            for mt in range(KT):
                for q in range(4):
                    pair = mt * 4 + q
                    for r in range(2):
                        mm = pe.matmul(up[32 * q:32 * q + 32, mt // 4, (mt % 4) * P:(mt % 4 + 1) * P],
                                       bpow[:, r, pair, LCH - 1, :], cpow[:, :, r, pair * 32:pair * 32 + 32],
                                       start=(r == 0), stop=(r == 1))
            mm.then_inc(k_done, 1)

            norm(2, 2 * CH, misc[:, T:2 * T])
            def transpose_b(mt):
                if mt:
                    pe.wait_ge(bt_act, mt)
                    pe.wait_ge(bt_dve, mt)
                for r, bank in ((0, gv), (1, misc)):
                    for q in range(4):
                        mm = pe.transpose(bank[:, q * P:(q + 1) * P], bpow_r[:, r, (4 * mt + q) * P:(4 * mt + q + 1) * P],
                                          ident[:])
                mm.then_inc(bt_done, 1)

            def stack_u(mt):
                pe.wait_ge(u_ready, mt + 1)
                for q in range(4):
                    for l in range(LCH):
                        mm = pe.matmul(acc[32 * l:32 * l + 32, mt % 2, T + q * NJ:T + (q + 1) * NJ],
                                       ident[:, 32 * q:32 * q + 32], u[:, mt, :, l], start=True, stop=True)
                mm.then_inc(st_done, 1)

            def inject(mt):
                pe.wait_ge(bt_act, mt + 1)
                pe.wait_ge(bt_dve, mt + 1)
                pe.wait_ge(st_ready, mt + 1)
                if mt >= 2:
                    pe.wait_ge(v_read, 2 * mt - 2)
                for r in range(2):
                    for q in range(4):
                        c = (4 * mt + q) * P
                        mm = pe.matmul(acc[:, 2 + mt % 2, (2 * q + r) * NJ:(2 * q + r + 1) * NJ],
                                       bpow_r[:, r, c:c + P], ust[:, mt % 2, q, :], start=True, stop=True)
                mm.then_inc(v_done, 1)

            def lags(mt):
                if mt == 0:
                    pe.wait_ge(k_out, 4)
                if mt >= 2:
                    pe.wait_ge(yv_ready, mt - 1)
                y = up[:, mt % 2, 0:T].rearrange("p (j l) -> p j l", l=LCH)
                for lag in range(LCH):
                    pe.matmul(y[:, :, lag:LCH], kbd[:, mt, lag, :], u[:, mt, :, 0:LCH - lag],
                              start=(lag == 0), stop=False, skip_group_check=True)

            def emit(mt):
                if mt == 0:
                    pe.wait_ge(pw, PW_ALL)
                pe.wait_ge(h_ready, 2 * (mt + 1))
                y = up[:, mt % 2, 0:T].rearrange("p (j l) -> p j l", l=LCH)
                for l in range(LCH):
                    for r in range(2):
                        for q in range(4):
                            pair = mt * 4 + q
                            mm = pe.matmul(y[32 * q:32 * q + 32, :, l], cpow[:, (l + 1) % 4, r, pair * 32:pair * 32 + 32],
                                           hst[:, r, q, :], start=False, stop=(l == LCH - 1 and r == 1),
                                           skip_group_check=True)
                mm.then_inc(y_done, 1)

            for m in range(KT + 2):
                if m < KT:
                    if m >= 2:
                        pe.wait_ge(st_ready, m - 1)
                    if m == 0:
                        project_two((acc[:, 0, 0:T], acc[:, 1, 0:T]), W_SIN, 3)
                    elif m > 1:
                        project(acc[:, m % 2, 0:T], W_SIN + m)
                    transpose_b(m)
                if 1 <= m <= KT:
                    inject(m - 1)
                    lags(m - 1)
                if m >= 2:
                    emit(m - 2)
                if m < KT:
                    stack_u(m)

            for m in range(KT):
                for g in range(2):
                    if m >= 2:
                        pe.wait_ge(glu_s, m - 1)
                    if m == 0 and g == 0:
                        project_two((acc[:, 0, 0:T], acc[:, 1, 0:T]), W_GLU, 4)
                    elif m > 0:
                        project(acc[:, 2 * (m % 2) + g, 0:T], W_GLU + 2 * m + g)
            pe.wait_ge(set_up, 3)
            norm(3, 2 * CH, misc[:, T:2 * T])
            ffn_phase(1, W_FFN1, 5)
            norm(4, 2 * CH, misc[:, T:2 * T])

        @block.scalar
        def _(act):
            def split_hi(n, i=0, ring=True):
                act.wait_ge(w_loaded[n % RAW], 16 * (n // RAW + 1 + i))
                if ring:
                    act.wait_ge(slot_used, n + RAW * i - SPL + 1)
                act.activation(whi[:, n % SPL, :], raw[:, n % RAW, :], ACT.Copy).then_inc(hi_ready, 1)

            def row_out(c, i=0):
                act.wait_ge(mod_used, MS * (c + i + 1))
                if not (isinstance(i, int) and c + i == 0):
                    act.wait_ge(cols_done, c + i)
                act.activation(gm[:], gv[:], ACT.Copy).then_inc(gm_ready, 1)

            def load_m(c, i=0):
                for s in range(MS):
                    act.dma_start(mslot[c % 2][s], t["mw"][(c + i) * MS + s, :, :]).then_inc((m_loaded, m_odd)[c % 2][s], 16)

            def square(norm, k):
                if norm == 0:
                    if k % 2 == 0:
                        act.wait_ge(x_in, 64)
                else:
                    act.wait_ge(x_upd, KT * (norm - 1) + k + 1)
                act.activation(tmp[:, k, :], x[:, k, :], ACT.Square).then_inc(sq_ready, 1)

            def root(norm):
                act.wait_ge(ssum, norm + 1)
                act.wait_ge(cols_done, 2 if norm == 0 else C_FFN if norm == 1 else 2 * CH)
                act.activation(gm[:, 0:T], gv[:, 0:T], ACT.Copy).then_inc(sum_row, 1)
                act.wait_ge(csum, norm + 1)
                act.activation(rt[:], misc[:, 4:6], ACT.Sqrt, scale=1.0 / D, bias=epsc[:, 0:1]).then_inc(rt_ready, 1)

            def norm_hi(norm, phase, sh):
                for k in range(KT):
                    act.wait_ge(hp_ready, KT * norm + k + 1)
                    act.activation(hh[:, k, :], tmp[:, k, :], ACT.Identity, bias=modc[:, sh + k:sh + k + 1]).then_inc(act_hi, 1)

            act.wait_ge(cond_in, 16)
            act.activation(cond[:], craw[:], ACT.Silu).then_inc(cond_ready, 1)
            act.wait_ge(prm_in, 16 * N_PRM)
            act.activation(pr("dt"), pr("ldt"), ACT.Exp).then_inc(prm_a, 1)
            act.wait_ge(prm_v, 1)
            act.activation(pr("mag"), pr("t0"), ACT.Exp).then_inc(prm_a, 1)
            act.wait_ge(prm_v, PRM_SIN)
            act.activation(pr("sin"), pr("t2"), ACT.Sin).then_inc(prm_a, 1)
            act.activation(pr("cos"), pr("t3"), ACT.Sin).then_inc(prm_a, 1)
            row_out(0)
            row_out(1)
            for k in range(KT):
                square(0, k)
            act.wait_ge(early_in, 16 * N_EARLY)
            root(0)
            row_out(2)
            row_out(3)
            for n in range(SPL):
                split_hi(n, ring=False)
            act.wait_ge(mod_col, 4)
            norm_hi(0, 0, 8)

            for n in range(RAW):
                act.wait_ge(slot_used, n + 1)
                act.activation(qkv[:, n, :], up[:, n % 2, 0:T], ACT.Copy).then_inc(qkv_ready, 1)
                split_hi(n + SPL)
                if n == 3:
                    row_out(C_PROJ)
                    act.wait_ge(act_lo, KT)
                    load_m(C_PROJ + 1)
                    load_m(C_PROJ + 2)
            for step, keys in enumerate((T, P)):
                act.wait_ge(idx_done, step + 2)
                if step:
                    row_out(C_PROJ + 1)
                    load_m(C_PROJ + 3)
                    act.wait_ge(idx_acc, 8)
                act.activation(rbuf[:, :, :, 0:keys], acc[:].rearrange("p b (h t) -> p b h t", h=2)[:, :, :, 0:keys],
                               ACT.Relu, scale=HD ** -0.5).then_inc(idx_relu, 1)
            act.wait_ge(tab_arg, TAB_STEPS)
            act.activation(tab, tab, ACT.Sin, scale=TWO_PI * (1 - 2 ** -23)).then_inc(tab_ready, 1)
            with act.Fori(1, N_IN // RAW) as i:
                for n in range(RAW):
                    act.wait_ge(slot_used, n + RAW * i + 1)
                    act.activation(qkv_f[:, ds((n + RAW * i) * T, T)], up[:, n % 2, 0:T], ACT.Copy).then_inc(qkv_ready, 1)
                    split_hi(n + SPL, i)

            def exps(p, a):
                act.wait_ge(mx_ready, 2 * (p + 1))
                for e in range(2):
                    act.activation(sp[:, a, e, 0:T], sp[:, a, e, 0:T], ACT.Exp, bias=nmx[:, a, e:e + 1],
                                   accum_out=rs[:, a, e:e + 1]).then_inc(exp_done, 1)
                    act.activation(sp[:, a, e, T:T + P], sp[:, a, e, T:T + P], ACT.Exp,
                                   bias=nmx[:, a, 2 + e:3 + e], accum_out=rs[:, a, 2 + e:3 + e]).then_inc(exp_done, 1)

            def turned_out(p, a):
                act.wait_ge(tr_done, p + 1)
                act.activation(pt[:, a, :, :], up[:, :, 0:384], ACT.Copy).then_inc(tr_out, 1)
                act.wait_ge(pv_done, p + 1)
                act.activation(hh_f[:, ds(p * T, T)].rearrange("p (b t) -> p b t", b=2), up[:, :, 384:512],
                               ACT.Copy).then_inc(act_hi, 1)

            exps(0, 0)
            exps(1, 1)
            turned_out(0, 0)
            with act.Fori(0, 2) as i:
                for h in range(2):
                    exps(2 * i + 2 + h, h % 2)
                    row_out(C_ATT + h, 2 * i)
                    turned_out(2 * i + 1 + h, (1 + h) % 2)
            for p in range(5, PAIRS):
                if p + 1 < PAIRS:
                    exps(p + 1, (p + 1) % 2)
                row_out(C_ATT + p - 1)
                turned_out(p, p % 2)
            row_out(C_ATT + PAIRS - 1)

            for m in range(KT):
                square(1, m)
                split_hi(W_OUT + m + SPL)
            root(1)
            norm_hi(1, 2, 24)

            def ffn_phase(layer, base):
                def chain_a(par, s, need):
                    act.wait_ge(slot_used, need)
                    for e in range(2):
                        act.activation(cb[:, par, e, :], up[:, par, e * T:(e + 1) * T], ACT.Identity,
                                       scale=conv[:, layer, 2, ds(s + e * FT, 1)],
                                       bias=conv[:, layer, 3, ds(s + e * FT, 1)]).then_inc(tap, 1)

                def chain_b(par, s, cnt, down_used=None):
                    act.wait_ge(conv_s, 4 * (cnt + 1))
                    act.activation(sg[:, par, :], cb[:, par, 1, :], ACT.Silu).then_inc(sg_ready, 1)
                    act.wait_ge(am, cnt + 1)
                    if down_used is not None:
                        act.wait_ge(slot_used, down_used)
                    act.activation(ah[:, par, :], ab[:, par, :], ACT.Copy).then_inc(a_hi, 1)

                off = FT * layer
                chain_a(0, 0, base + 2)
                split_hi(base + 3)
                chain_b(0, 0, off)
                split_hi(base + 4)
                split_hi(base + 5)
                with act.Fori(0, 10) as i:
                    for h in range(2):
                        par = 1 - h
                        chain_a(par, 2 * i + 1 + h, base + 4 + 3 * h + RAW * i)
                        if layer == 0 and h == 0:
                            row_out(C_FFN, i)
                        split_hi(base + 6 + 3 * h, i)
                        chain_b(par, 2 * i + 1 + h, off + 2 * i + 1 + h, base + 2 + 3 * h + RAW * i)
                        split_hi(base + 7 + 3 * h, i)
                        split_hi(base + 8 + 3 * h, i)
                chain_a(1, FT - 1, base + 64)
                chain_b(1, FT - 1, off + FT - 1, base + 62)
                if layer == 0:
                    split_hi(base + 66)
                    split_hi(base + 67)

            act.wait_ge(small_in, 16 * N_SMALL)
            ffn_phase(0, W_FFN0)
            for k in range(KT):
                square(2, k)
            root(2)
            split_hi(W_SIN + 2)
            norm_hi(2, 3, 56)
            act.wait_ge(k_done, 1)
            act.wait_ge(kz, 1)
            for q in (1, 3):
                rows = slice(32 * q, 32 * q + 32)
                act.activation(kbd[rows, :, :, 32 * q:32 * q + 32],
                               up[rows, :, :].rearrange("p b (m l n) -> p (b m) l n", m=4, l=LCH),
                               ACT.Copy).then_inc(k_out, 1)

            def gelu(mt):
                act.wait_ge(yv_ready, mt + 1)
                act.activation(yg[:, mt, :], yv[:, mt % 2, :], ACT.Gelu_apprx_tanh).then_inc(yg_ready, 1)

            def hi(mt):
                act.wait_ge(yg_ready, mt + 1)
                act.activation(hh[:, mt, :], yg[:, mt, :], ACT.Copy).then_inc(act_hi, 1)

            for m in range(KT + 2):
                if m < KT:
                    act.wait_ge(slot_used, W_SIN + m + 1)
                    act.activation(ffn[:, m * T:(m + 1) * T], acc[:, m % 2, 0:T], ACT.Copy).then_inc(u_ready, 1)
                    split_hi(W_SIN + m + SPL)
                    act.wait_ge(bt_done, m + 1)
                    act.activation(bpow_r[:, 0, m * 512:(m + 1) * 512], gv[:], ACT.Copy).then_inc(bt_act, 1)
                    act.wait_ge(st_done, m + 1)
                    if m >= 2:
                        act.wait_ge(v_done, m - 1)
                    act.activation(ust[:, m % 2, :, :].rearrange("p q j -> p (q j)"), acc[:, m % 2, T:2 * T],
                                   ACT.Copy).then_inc(st_ready, 1)
                if m >= 2:
                    gelu(m - 2)
                if m == KT:
                    act.wait_ge(slot_used, W_GLU)
                    for mt in range(KT - 1):
                        hi(mt)
            hi(KT - 1)

            for m in range(KT):
                split_hi(W_GLU + 2 * m + SPL)
                act.wait_ge(slot_used, W_GLU + 2 * m + 2)
                if m >= 2:
                    act.wait_ge(glu_s, m - 1)
                act.activation(sg[:, m % 2, :], acc[:, 2 * (m % 2) + 1, 0:T], ACT.Sigmoid).then_inc(sig_ready, 1)
                split_hi(W_GLU + 2 * m + 1 + SPL)
                if m:
                    square(3, m - 1)
            square(3, KT - 1)
            root(3)
            norm_hi(3, 5, 48 + 24)
            ffn_phase(1, W_FFN1)
            for k in range(KT):
                square(4, k)
            root(4)

        @block.vector
        def _(dve):
            def split_lo(n, i=0):
                dve.wait_ge(hi_ready, n + RAW * i + 1)
                dve.tensor_tensor(wlo[:, n % SPL, :], raw[:, n % RAW, :], whi[:, n % SPL, :].bitcast(F32),
                                  ALU.subtract).then_inc(lo_ready, 1)

            def col_out(c, i=0):
                dve.wait_ge(cols_done, c + i + 1)
                dve.tensor_tensor(modc[:, ds(4 * (c + i), 4)], misc[:, 0:4], modb[:, ds(4 * (c + i), 4)],
                                  ALU.add).then_inc(mod_col, 1)

            def scale_columns(norm, sc):
                dve.wait_ge(mod_col, (sc + 8) // 4)
                dve.scalar_tensor_tensor(amul[:, norm, :], modc[:, sc:sc + KT], 1.0, gains[:, norm, :],
                                         ALU.add, ALU.mult).then_inc(amul_ready, 1)

            def normalise(norm):
                dve.wait_ge(rt_ready, norm + 1)
                dve.reciprocal(rt[:], rt[:]).then_inc(ri_norm, 1)
                dve.wait_ge(ri_norm, norm + 1)
                for h in range(2):
                    dve.tensor_scalar(diag[:, h, :], ident[:], rt[:, h:h + 1], None, ALU.mult).then_inc(diag_ready, 1)

            def scaled(norm, k, spread=misc[:, T:2 * T]):
                dve.scalar_tensor_tensor(tmp[:, k, :], x[:, k, :], amul[:, norm, k:k + 1], spread,
                                         ALU.mult, ALU.mult).then_inc(hp_ready, 1)

            def low_in(k, phase, sh):
                dve.wait_ge(act_hi, KT * phase + k + 1)
                dve.scalar_tensor_tensor(hl[:, k, :], tmp[:, k, :], modc[:, sh + k:sh + k + 1],
                                         hh[:, k, :].bitcast(F32), ALU.add, ALU.subtract).then_inc(act_lo, 1)

            def norm_out(norm, phase, sh):
                dve.wait_ge(amul_ready, norm + 1)
                dve.wait_ge(rstd_ready, norm + 1)
                scaled(norm, 0)
                scaled(norm, 1)
                for k in range(KT):
                    low_in(k, phase, sh)
                    if k + 2 < KT:
                        scaled(norm, k + 2)

            dve.memset(gv[:], 0.0).then_inc(set_up, 1)
            dve.memset(zrow[:], 0.0).then_inc(set_up, 1)
            np_ = [0]

            def step(ins):
                ins.then_inc(prm_v, 1)
                np_[0] += 1
                dve.wait_ge(prm_v, np_[0])

            dve.wait_ge(prm_a, 1)
            step(dve.tensor_tensor(pr("t0"), pr("lr"), pr("dt"), ALU.mult))
            step(dve.tensor_tensor(pr("th"), pr("li"), pr("dt"), ALU.mult))
            for dst, quarter in (("t2", 0.0), ("t3", 0.25)):
                step(dve.tensor_scalar(pr("t1"), pr("th"), 1.0 / TWO_PI, quarter, ALU.mult, ALU.add))
                step(dve.tensor_scalar(pr("t1"), pr("t1"), ROUND, -ROUND, ALU.add, ALU.add))
                step(dve.scalar_tensor_tensor(pr(dst), pr("t1"), -C1, pr("th"), ALU.mult, ALU.add))
                step(dve.scalar_tensor_tensor(pr(dst), pr("t1"), -C2, pr(dst), ALU.mult, ALU.add))
                if quarter:
                    step(dve.tensor_scalar(pr("t1"), pr("t1"), -C3, TWO_PI / 4, ALU.mult, ALU.add))
                    step(dve.tensor_tensor(pr(dst), pr(dst), pr("t1"), ALU.add))
                else:
                    step(dve.scalar_tensor_tensor(pr(dst), pr("t1"), -C3, pr(dst), ALU.mult, ALU.add))
            pi_f = 3.1415925
            step(dve.tensor_scalar(pr("frac"), pr("t2"), LCH / TWO_PI, None, ALU.mult))
            step(dve.tensor_scalar(pr("t1"), pr("frac"), ROUND, -ROUND, ALU.add, ALU.add))
            step(dve.tensor_tensor(pr("frac"), pr("frac"), pr("t1"), ALU.subtract))
            step(dve.tensor_scalar(pr("t2"), pr("t2"), pi_f, -pi_f, ALU.min, ALU.max))
            step(dve.tensor_scalar(pr("t3"), pr("t3"), pi_f, -pi_f, ALU.min, ALU.max))
            dve.wait_ge(prm_a, 4)
            step(dve.tensor_tensor(pr("are"), pr("mag"), pr("cos"), ALU.mult))
            step(dve.tensor_tensor(pr("aim"), pr("mag"), pr("sin"), ALU.mult))
            step(dve.tensor_tensor(pr("t0"), pr("mag"), pr("mag"), ALU.mult))
            step(dve.tensor_tensor(pr("rho"), pr("t0"), pr("t0"), ALU.mult))
            step(dve.tensor_tensor(pr("t0"), pr("lr"), pr("lr"), ALU.mult))
            step(dve.tensor_tensor(pr("t1"), pr("li"), pr("li"), ALU.mult))
            step(dve.tensor_tensor(pr("t0"), pr("t0"), pr("t1"), ALU.add))
            step(dve.reciprocal(pr("t3"), pr("t0")))
            step(dve.tensor_scalar(pr("t2"), pr("are"), -1.0, None, ALU.add))
            step(dve.tensor_tensor(pr("t0"), pr("t2"), pr("lr"), ALU.mult))
            step(dve.tensor_tensor(pr("t1"), pr("aim"), pr("li"), ALU.mult))
            step(dve.tensor_tensor(pr("t0"), pr("t0"), pr("t1"), ALU.add))
            step(dve.tensor_tensor(pr("cre"), pr("t0"), pr("t3"), ALU.mult))
            step(dve.tensor_tensor(pr("t0"), pr("aim"), pr("lr"), ALU.mult))
            step(dve.tensor_tensor(pr("t1"), pr("t2"), pr("li"), ALU.mult))
            step(dve.tensor_tensor(pr("t0"), pr("t0"), pr("t1"), ALU.subtract))
            step(dve.tensor_tensor(pr("cim"), pr("t0"), pr("t3"), ALU.mult))

            assert np_[0] == PRM_STEPS
            dve.wait_ge(early_in, 16 * N_EARLY)
            col_out(0)
            col_out(1)
            scale_columns(0, 0)
            normalise(0)
            dve.wait_ge(amul_ready, 1)
            dve.wait_ge(rstd_ready, 1)
            for k in range(KT):
                scaled(0, k, up[:, 0, 0:T])
            col_out(2)
            col_out(3)
            split_lo(0)
            split_lo(1)
            for k in range(KT):
                low_in(k, 0, 8)
                if k == 3:
                    split_lo(2)

            for n in range(RAW):
                split_lo(n + SPL)
                if n == 4:
                    col_out(C_PROJ)
            dve.wait_ge(idx_done, 1)
            dve.tensor_scalar(wit, misc[:, 0:T].rearrange("p (q n) -> p q n", q=2)[:, :, 0:IH], float(IH) ** -0.5, None,
                              ALU.mult).then_inc(wit_ready, 1)
            dve.wait_ge(wit_ready, 1)
            for step, (qt, keys, off) in enumerate(((1, T, 0), (0, P, T))):
                dve.wait_ge(idx_relu, step + 1)
                for h in range(IH):
                    r = rbuf[:, h % 4, h // 4, 0:keys]
                    out = scr[:, off:off + keys]
                    if h == 0:
                        dve.tensor_scalar(out, r, wit[:, qt, h:h + 1], None, ALU.mult).then_inc(idx_acc, 1)
                    else:
                        dve.wait_ge(idx_acc, step * 8 + h)
                        dve.scalar_tensor_tensor(out, r, wit[:, qt, h:h + 1], out, ALU.mult, ALU.add).then_inc(idx_acc, 1)
            col_out(C_PROJ + 1)
            dve.wait_ge(idx_acc, 16)
            dve.memset(scr[0:64, 192:256], NEG).then_inc(sel, 1)
            dve.memset(scr[0:64, T + 64:T + P], NEG).then_inc(sel, 1)
            dve.wait_ge(sel, 2)
            with dve.Fori(1, N_IN // RAW) as i:
                for n in range(RAW):
                    if n in (1, 2, 4, 5):
                        dve.wait_ge(sel, 2 + 8 * (i - 1) + 2 * (n - n // 3 - 1))
                    split_lo(n + SPL, i)
                    for qt, off, keys in ((0, 0, T), (1, T, P)):
                        sc = scr[:, off:off + keys]
                        if n in (1, 4):
                            dve.max(max8[:, qt, :], sc).then_inc(sel, 1)
                        if n in (2, 5):
                            dve.match_replace(sc, max8[:, qt, :], sc, TAKEN).then_inc(sel, 1)
            dve.wait_ge(sel, 34)
            dve.tensor_scalar(msk, scr, TAKEN, MASKED, ALU.not_equal, ALU.mult).then_inc(sel, 1)
            dve.wait_ge(sel, 35)

            dve.wait_ge(small_in, 16 * N_SMALL)
            def masked(p, a):
                for e in range(2):
                    dve.scalar_tensor_tensor(bm[:, a, e, :], ndist, slope[:, ds(2 * p + e, 1)], msk,
                                             ALU.mult, ALU.add).then_inc(bias_ready, 1)
                dve.wait_ge(s_done, p + 1)
                if not (isinstance(p, int) and p < 2):
                    dve.wait_ge(tr_done, p - 1)
                for e in range(2):
                    dve.wait_ge(bias_ready, 2 * p + e + 1)
                    dve.scalar_tensor_tensor(sp[:, a, e, :], acc[:, 2 * a + e, 0:384], HD ** -0.5, bm[:, a, e, :],
                                             ALU.mult, ALU.add).then_inc(sp_ready, 1)
                dve.wait_ge(sp_ready, 2 * p + 2)
                dve.tensor_reduce(nmx[:, a, 0:2], sp[:, a, :, 0:T], AX.X, ALU.max, negate=True).then_inc(mx_ready, 1)
                dve.tensor_reduce(nmx[:, a, 2:4], sp[:, a, :, T:T + P], AX.X, ALU.max, negate=True).then_inc(mx_ready, 1)

            def v_out(p, a):
                if not (isinstance(p, int) and p < 2):
                    dve.wait_ge(pv_done, p - 1)
                dve.tensor_copy(vsb[:, a, :, :], acc[:, 2 * a:2 * a + 2, 384:512]).then_inc(v_ready, 1)

            def normed(p, a):
                dve.wait_ge(exp_done, 4 * (p + 1))
                dve.reciprocal(ri[:, a, :], rs[:, a, :]).then_inc(ri_ready, 1)
                dve.wait_ge(ri_ready, p + 1)
                for e in range(2):
                    dve.tensor_scalar(sp[:, a, e, 0:T], sp[:, a, e, 0:T], ri[:, a, e:e + 1], None,
                                      ALU.mult).then_inc(p_ready, 1)
                    dve.tensor_scalar(sp[:, a, e, T:T + P], sp[:, a, e, T:T + P], ri[:, a, 2 + e:3 + e], None,
                                      ALU.mult).then_inc(p_ready, 1)

            def out_low(p):
                dve.wait_ge(act_hi, KT + p + 1)
                dve.tensor_tensor(hl_f[:, ds(p * T, T)].rearrange("p (b t) -> p b t", b=2), up[:, :, 384:512],
                                  hh_f[:, ds(p * T, T)].bitcast(F32).rearrange("p (b t) -> p b t", b=2),
                                  ALU.subtract).then_inc(act_lo, 1)

            masked(0, 0)
            v_out(0, 0)
            masked(1, 1)
            normed(0, 0)
            v_out(1, 1)
            masked(2, 0)
            out_low(0)
            normed(1, 1)
            v_out(2, 0)
            with dve.Fori(0, 2) as i:
                for h in range(2):
                    masked(2 * i + 3 + h, (1 + h) % 2)
                    out_low(2 * i + 1 + h)
                    normed(2 * i + 2 + h, h % 2)
                    v_out(2 * i + 3 + h, (1 + h) % 2)
                    col_out(C_ATT + h, 2 * i)
            for p in range(6, PAIRS):
                if p + 1 < PAIRS:
                    masked(p + 1, (p + 1) % 2)
                out_low(p - 1)
                normed(p, p % 2)
                if p + 1 < PAIRS:
                    v_out(p + 1, (p + 1) % 2)
                col_out(C_ATT + p - 2)
            out_low(PAIRS - 1)
            col_out(C_ATT + PAIRS - 2)
            col_out(C_ATT + PAIRS - 1)
            scale_columns(1, 32)
            dve.wait_ge(mod_col, CH)

            def residual(psum, k, gate):
                dve.scalar_tensor_tensor(x[:, k, :], psum, modc[:, gate + k:gate + k + 1], x[:, k, :],
                                         ALU.mult, ALU.add).then_inc(x_upd, 1)

            for m in range(KT):
                dve.wait_ge(slot_used, W_OUT + m + 1)
                residual(acc[:, (m + 1) % 4, 0:T], m, 16)
                if m < KT - 1:
                    split_lo(W_OUT + m + SPL)
            normalise(1)
            split_lo(W_OUT + KT - 1 + SPL)
            norm_out(1, 2, 24)

            def ffn_phase(layer, base):
                def conv_rest(par, s, cnt):
                    dve.wait_ge(tap, 2 * (cnt + 1))
                    for back in range(2):
                        for e in range(2):
                            if back:
                                dve.wait_ge(conv_s, 4 * cnt + e + 1)
                            w = conv[:, layer, 1 - back, ds(s + e * FT, 1)]
                            dve.scalar_tensor_tensor(cb[:, par, e, 1 + back:T], up[:, par, e * T:e * T + T - 1 - back], w,
                                                     cb[:, par, e, 1 + back:T], ALU.mult, ALU.add).then_inc(conv_s, 1)

                def gate(par, cnt):
                    dve.wait_ge(sg_ready, cnt + 1)
                    dve.tensor_tensor(ab[:, par, :], sg[:, par, :], cb[:, par, 0, :], ALU.mult).then_inc(am, 1)

                def low(par, cnt):
                    dve.wait_ge(a_hi, cnt + 1)
                    dve.tensor_tensor(al[:, par, :], ab[:, par, :], ah[:, par, :].bitcast(F32),
                                      ALU.subtract).then_inc(a_lo, 1)

                off = FT * layer
                conv_rest(0, 0, off)
                split_lo(base + 3)
                gate(0, off)
                low(0, off)
                split_lo(base + 4)
                split_lo(base + 5)
                with dve.Fori(0, 10) as i:
                    for h in range(2):
                        par = 1 - h
                        cnt = off + 2 * i + 1 + h
                        conv_rest(par, 2 * i + 1 + h, cnt)
                        split_lo(base + 6 + 3 * h, i)
                        gate(par, cnt)
                        low(par, cnt)
                        if layer == 0 and h == 1:
                            col_out(C_FFN, i)
                        split_lo(base + 7 + 3 * h, i)
                        split_lo(base + 8 + 3 * h, i)
                conv_rest(1, FT - 1, off + FT - 1)
                gate(1, off + FT - 1)
                low(1, off + FT - 1)
                if layer == 0:
                    split_lo(base + 66)
                    split_lo(base + 67)
                for k in range(KT):
                    if k < KT - 2:
                        dve.wait_ge(fold_done, 3 * layer + k // 2 + 1)
                    else:
                        dve.wait_ge(slot_used, base + N_FFN)
                    residual(acc[:, k // 2, (k % 2) * T:(k % 2 + 1) * T], k, 48 * layer + 40)

            ffn_phase(0, W_FFN0)
            scale_columns(2, 48)
            scale_columns(3, 48 + 32)
            normalise(2)
            split_lo(W_SIN + 2)
            norm_out(2, 3, 56)
            dve.wait_ge(k_done, 1)
            dve.wait_ge(kz, 1)
            for q in (0, 2):
                rows = slice(32 * q, 32 * q + 32)
                dve.tensor_copy(kbd[rows, :, :, 32 * q:32 * q + 32],
                                up[rows, :, :].rearrange("p b (m l n) -> p (b m) l n", m=4, l=LCH)).then_inc(k_out, 1)

            dve.wait_ge(tab_ready, 1)

            def turn_in(mt):
                dve.wait_ge(v_done, mt + 1)
                if mt:
                    dve.wait_ge(g2_ready, 8 * mt)
                pairs = slice(4 * mt, 4 * mt + 4)
                v = acc[:, 2 + mt % 2, :].rearrange("p (q r j) -> p q r j", q=4, r=2)
                shape = [P, 4, 2, NJ]
                dve.tensor_tensor(va, v, tcos_v[:, pairs, :].unsqueeze(2).broadcast_to(shape), ALU.mult).then_inc(v_read, 1)
                dve.tensor_tensor(vb, v, tsin_v[:, pairs, :].unsqueeze(2).broadcast_to(shape), ALU.mult).then_inc(v_read, 1)
                dve.wait_ge(v_read, 2 * mt + 2)
                dve.tensor_tensor(va[:, :, 0, :], va[:, :, 0, :], vb[:, :, 1, :], ALU.add).then_inc(g_ready, 1)
                dve.tensor_tensor(va[:, :, 1, :], va[:, :, 1, :], vb[:, :, 0, :], ALU.subtract).then_inc(g_ready, 1)
                dve.wait_ge(g_ready, 2 * mt + 2)
                if mt:
                    dve.wait_ge(rot_s, 2 * mt)
                for q in range(4):
                    for r in range(2):
                        p_ = 4 * mt + q
                        dve.tensor_tensor_scan(g2[:, r, q, :],
                                               prm[:, PRM.index("rho"), p_:p_ + 1].broadcast_to([P, NJ]),
                                               va[:, q, r, :], 0.0, ALU.mult, ALU.add).then_inc(g2_ready, 1)

            def skip(mt):
                dve.wait_ge(y_done, mt + 1)
                if mt >= 2:
                    dve.wait_ge(yg_ready, mt - 1)
                dve.scalar_tensor_tensor(yv[:, mt % 2, :], ffn[:, mt * T:(mt + 1) * T], dcol[:, mt:mt + 1],
                                         up[:, mt % 2, 0:T], ALU.mult, ALU.add).then_inc(yv_ready, 1)

            def low(mt):
                dve.wait_ge(act_hi, 4 * KT + mt + 1)
                dve.tensor_tensor(hl[:, mt, :], yg[:, mt, :], hh[:, mt, :].bitcast(F32),
                                  ALU.subtract).then_inc(act_lo, 1)

            for m in range(KT + 2):
                if m < KT:
                    split_lo(W_SIN + m + SPL)
                    dve.wait_ge(bt_done, m + 1)
                    dve.tensor_copy(bpow_r[:, 1, m * 512:(m + 1) * 512], misc[:]).then_inc(bt_dve, 1)
                if 1 <= m <= KT:
                    turn_in(m - 1)
                if m >= 2:
                    skip(m - 2)
            dve.wait_ge(bt_act, KT)
            dve.memset(gv[:], 0.0).then_inc(set_up, 1)
            for mt in range(KT):
                low(mt)

            for m in range(KT):
                split_lo(W_GLU + 2 * m + SPL)
                dve.wait_ge(sig_ready, m + 1)
                dve.tensor_tensor(ab[:, m % 2, :], sg[:, m % 2, :], acc[:, 2 * (m % 2), 0:T], ALU.mult).then_inc(glu_s, 1)
                split_lo(W_GLU + 2 * m + 1 + SPL)
                dve.wait_ge(glu_s, m + 1)
                dve.scalar_tensor_tensor(x[:, m, :], ab[:, m % 2, :], modc[:, 64 + m:65 + m], x[:, m, :],
                                         ALU.mult, ALU.add).then_inc(x_upd, 1)
            normalise(3)
            norm_out(3, 5, 48 + 24)
            ffn_phase(1, W_FFN1)
            normalise(4)
            dve.wait_ge(rstd_ready, 5)
            for k in range(KT):
                dve.scalar_tensor_tensor(tmp[:, k, :], x[:, k, :], gains[:, 4, k:k + 1], misc[:, T:2 * T],
                                         ALU.mult, ALU.mult).then_inc(fin_ready, 1)

        @block.gpsimd
        def _(pool):
            tabs = [0]

            def tab_step(ins):
                ins.then_inc(tab_arg, 1)
                tabs[0] += 1
                if tabs[0] < TAB_STEPS:
                    pool.wait_ge(tab_arg, tabs[0])

            turns = arena[:, 13 * 1024:15 * 1024]
            ang = turns.rearrange("p (n j) -> p n j", j=NJ)
            shape = [P, PR, NJ]
            pool.wait_ge(prm_v, PRM_SIN)
            tab_step(pool.tensor_tensor(ang, pr("frac").unsqueeze(2).broadcast_to(shape),
                                        jrow[:].unsqueeze(1).broadcast_to(shape), ALU.mult))
            tab_step(pool.tensor_scalar(tsin, turns, ROUND, -ROUND, ALU.add, ALU.add))
            tab_step(pool.tensor_tensor(tsin, turns, tsin, ALU.subtract))
            tab_step(pool.tensor_scalar(turns, turns, 0.25, None, ALU.add))
            tab_step(pool.tensor_scalar(tcos, turns, ROUND, -ROUND, ALU.add, ALU.add))
            tab_step(pool.tensor_tensor(tcos, turns, tcos, ALU.subtract))
            pool.wait_ge(qkv_ready, N_IN)
            for a in range(2):
                for j, s in enumerate((S_Q, S_K, S_V)):
                    pool.tensor_copy(stage[:, a, j, :], qkv[:, s + a, :]).then_inc(stage_ready, 1)
            with pool.Fori(1, PAIRS // 2) as i:
                for a in range(2):
                    pool.wait_ge(s_done, 2 * i + a - 1)
                    for j, s in enumerate((S_Q, S_K, S_V)):
                        pool.tensor_copy(stage[:, a, j, :], qkv_f[:, ds((s + a + 2 * i) * T, T)]).then_inc(stage_ready, 1)

            cnt = [0]

            def step(ins):
                ins.then_inc(pw, 1)
                cnt[0] += 1
                pool.wait_ge(pw, cnt[0])

            def wide(name):
                return pr(name).unsqueeze(2).broadcast_to([P, PR, 32])

            def w3(a):
                return a.rearrange("p (n c) -> p n c", c=32)

            def b_at(k):
                return bpow[:, :, :, LCH - 1 - k, :]

            def c_at(k):
                return cpow[:, k].rearrange("p r (n c) -> p r n c", c=32)

            def times(dst, src, re, im, minus_im):
                ops = (ALU.subtract, ALU.add) if not minus_im else (ALU.add, ALU.subtract)
                step(pool.tensor_tensor(w3(t1), src[:, 0], wide(re), ALU.mult))
                step(pool.tensor_tensor(w3(t2), src[:, 1], wide(im), ALU.mult))
                step(pool.tensor_tensor(dst[:, 0], w3(t1), w3(t2), ops[0]))
                step(pool.tensor_tensor(w3(t1), src[:, 1], wide(re), ALU.mult))
                step(pool.tensor_tensor(w3(t2), src[:, 0], wide(im), ALU.mult))
                step(pool.tensor_tensor(dst[:, 1], w3(t1), w3(t2), ops[1]))

            pool.wait_ge(act_lo, 16)
            for ri_, name in ((0, "b_re"), (1, "b_im")):
                pool.dma_start(cpow[:, 1, ri_, :], t[name]).then_inc(ssm_in, 16)
            for ri_, name in ((0, "c_re"), (1, "c_im")):
                pool.dma_start(cpow[:, 0, ri_, :], t[name]).then_inc(ssm_in, 16)
            pool.wait_ge(prm_v, PRM_STEPS)
            pool.wait_ge(ssm_in, 16 * N_SSM)
            times(b_at(0), c_at(1), "cre", "cim", False)
            for k in range(3):
                times(b_at(k + 1), b_at(k), "are", "aim", False)
            step(pool.tensor_scalar(cpow[:, 0, 1, :], cpow[:, 0, 1, :], -1.0, None, ALU.mult))
            for k in range(3):
                times(c_at(k + 1), c_at(k), "are", "aim", True)
            assert cnt[0] == PW_K
            pool.wait_ge(mod_used, 2 * CH * MS)
            pool.memset(mraw[:].rearrange("p a b -> p (a b)"), 0.0).then_inc(kz, 1)
            pool.wait_ge(k_done, 1)
            times(c_at(0), c_at(3), "are", "aim", True)
            assert cnt[0] == PW_ALL
            step(pool.memset(hst[:, :, :, 0:1], 0.0))
            pool.wait_ge(tab_ready, 1)
            for mt in range(KT):
                pool.wait_ge(g2_ready, 8 * (mt + 1))
                pairs = slice(4 * mt, 4 * mt + 4)
                sh4 = [P, 2, 4, NJ]
                pool.tensor_tensor(rot1, g2, tcos_v[:, pairs, :].unsqueeze(1).broadcast_to(sh4), ALU.mult).then_inc(rot_s, 1)
                pool.tensor_tensor(rot2, g2, tsin_v[:, pairs, :].unsqueeze(1).broadcast_to(sh4), ALU.mult).then_inc(rot_s, 1)
                pool.wait_ge(rot_s, 2 * mt + 2)
                if mt:
                    pool.wait_ge(y_done, mt)
                pool.tensor_tensor(hst[:, 0, :, 1:NJ], rot1[:, 0, :, 0:NJ - 1], rot2[:, 1, :, 0:NJ - 1],
                                   ALU.subtract).then_inc(h_ready, 1)
                pool.tensor_tensor(hst[:, 1, :, 1:NJ], rot1[:, 1, :, 0:NJ - 1], rot2[:, 0, :, 0:NJ - 1],
                                   ALU.add).then_inc(h_ready, 1)
                pool.wait_ge(h_ready, 2 * mt + 2)


PRM_SIN = 18
PRM_STEPS = 35
TAB_STEPS = 6
PW_K = 4 * 6 + 1 + 3 * 6
PW_ALL = PW_K + 6


def _weights(a):
    k, m = a.shape
    return a.reshape(k // P, P, m // P, P).transpose(2, 1, 0, 3).reshape(m // P, P, k * P // P)


def _ffn_weights(up, down):
    u, d = _weights(up), down.reshape(FT, P, D)
    order = [u[0], u[FT], u[1], u[FT + 1]]
    for s in range(2, FT):
        order += [d[s - 2], u[s], u[FT + s]]
    return order + [d[FT - 2], d[FT - 1]]


def _columns(a):
    a = a.reshape(*a.shape[:-1], a.shape[-1] // P, P)
    return np.moveaxis(a, -1, 0)


def _pairs(a):
    return a.reshape(PR, 2, 64).transpose(1, 2, 0).reshape(P, PR)


def _blocks(a):
    out = np.zeros((2, 64, PR, 2, 16), a.dtype)
    v = a.reshape(PR, 2, 64, 16)
    for g in range(2):
        out[g, :, :, g, :] = v[:, g].transpose(1, 0, 2)
    return out.reshape(P, 1024)


def layout(i):
    f = np.float32
    w_in = i["attn_w_in"][0]
    qi0 = 3 * D
    ki0 = qi0 + IH * HD
    ki, wi = w_in[:, ki0:ki0 + HD], w_in[:, ki0 + HD:]
    w_first = np.concatenate([ki, ki, wi, np.zeros((D, P - IH), f), w_in[:, qi0:ki0], w_in[:, 0:qi0]], axis=1)
    glu = _weights(i["ssm_w_glu"][0])
    glu = glu.reshape(2, KT, P, D).transpose(1, 0, 2, 3).reshape(N_GLU, P, D)
    stream = [*_weights(w_first), *_weights(i["attn_w_out"][0]),
              *_ffn_weights(i["ffn_w_up"][0], i["ffn_w_down"][0]), *_weights(i["ssm_w_in"][0]), *glu,
              *_ffn_weights(i["ffn_w_up"][1], i["ffn_w_down"][1])]
    order = [1, 0, 2, 3, 4, 5]
    mod_w = i["mod_w"].reshape(2, D, 6, D)[:, :, order].reshape(2, D, 6 * D)
    mod_b = i["mod_b"].reshape(2, 6, D)[:, order].reshape(2, 6 * D)
    mw = mod_w.reshape(2, MS, 2, P, CH, 512).transpose(0, 4, 1, 3, 2, 5).reshape(2 * CH * MS, P, 1024)
    q = np.arange(P)[:, None]
    ndist = -np.abs(np.concatenate([q + P - np.arange(T)[None], q - np.arange(P)[None]], axis=1)).astype(f)
    conv = np.concatenate([i["ffn_conv_w"], i["ffn_conv_b"][:, None]], axis=1)
    slopes = (2.0 ** (-8.0 * np.arange(1, HEADS + 1, dtype=f) / HEADS)).astype(f)
    return {
        "w": np.stack(stream),
        "mw": mw,
        "x": i["x"][0].T.reshape(KT, P, T).transpose(1, 0, 2),
        "cond": _columns(i["c"][0]),
        "modb": _columns(mod_b).reshape(P, 96),
        "ident": np.eye(P, dtype=f),
        "ones": np.ones((P, P), f),
        "prm": np.stack([_pairs(i["ssm_lam_re"][0]), _pairs(i["ssm_lam_im"][0]),
                         _pairs(np.repeat(i["ssm_log_dt"][0][:, None], 64, axis=1))], axis=1),
        "conv": _columns(conv),
        "gains": _columns(np.stack([i["norm_mix_g"][0], i["norm_ffn_g"][0], i["norm_mix_g"][1], i["norm_ffn_g"][1],
                                    i["final_g"]])),
        "dcol": _columns(i["ssm_d"][0].reshape(D)),
        "jrow": np.repeat(np.arange(NJ, dtype=f)[None], P, axis=0),
        "slope": np.repeat(slopes[None], P, axis=0),
        "epsc": np.full((P, 1), EPS, f),
        "ndist": ndist,
        "b_re": _blocks(i["ssm_b_re"][0]),
        "b_im": _blocks(i["ssm_b_im"][0]),
        "c_re": _blocks(i["ssm_c_re"][0].transpose(0, 2, 1)),
        "c_im": _blocks(i["ssm_c_im"][0].transpose(0, 2, 1)),
    }


def kernel(**inputs):
    import concourse.bacc as bacc
    from concourse.bass_utils import run_bass_kernel_spmd

    nc = bacc.Bacc("TRN2", target_bir_lowering=False, num_devices=1)
    given = {k: np.asarray(v) for k, v in inputs.items()}
    arrays, tensors = {}, {}
    for name, a in layout(given).items():
        a = np.ascontiguousarray(a)
        arrays[f"in_{name}"] = a
        tensors[name] = nc.dram_tensor(f"in_{name}", a.shape, mybir.dt.from_np(a.dtype), kind="ExternalInput").ap()
    tensors["out"] = nc.dram_tensor("out_0", (P, KT, T), F32, kind="ExternalOutput").ap()
    build(nc, tensors)
    r = run_bass_kernel_spmd(nc, [arrays], core_ids=[0])
    y = r.results[0]["out_0"]
    return np.ascontiguousarray(y.transpose(1, 0, 2).reshape(D, T).T).reshape(1, T, D)
```

```python
from contextlib import ExitStack

import numpy as np

import concourse.bass as bass
from concourse import mybir
from concourse.bass import ds

F32 = mybir.dt.float32
F32R = mybir.dt.float32r
ALU = mybir.AluOpType
ACT = mybir.ActivationFunctionType
AX = mybir.AxisListType

P = 128
D = 1024
KT = D // P
T = 256
HEADS, HD = 16, 64
PAIRS = HEADS // 2
IH = 8
KEEP = T // 4
FF = 2816
FT = FF // P
EPS = 1e-6

RAW, SPL = 6, 3
N_IN = 30
N_OUT = KT
N_FFN = 3 * FT
N_SIN = KT
N_GLU = 2 * KT
W_IN = 0
W_OUT = W_IN + N_IN
W_FFN0 = W_OUT + N_OUT
W_SIN = W_FFN0 + N_FFN
W_GLU = W_SIN + N_SIN
W_FFN1 = W_GLU + N_GLU
N_SLOTS = W_FFN1 + N_FFN
S_KI, S_WI, S_QI, S_Q, S_K, S_V = 0, 1, 2, 6, 14, 22

CH = 6 * D // 512
MS = 4
C_PROJ, C_ATT, C_FFN = 4, 6, 14

LCH = 4
NJ = T // LCH
PR = 32
TWO_PI = 6.283185307179586
ROUND = 12582912.0
C1, C2 = 6.28125, 0.0019350051879882812
C3 = TWO_PI - C1 - C2

NEG = -3.0e38
TAKEN = -3.3e38
MASKED = -1.0e30

PRM = ["lr", "li", "ldt", "dt", "th", "mag", "sin", "cos", "are", "aim", "cre", "cim", "rho", "frac",
       "t0", "t1", "t2", "t3"]
PRM_IN = 3


def build(nc, t):
    with ExitStack() as ctx:
        def sb(name, shape, dt=F32):
            return ctx.enter_context(nc.sbuf_tensor(name, shape, dt))

        def sem(name):
            return ctx.enter_context(nc.semaphore(name))

        x = sb("x", [P, KT, T])
        hh = sb("hh", [P, KT, T], F32R)
        hl = sb("hl", [P, KT, T], F32R)
        raw = sb("raw", [P, RAW, 1024])
        whi = sb("whi", [P, SPL, 1024], F32R)
        wlo = sb("wlo", [P, SPL, 1024], F32R)
        mraw = sb("mraw", [P, MS, 1024])
        gm = sb("gm", [P, 512])
        tmp8 = sb("tmp8", [P, KT * T])
        ffn = sb("ffn", [P, KT * T])
        ah = sb("ah", [P, 2, T], F32R)
        al = sb("al", [P, 2, T], F32R)
        arena = sb("arena", [P, 22528])
        ident = sb("ident", [P, P])
        ones = sb("ones", [P, P])
        craw = sb("craw", [P, KT])
        cond = sb("cond", [P, KT, 3])
        picks = sb("picks", [P, 2])
        prm = sb("prm", [P, len(PRM), PR])
        conv = sb("conv", [P, 2, 4, 2 * FT])
        modc = sb("modc", [P, 2 * 48])
        modb = sb("modb", [P, 2 * 48])
        gains = sb("gains", [P, 5, KT])
        amul = sb("amul", [P, 4, KT])
        dcol = sb("dcol", [P, KT])
        rt = sb("rt", [P, 2])
        diag = sb("diag", [P, 2, P])
        jrow = sb("jrow", [P, NJ])
        slope = sb("slope", [P, HEADS])
        epsc = sb("epsc", [P, 1])
        idle = sb("idle", [P, 1])
        zrow = sb("zrow", [1, 512], mybir.dt.bfloat16)

        tmp = tmp8[:].rearrange("p (k t) -> p k t", k=KT)

        def carve(cursor, n):
            a = arena[:, cursor[0]:cursor[0] + n]
            cursor[0] += n
            return a

        cur = [0]
        qkv = carve(cur, N_IN * T).rearrange("p (n t) -> p n t", n=N_IN)
        stage = carve(cur, 2 * 3 * T).rearrange("p (a n t) -> p a n t", a=2, n=3)
        rbuf = carve(cur, 8 * T).rearrange("p (b h t) -> p b h t", b=4, h=2)
        scr = carve(cur, 384)
        msk = carve(cur, 384)
        bm = carve(cur, 4 * 384).rearrange("p (a e t) -> p a e t", a=2, e=2)
        sp = carve(cur, 4 * 384).rearrange("p (a e t) -> p a e t", a=2, e=2)
        pt = carve(cur, 4 * 384).rearrange("p (a e t) -> p a e t", a=2, e=2)
        vsb = carve(cur, 2 * T).rearrange("p (a k d) -> p a k d", a=2, k=2)
        max8 = carve(cur, 16).rearrange("p (q n) -> p q n", q=2)
        wit = carve(cur, 16).rearrange("p (q n) -> p q n", q=2)
        nmx = carve(cur, 8).rearrange("p (a n) -> p a n", a=2)
        rs = carve(cur, 8).rearrange("p (a n) -> p a n", a=2)
        ri = carve(cur, 8).rearrange("p (a n) -> p a n", a=2)
        ndist = carve(cur, 384)
        ATT_END = cur[0]
        cur = [0]
        bpow = carve(cur, 8192).rearrange("p (r n l c) -> p r n l c", r=2, n=PR, l=LCH)
        cpow = carve(cur, 8192).rearrange("p (k r n) -> p k r n", k=4, r=2)
        tpool = carve(cur, 2048)
        tab = carve(cur, 4096)
        assert ATT_END <= cur[0] - 4096 and cur[0] <= 22528
        t1, t2 = tpool[:, 0:1024], tpool[:, 1024:2048]
        rot1 = tpool[:, 0:512].rearrange("p (r q j) -> p r q j", r=2, q=4)
        rot2 = tpool[:, 512:1024].rearrange("p (r q j) -> p r q j", r=2, q=4)
        hst = tpool[:, 1024:1536].rearrange("p (r q j) -> p r q j", r=2, q=4)
        yv = tpool[:, 1536:2048].rearrange("p (a t) -> p a t", a=2)
        yg = ffn[:].rearrange("p (m t) -> p m t", m=KT)
        kbd = mraw[:].rearrange("p a (m l n) -> p (a m) l n", m=2, l=LCH)
        tcos, tsin = tab[:, 0:2048], tab[:, 2048:4096]
        tcos_v = tcos.rearrange("p (n j) -> p n j", j=NJ)
        tsin_v = tsin.rearrange("p (n j) -> p n j", j=NJ)
        va = tmp8[:, 0:512].rearrange("p (q r j) -> p q r j", q=4, r=2)
        vb = tmp8[:, 512:1024].rearrange("p (q r j) -> p q r j", q=4, r=2)
        ust = tmp8[:, 1024:1536].rearrange("p (a q j) -> p a q j", a=2, q=4)
        g2 = tmp8[:, 1536:2048].rearrange("p (r q j) -> p r q j", r=2, q=4)
        bpow_r = bpow.rearrange("p r n l c -> p r (n l c)")
        u = ffn[:].rearrange("p (m j l) -> p m j l", m=KT, l=LCH)
        cb = ffn[:, 0:1024].rearrange("p (a e t) -> p a e t", a=2, e=2)
        sg = ffn[:, 1024:1536].rearrange("p (a t) -> p a t", a=2)
        ab = ffn[:, 1536:2048].rearrange("p (a t) -> p a t", a=2)

        mslot = ([mraw[:, s, :] for s in range(MS)],
                 [tmp8[:, 0:1024], tmp8[:, 1024:2048], ffn[:, 0:1024], ffn[:, 1024:2048]])
        early = arena[:, 0:3 * MS * 1024].rearrange("p (s n) -> p s n", n=1024)
        qkv_f = arena[:, 0:N_IN * T]
        hh_f = hh[:].rearrange("p k t -> p (k t)")
        hl_f = hl[:].rearrange("p k t -> p (k t)")

        def pr(name):
            return prm[:, PRM.index(name), :]

        acc = ctx.enter_context(nc.psum_tensor("acc", [P, 4, 512], F32))
        up = ctx.enter_context(nc.psum_tensor("up", [P, 2, 512], F32))
        gv = ctx.enter_context(nc.psum_tensor("gv", [P, 512], F32))
        misc = ctx.enter_context(nc.psum_tensor("misc", [P, 512], F32))

        diag_ready, rstd_ready = sem("diag_ready"), sem("rstd_ready")
        fold_done = sem("fold_done")
        cond_in = sem("cond_in")
        prm_in = sem("prm_in")
        early_in = sem("early_in")
        small_in = sem("small_in")
        m_early = [sem(f"m_early{j}") for j in range(3 * MS)]
        sum_row, csum = sem("sum_row"), sem("csum")
        x_in = sem("x_in")
        w_loaded = [sem(f"w_loaded{j}") for j in range(RAW)]
        m_loaded = [sem(f"m_loaded{j}") for j in range(MS)]
        m_odd = [sem(f"m_odd{j}") for j in range(MS)]
        hi_ready, lo_ready, slot_used = sem("hi_ready"), sem("lo_ready"), sem("slot_used")
        mod_used = sem("mod_used")
        gm_ready = sem("gm_ready")
        cols_done = sem("cols_done")
        mod_col = sem("mod_col")
        amul_ready = sem("amul_ready")
        set_up = sem("set_up")
        cond_ready = sem("cond_ready")
        prm_v, prm_a = sem("prm_v"), sem("prm_a")
        x_upd = sem("x_upd")
        sq_ready, ssum, rt_ready, ri_norm, hp_ready = (
            sem("sq_ready"), sem("ssum"), sem("rt_ready"), sem("ri_norm"), sem("hp_ready"))
        act_hi, act_lo = sem("act_hi"), sem("act_lo")
        qkv_ready = sem("qkv_ready")
        idx_done, idx_relu, idx_acc = sem("idx_done"), sem("idx_relu"), sem("idx_acc")
        wit_ready = sem("wit_ready")
        sel = sem("sel")
        stage_ready, s_done, v_ready, bias_ready, sp_ready, mx_ready = (
            sem("stage_ready"), sem("s_done"), sem("v_ready"), sem("bias_ready"), sem("sp_ready"), sem("mx_ready"))
        exp_done, ri_ready, p_ready, tr_done, tr_out, pv_done = (
            sem("exp_done"), sem("ri_ready"), sem("p_ready"), sem("tr_done"), sem("tr_out"), sem("pv_done"))
        tap, conv_s, sg_ready, am, a_hi, a_lo = (
            sem("tap"), sem("conv_s"), sem("sg_ready"), sem("am"), sem("a_hi"), sem("a_lo"))
        ssm_in = sem("ssm_in")
        pw = sem("pw")
        k_done, k_out = sem("k_done"), sem("k_out")
        bt_done, bt_act, bt_dve = sem("bt_done"), sem("bt_act"), sem("bt_dve")
        kz = sem("kz")
        st_done, st_ready = sem("st_done"), sem("st_ready")
        tab_arg, tab_ready = sem("tab_arg"), sem("tab_ready")
        u_ready = sem("u_ready")
        v_done, v_read, g_ready, g2_ready, rot_s, h_ready = (
            sem("v_done"), sem("v_read"), sem("g_ready"), sem("g2_ready"), sem("rot_s"), sem("h_ready"))
        y_done, yv_ready, yg_ready = sem("y_done"), sem("yv_ready"), sem("yg_ready")
        sig_ready, glu_s = sem("sig_ready"), sem("glu_s")
        fin_ready, out_done = sem("fin_ready"), sem("out_done")

        N_PRM, N_EARLY, N_SMALL = 2, 6, 4
        N_SSM = 4

        block = ctx.enter_context(nc.Block())

        @block.sync
        def _(sp_):
            def load_w(n, i=0, free=True):
                if free:
                    sp_.wait_ge(lo_ready, n + RAW * i - RAW + 1)
                sp_.dma_start(raw[:, n % RAW, :], t["w"][n + RAW * i, :, :]).then_inc(w_loaded[n % RAW], 16)

            def load_m(c, i=0):
                for s in range(MS):
                    if not (isinstance(c, int) and isinstance(i, int) and c + i == 0):
                        sp_.wait_ge(mod_used, (c + i - 1) * MS + s + 1)
                    sp_.dma_start(mraw[:, s, :], t["mw"][(c + i) * MS + s, :, :]).then_inc(m_loaded[s], 16)

            sp_.dma_start(craw[:], t["cond"]).then_inc(cond_in, 16)
            for dst, name in ((prm[:, 0:PRM_IN, :], "prm"), (jrow[:], "jrow")):
                sp_.dma_start(dst, t[name]).then_inc(prm_in, 16)
            load_m(0)
            for dst, name in ((modb[:], "modb"), (ones[:], "ones"), (ident[:], "ident"), (gains[:], "gains"),
                              (epsc[:], "epsc"), (picks[:], "picks")):
                sp_.dma_start(dst, t[name]).then_inc(early_in, 16)
            for k in range(0, KT, 2):
                sp_.dma_start(x[:, k:k + 2, :], t["x"][:, k:k + 2, :]).then_inc(x_in, 16)
            for s in range(3 * MS):
                sp_.dma_start(early[:, s, :], t["mw"][MS + s, :, :]).then_inc(m_early[s], 16)
            for n in range(RAW):
                load_w(n, free=False)
            for dst, name in ((conv[:], "conv"), (dcol[:], "dcol"), (slope[:], "slope"), (ndist, "ndist")):
                sp_.dma_start(dst, t[name]).then_inc(small_in, 16)
            load_m(4)
            with sp_.Fori(0, 4) as i:
                for n in range(RAW, 2 * RAW):
                    load_w(n, i)
            for n in range(W_OUT, W_OUT + RAW):
                load_w(n)

            def load_att(c, i=0):
                for s in range(MS):
                    sp_.wait_ge(mod_used, (c - 2 + 2 * i) * MS + s + 1)
                    sp_.dma_start(mslot[c % 2][s], t["mw"][(c + 2 * i) * MS + s, :, :]).then_inc((m_loaded, m_odd)[c % 2][s], 16)

            with sp_.Fori(0, 3) as i:
                load_att(C_ATT + 2, i)
                load_att(C_ATT + 3, i)
            load_att(C_FFN)
            for n in range(W_OUT + RAW, W_FFN0 + RAW):
                load_w(n)
            with sp_.Fori(0, 9) as i:
                for n in range(W_FFN0 + RAW, W_FFN0 + 2 * RAW):
                    load_w(n, i)
                load_m(C_FFN + 1, i)
            for n in range(W_FFN0 + 10 * RAW, W_FFN0 + 11 * RAW):
                load_w(n)
            for n in range(W_SIN, W_SIN + 3):
                load_w(n)
            first = W_SIN + 3
            loops = (N_SLOTS - first) // RAW
            with sp_.Fori(0, loops) as i:
                for n in range(first, first + RAW):
                    load_w(n, i)
            for n in range(first + RAW * loops, N_SLOTS):
                load_w(n)
            for m in range(KT):
                sp_.wait_ge(fin_ready, m + 1)
                sp_.dma_start(t["out"][:, m, :], tmp[:, m, :]).then_inc(out_done, 16)
            sp_.wait_ge(out_done, 16 * KT)

        @block.tensor
        def _(pe):
            def three(out, n, cols, xh, xl, first, last, skip=False):
                w_h, w_l = whi[:, n % SPL, cols:cols + P], wlo[:, n % SPL, cols:cols + P]
                pe.matmul(out, w_h, xh, start=first, stop=False, skip_group_check=skip)
                pe.matmul(out, w_h, xl, start=False, stop=False, skip_group_check=skip)
                return pe.matmul(out, w_l, xh, start=False, stop=last, skip_group_check=skip)

            def project(out, n, i=0, phase=None):
                pe.wait_ge(lo_ready, n + RAW * i + 1)
                for k in range(KT):
                    if phase is not None:
                        pe.wait_ge(act_lo, KT * phase + k + 1)
                    mm = three(out, n, k * P, hh[:, k, :], hl[:, k, :], k == 0, k == KT - 1)
                mm.then_inc(slot_used, 1)

            def gemv(c, i=0, slots=range(MS)):
                odd = c % 2
                if c >= 2 and not odd and slots[0] == 0:
                    pe.wait_ge(gm_ready, c // 2 + i)
                for s in slots:
                    src = mraw[:, s, :]
                    if c >= C_FFN:
                        pe.wait_ge(m_loaded[s], 16 * (c - C_FFN // 2 + 2 * i))
                    elif c == 0:
                        pe.wait_ge(m_loaded[s], 16)
                    elif c < 4:
                        src = early[:, (c - 1) * MS + s, :]
                        pe.wait_ge(m_early[(c - 1) * MS + s], 16)
                    elif not odd:
                        pe.wait_ge(m_loaded[s], 16 * (c // 2 + i))
                    else:
                        src = mslot[1][s]
                        pe.wait_ge(m_odd[s], 16 * ((c - 3) // 2 + i))
                    for kk in range(2):
                        k = 2 * s + kk
                        j = k % 4
                        mm = pe.matmul(gv[32 * j:32 * j + 2, :], cond[:, k, 1 - odd:3 - odd],
                                       src[:, kk * 512:kk * 512 + 512], start=(k < 4 and not odd),
                                       stop=(k >= 4 and odd == 1), skip_group_check=True)
                    mm.then_inc(mod_used, 1)

            def columns(pair, i=0):
                pe.wait_ge(gm_ready, pair + i + 1)
                if pair:
                    pe.wait_ge(mod_col, pair + i)
                for q in range(4):
                    mm = pe.matmul(misc[:, 2 * q:2 * q + 2], gm[:, q * P:(q + 1) * P], picks[:], start=True, stop=True)
                mm.then_inc(cols_done, 1)

            def open_bank(bank):
                pe.matmul(bank, zrow[:, 0:P], zrow[:], start=True, stop=True, skip_group_check=True)

            def part(out, n, tiles, phase):
                pe.wait_ge(lo_ready, n + 1)
                for k in tiles:
                    pe.wait_ge(act_lo, KT * phase + k + 1)
                    mm = three(out, n, k * P, hh[:, k, :], hl[:, k, :], k == 0, k == KT - 1, skip=True)
                    if k == KT - 1:
                        mm.then_inc(slot_used, 1)

            def project_two(outs, n, phase, opened=False, tiles=range(KT)):
                pe.wait_ge(lo_ready, n + 2)
                for k in tiles:
                    pe.wait_ge(act_lo, KT * phase + k + 1)
                    for j in range(2):
                        mm = three(outs[j], n + j, k * P, hh[:, k, :], hl[:, k, :], k == 0 and not opened,
                                   k == KT - 1, skip=True)
                        if k == KT - 1:
                            mm.then_inc(slot_used, 1)

            def norm(n, pairs, spread, meanwhile=None):
                pe.wait_ge(gm_ready, pairs)
                for k in range(KT):
                    pe.wait_ge(sq_ready, KT * n + k + 1)
                    mm = pe.matmul(gv[32 * (k % 4):32 * (k % 4) + 1, 0:T], ones[:, 0:1], tmp[:, k, :],
                                   start=(k < 4), stop=(k >= 4))
                mm.then_inc(ssum, 1)
                pe.wait_ge(sum_row, n + 1)
                pe.wait_ge(mod_col, pairs)
                for h in range(2):
                    mm = pe.matmul(misc[:, 8 + h:9 + h], gm[:, h * P:(h + 1) * P], picks[:, 0:1], start=True, stop=True)
                mm.then_inc(csum, 1)
                if meanwhile:
                    meanwhile()
                if n:
                    spread_root(n, spread)

            def spread_root(n, spread):
                for h in range(2):
                    pe.wait_ge(diag_ready, 2 * n + h + 1)
                    mm = pe.matmul(spread[:, h * P:(h + 1) * P], ones[:], diag[:, h, :], start=True, stop=True)
                mm.then_inc(rstd_ready, 1)

            pe.wait_ge(set_up, 4)
            pe.wait_ge(cond_ready, 1)
            gemv(0)
            gemv(1)
            pe.wait_ge(early_in, 16 * N_EARLY)
            columns(0)
            norm(0, 1, None)
            gemv(2)
            spread_root(0, up[:, 0, 0:T])
            gemv(3)
            columns(1)

            for n in range(RAW):
                if n >= 2:
                    pe.wait_ge(qkv_ready, n - 1)
                if n == 0:
                    project_two((up[:, 0, 0:T], up[:, 1, 0:T]), 0, 0)
                elif n > 1:
                    project(up[:, n % 2, 0:T], n)
                if n == 3:
                    gemv(C_PROJ)
            pe.wait_ge(mod_col, C_PROJ // 2)
            pe.wait_ge(qkv_ready, RAW)
            for qt in range(2):
                mm = pe.transpose(misc[:, qt * P:(qt + 1) * P], qkv[:, S_WI, qt * P:(qt + 1) * P], ident[:])
            mm.then_inc(idx_done, 1)
            for step, (qt, keys) in enumerate(((1, T), (0, P))):
                if step:
                    gemv(C_PROJ + 1)
                    pe.wait_ge(idx_relu, 1)
                for h in range(IH):
                    r = HD * (h % 2)
                    mm = pe.matmul(acc[:, h % 4, (h // 4) * T:(h // 4) * T + keys],
                                   qkv[r:r + HD, S_QI + h // 2, qt * P:(qt + 1) * P], qkv[r:r + HD, S_KI, 0:keys],
                                   start=True, stop=True)
                mm.then_inc(idx_done, 1)
            pe.wait_ge(wit_ready, 1)
            columns(C_PROJ // 2)
            with pe.Fori(1, N_IN // RAW) as i:
                for n in range(RAW):
                    pe.wait_ge(qkv_ready, n - 1 + RAW * i)
                    project(up[:, n % 2, 0:T], n, i)

            pe.wait_ge(idx_relu, 2)
            pe.wait_ge(qkv_ready, N_IN)

            def scores(p, a):
                pe.wait_ge(stage_ready, 6 if isinstance(p, int) and p < 2 else 3 * (p + 1))
                if not (isinstance(p, int) and p < 2):
                    pe.wait_ge(v_ready, p - 1)
                for e in range(2):
                    r = HD * e
                    pe.matmul(acc[:, 2 * a + e, 0:T], stage[r:r + HD, a, 0, P:T], stage[r:r + HD, a, 1, :],
                              start=True, stop=True)
                    pe.matmul(acc[:, 2 * a + e, T:T + P], stage[r:r + HD, a, 0, 0:P], stage[r:r + HD, a, 1, 0:P],
                              start=True, stop=True)
                for kt in range(2):
                    mm = pe.transpose(acc[:, 2 * a + kt, 384:512], stage[:, a, 2, kt * P:(kt + 1) * P], ident[:])
                mm.then_inc(s_done, 1)

            def turn(p, a):
                pe.wait_ge(p_ready, 4 * (p + 1))
                pe.wait_ge(act_lo, KT + p)
                for e in range(2):
                    for b, src in ((0, T), (1, 0), (2, P)):
                        mm = pe.transpose(up[:, e, b * P:(b + 1) * P], sp[:, a, e, src:src + P], ident[:])
                mm.then_inc(tr_done, 1)

            def values(p, a):
                pe.wait_ge(tr_out, p + 1)
                pe.wait_ge(v_ready, p + 1)
                for e in range(2):
                    rows = slice(HD * e, HD * e + HD)
                    v0, v1 = vsb[:, a, 0, rows], vsb[:, a, 1, rows]
                    pe.matmul(up[rows, 0, 384:512], v0, pt[:, a, e, 0:P], start=True, stop=True)
                    pe.matmul(up[rows, 1, 384:512], v0, pt[:, a, e, P:2 * P], start=True, stop=False)
                    mm = pe.matmul(up[rows, 1, 384:512], v1, pt[:, a, e, 2 * P:3 * P], start=False, stop=True)
                mm.then_inc(pv_done, 1)

            scores(0, 0)
            scores(1, 1)
            gemv(C_ATT)
            gemv(C_ATT + 1)
            scores(2, 0)
            turn(0, 0)
            columns(C_ATT // 2)
            values(0, 0)
            gemv(C_ATT + 2)
            with pe.Fori(0, 2) as i:
                for h in range(2):
                    scores(2 * i + 3 + h, (1 + h) % 2)
                    turn(2 * i + 1 + h, (1 + h) % 2)
                    if h == 0:
                        gemv(C_ATT + 3, i, range(2))
                    else:
                        columns(C_ATT // 2 + 1, i)
                    values(2 * i + 1 + h, (1 + h) % 2)
                    if h == 0:
                        gemv(C_ATT + 3, i, range(2, MS))
                    else:
                        gemv(C_ATT + 4, i)
            for p in range(5, PAIRS):
                if p + 2 < PAIRS:
                    scores(p + 2, p % 2)
                if p == PAIRS - 1:
                    pe.wait_ge(v_ready, p)
                    part(acc[:, 0, 0:T], W_OUT, range(6), 1)
                turn(p, p % 2)
                if p == PAIRS - 1:
                    part(acc[:, 1, 0:T], W_OUT + 1, range(4), 1)
                if p == 6:
                    columns((C_ATT + p) // 2)
                values(p, p % 2)
                if p + 2 < PAIRS:
                    gemv(C_ATT + p + 2)

            part(acc[:, 1, 0:T], W_OUT + 1, range(4, 6), 1)
            project_two((acc[:, 0, 0:T], acc[:, 1, 0:T]), W_OUT, 1, tiles=range(6, KT))
            for m in range(2, KT):
                if m >= 4:
                    pe.wait_ge(x_upd, m - 3)
                project(acc[:, m % 4, 0:T], W_OUT + m)
            norm(1, C_FFN // 2, misc[:, T:2 * T])

            def ffn_phase(layer, base, phase):
                def up_step(par, n_v, i=0):
                    project(up[:, par, 0:T], n_v, i)
                    project(up[:, par, T:2 * T], n_v + 1, i)

                def down_step(par, n, i, s, last=False):
                    pe.wait_ge(lo_ready, n + RAW * i + 1)
                    pe.wait_ge(a_lo, FT * layer + s + 1)
                    for m in range(KT):
                        mm = three(acc[:, m // 2, (m % 2) * T:(m % 2 + 1) * T], n, m * P, ah[:, par, :], al[:, par, :],
                                   False, last, skip=True)
                        if last and m % 2 and m < KT - 1:
                            mm.then_inc(fold_done, 1)
                    mm.then_inc(slot_used, 1)

                for bank in (acc[:, 0, :], acc[:, 1, :], acc[:, 2, :], acc[:, 3, :], up[:, 0, :]):
                    open_bank(bank)
                project_two((up[:, 0, 0:T], up[:, 0, T:2 * T]), base, phase, opened=True)
                up_step(1, base + 2)
                def two_steps(i, pair=None):
                    for h in range(2):
                        n = base + 4 + 3 * h
                        pe.wait_ge(conv_s, 4 * (FT * layer + 2 * i + h + 1))
                        up_step(h, n, i)
                        down_step(h, n + 2, i, 2 * i + h)
                        if pair is not None and h == 0:
                            columns(C_FFN // 2, pair)

                if layer == 0:
                    with pe.Fori(0, 5) as i:
                        gemv(C_FFN, i)
                        two_steps(2 * i)
                        gemv(C_FFN + 1, i)
                        two_steps(2 * i + 1, i)
                else:
                    with pe.Fori(0, 10) as i:
                        two_steps(i)
                down_step(0, base + 64, 0, 20)
                down_step(1, base + 65, 0, 21, last=True)

            ffn_phase(0, W_FFN0, 2)
            def lag_kernels(mts):
                for mt in mts:
                    for q in range(4):
                        pair = mt * 4 + q
                        for r in range(2):
                            mm = pe.matmul(up[32 * q:32 * q + 32, mt // 4, (mt % 4) * P:(mt % 4 + 1) * P],
                                           bpow[:, r, pair, LCH - 1, :], cpow[:, :, r, pair * 32:pair * 32 + 32],
                                           start=(r == 0), stop=(r == 1))
                return mm

            pe.wait_ge(pw, PW_K)
            lag_kernels(range(0, 5))
            norm(2, CH, misc[:, T:2 * T], lambda: lag_kernels(range(5, KT - 1)))
            lag_kernels(range(KT - 1, KT)).then_inc(k_done, 1)

            def transpose_b(mt):
                if mt:
                    pe.wait_ge(bt_act, mt)
                    pe.wait_ge(bt_dve, mt)
                for r, bank in ((0, gv), (1, misc)):
                    for q in range(4):
                        mm = pe.transpose(bank[:, q * P:(q + 1) * P], bpow_r[:, r, (4 * mt + q) * P:(4 * mt + q + 1) * P],
                                          ident[:])
                mm.then_inc(bt_done, 1)

            def stack_u(mt):
                pe.wait_ge(u_ready, mt + 1)
                for q in range(4):
                    for l in range(LCH):
                        mm = pe.matmul(acc[32 * l:32 * l + 32, mt % 2, T + q * NJ:T + (q + 1) * NJ],
                                       ident[:, 32 * q:32 * q + 32], u[:, mt, :, l], start=True, stop=True)
                mm.then_inc(st_done, 1)

            def inject(mt):
                pe.wait_ge(bt_act, mt + 1)
                pe.wait_ge(bt_dve, mt + 1)
                pe.wait_ge(st_ready, mt + 1)
                if mt >= 2:
                    pe.wait_ge(v_read, 2 * mt - 2)
                for r in range(2):
                    for q in range(4):
                        c = (4 * mt + q) * P
                        mm = pe.matmul(acc[:, 2 + mt % 2, (2 * q + r) * NJ:(2 * q + r + 1) * NJ],
                                       bpow_r[:, r, c:c + P], ust[:, mt % 2, q, :], start=True, stop=True)
                mm.then_inc(v_done, 1)

            def lags(mt):
                if mt == 0:
                    pe.wait_ge(k_out, 4)
                if mt >= 2:
                    pe.wait_ge(yv_ready, mt - 1)
                y = up[:, mt % 2, 0:T].rearrange("p (j l) -> p j l", l=LCH)
                for lag in range(LCH):
                    pe.matmul(y[:, :, lag:LCH], kbd[:, mt, lag, :], u[:, mt, :, 0:LCH - lag],
                              start=(lag == 0), stop=False, skip_group_check=True)

            def emit(mt):
                if mt == 0:
                    pe.wait_ge(pw, PW_ALL)
                pe.wait_ge(h_ready, 2 * (mt + 1))
                y = up[:, mt % 2, 0:T].rearrange("p (j l) -> p j l", l=LCH)
                for l in range(LCH):
                    for r in range(2):
                        for q in range(4):
                            pair = mt * 4 + q
                            mm = pe.matmul(y[32 * q:32 * q + 32, :, l], cpow[:, (l + 1) % 4, r, pair * 32:pair * 32 + 32],
                                           hst[:, r, q, :], start=False, stop=(l == LCH - 1 and r == 1),
                                           skip_group_check=True)
                mm.then_inc(y_done, 1)

            for m in range(KT + 2):
                if m < KT:
                    if m >= 2:
                        pe.wait_ge(st_ready, m - 1)
                    if m == 0:
                        project_two((acc[:, 0, 0:T], acc[:, 1, 0:T]), W_SIN, 3)
                    elif m > 1:
                        project(acc[:, m % 2, 0:T], W_SIN + m)
                    transpose_b(m)
                if 1 <= m <= KT:
                    inject(m - 1)
                    lags(m - 1)
                if m == KT:
                    pe.wait_ge(st_ready, KT)
                if m >= KT:
                    project_two((acc[:, 0, 0:T], acc[:, 1, 0:T]), W_GLU, 4,
                                tiles=range(2) if m == KT else range(2, KT - 1))
                if m >= 2:
                    emit(m - 2)
                if m < KT:
                    stack_u(m)

            for m in range(KT):
                for g in range(2):
                    if m >= 2:
                        pe.wait_ge(glu_s, m - 1)
                    if m == 0 and g == 0:
                        part(acc[:, 2, 0:T], W_GLU + 2, range(2), 4)
                        project_two((acc[:, 0, 0:T], acc[:, 1, 0:T]), W_GLU, 4, tiles=range(KT - 1, KT))
                    elif m == 1 and g == 0:
                        part(acc[:, 2, 0:T], W_GLU + 2, range(2, KT), 4)
                    elif m > 0:
                        project(acc[:, 2 * (m % 2) + g, 0:T], W_GLU + 2 * m + g)
            pe.wait_ge(set_up, 5)
            norm(3, CH, misc[:, T:2 * T])
            ffn_phase(1, W_FFN1, 5)
            norm(4, CH, misc[:, T:2 * T])

        @block.scalar
        def _(act):
            def split_hi(n, i=0, ring=True):
                act.wait_ge(w_loaded[n % RAW], 16 * (n // RAW + 1 + i))
                if ring:
                    act.wait_ge(slot_used, n + RAW * i - SPL + 1)
                act.activation(whi[:, n % SPL, :], raw[:, n % RAW, :], ACT.Copy).then_inc(hi_ready, 1)

            def row_out(pair, i=0):
                act.wait_ge(mod_used, 2 * MS * (pair + i + 1))
                if pair:
                    act.wait_ge(cols_done, pair + i)
                act.activation(gm[:], gv[:], ACT.Copy).then_inc(gm_ready, 1)

            def load_m(c, i=0):
                for s in range(MS):
                    act.dma_start(mslot[c % 2][s], t["mw"][(c + i) * MS + s, :, :]).then_inc((m_loaded, m_odd)[c % 2][s], 16)

            def square(norm, k):
                if norm == 0:
                    if k % 2 == 0:
                        act.wait_ge(x_in, 64)
                else:
                    act.wait_ge(x_upd, KT * (norm - 1) + k + 1)
                act.activation(tmp[:, k, :], x[:, k, :], ACT.Square).then_inc(sq_ready, 1)

            def root(norm):
                act.wait_ge(ssum, norm + 1)
                act.wait_ge(cols_done, 1 if norm == 0 else C_FFN // 2 if norm == 1 else CH)
                act.activation(gm[:, 0:T], gv[:, 0:T], ACT.Copy).then_inc(sum_row, 1)
                act.wait_ge(csum, norm + 1)
                act.activation(rt[:], misc[:, 8:10], ACT.Sqrt, scale=1.0 / D, bias=epsc[:, 0:1]).then_inc(rt_ready, 1)

            def fetch_root():
                act.activation(idle[:], epsc[:], ACT.Sqrt)

            def norm_hi(norm, phase, sh):
                for k in range(KT):
                    act.wait_ge(hp_ready, KT * norm + k + 1)
                    act.activation(hh[:, k, :], tmp[:, k, :], ACT.Identity, bias=modc[:, sh + k:sh + k + 1]).then_inc(act_hi, 1)

            act.wait_ge(cond_in, 16)
            act.activation(cond[:, :, 1], craw[:], ACT.Silu).then_inc(cond_ready, 1)
            act.wait_ge(prm_in, 16 * N_PRM)
            act.activation(pr("dt"), pr("ldt"), ACT.Exp).then_inc(prm_a, 1)
            act.wait_ge(prm_v, 1)
            act.activation(pr("mag"), pr("t0"), ACT.Exp).then_inc(prm_a, 1)
            act.wait_ge(prm_v, PRM_SIN)
            act.activation(pr("sin"), pr("t2"), ACT.Sin).then_inc(prm_a, 1)
            act.activation(pr("cos"), pr("t3"), ACT.Sin).then_inc(prm_a, 1)
            row_out(0)
            for k in range(KT):
                square(0, k)
            act.wait_ge(early_in, 16 * N_EARLY)
            root(0)
            row_out(1)
            for n in range(SPL):
                split_hi(n, ring=False)
            act.wait_ge(mod_col, 2)
            norm_hi(0, 0, 8)

            for n in range(RAW):
                act.wait_ge(slot_used, n + 1)
                act.activation(qkv[:, n, :], up[:, n % 2, 0:T], ACT.Copy).then_inc(qkv_ready, 1)
                split_hi(n + SPL)
                if n == 3:
                    act.wait_ge(act_lo, KT)
                    load_m(C_PROJ + 1)
                    act.wait_ge(mod_used, MS * (C_PROJ + 1))
                    load_m(C_PROJ + 2)
            for step, keys in enumerate((T, P)):
                act.wait_ge(idx_done, step + 2)
                if step:
                    row_out(C_PROJ // 2)
                    load_m(C_PROJ + 3)
                    act.wait_ge(idx_acc, 8)
                act.activation(rbuf[:, :, :, 0:keys], acc[:].rearrange("p b (h t) -> p b h t", h=2)[:, :, :, 0:keys],
                               ACT.Relu, scale=HD ** -0.5).then_inc(idx_relu, 1)
            act.wait_ge(tab_arg, TAB_STEPS)
            act.activation(tab, tab, ACT.Sin, scale=TWO_PI * (1 - 2 ** -23)).then_inc(tab_ready, 1)
            with act.Fori(1, N_IN // RAW) as i:
                for n in range(RAW):
                    act.wait_ge(slot_used, n + RAW * i + 1)
                    act.activation(qkv_f[:, ds((n + RAW * i) * T, T)], up[:, n % 2, 0:T], ACT.Copy).then_inc(qkv_ready, 1)
                    split_hi(n + SPL, i)

            def exps(p, a):
                act.wait_ge(mx_ready, 2 * (p + 1))
                for e in range(2):
                    act.activation(sp[:, a, e, 0:T], sp[:, a, e, 0:T], ACT.Exp, bias=nmx[:, a, e:e + 1],
                                   accum_out=rs[:, a, e:e + 1]).then_inc(exp_done, 1)
                    act.activation(sp[:, a, e, T:T + P], sp[:, a, e, T:T + P], ACT.Exp,
                                   bias=nmx[:, a, 2 + e:3 + e], accum_out=rs[:, a, 2 + e:3 + e]).then_inc(exp_done, 1)

            def turned_out(p, a):
                act.wait_ge(tr_done, p + 1)
                act.activation(pt[:, a, :, :], up[:, :, 0:384], ACT.Copy).then_inc(tr_out, 1)
                act.wait_ge(pv_done, p + 1)
                act.activation(hh_f[:, ds(p * T, T)].rearrange("p (b t) -> p b t", b=2), up[:, :, 384:512],
                               ACT.Copy).then_inc(act_hi, 1)

            act.activation(idle[:], epsc[:], ACT.Exp)
            exps(0, 0)
            exps(1, 1)
            row_out(C_ATT // 2)
            turned_out(0, 0)
            with act.Fori(0, 2) as i:
                for h in range(2):
                    exps(2 * i + 2 + h, h % 2)
                    if h:
                        row_out(C_ATT // 2 + 1, i)
                    turned_out(2 * i + 1 + h, (1 + h) % 2)
            for p in range(5, PAIRS):
                if p + 1 < PAIRS:
                    exps(p + 1, (p + 1) % 2)
                if p == 6:
                    row_out((C_ATT + p) // 2)
                turned_out(p, p % 2)

            fetch_root()
            for m in range(KT):
                if m < KT - 1:
                    split_hi(W_OUT + m + SPL)
                square(1, m)
            root(1)
            split_hi(W_FFN0 + 2)
            norm_hi(1, 2, 24)

            def ffn_phase(layer, base):
                def chain_a(par, s, need):
                    act.wait_ge(slot_used, need)
                    for e in range(2):
                        act.activation(cb[:, par, e, :], up[:, par, e * T:(e + 1) * T], ACT.Identity,
                                       scale=conv[:, layer, 2, ds(s + e * FT, 1)],
                                       bias=conv[:, layer, 3, ds(s + e * FT, 1)]).then_inc(tap, 1)

                def chain_b(par, s, cnt, down_used=None):
                    act.wait_ge(conv_s, 4 * (cnt + 1))
                    act.activation(sg[:, par, :], cb[:, par, 1, :], ACT.Silu).then_inc(sg_ready, 1)
                    act.wait_ge(am, cnt + 1)
                    if down_used is not None:
                        act.wait_ge(slot_used, down_used)
                    act.activation(ah[:, par, :], ab[:, par, :], ACT.Copy).then_inc(a_hi, 1)

                off = FT * layer
                def step(h, s, c, i=0, extra=None):
                    chain_a(h, s, c + RAW * i)
                    if extra is not None:
                        row_out(C_FFN // 2, extra)
                    if c + 2 < N_SLOTS:
                        split_hi(c + 2, i)
                    chain_b(h, s, off + s, c + 1 + RAW * i)
                    if c + 4 < base + N_FFN:
                        split_hi(c + 3, i)
                        split_hi(c + 4, i)

                split_hi(base + 3)
                chain_a(0, 0, base + 2)
                split_hi(base + 4)
                chain_b(0, 0, off)
                split_hi(base + 5)
                chain_a(1, 1, base + 4)
                split_hi(base + 6)
                chain_b(1, 1, off + 1)
                split_hi(base + 7)
                def two_steps(i, extra=None):
                    for h in range(2):
                        step(h, 2 * i + 2 + h, base + 6 + 3 * h, i, extra if h == 0 else None)

                if layer == 0:
                    with act.Fori(0, 4) as i:
                        two_steps(2 * i)
                        two_steps(2 * i + 1, i)
                    two_steps(8)
                else:
                    with act.Fori(0, 9) as i:
                        two_steps(i)
                for h in range(2):
                    step(h, 20 + h, base + 60 + 3 * h, 0, 4 if layer == 0 and h == 0 else None)

            act.wait_ge(small_in, 16 * N_SMALL)
            ffn_phase(0, W_FFN0)
            split_hi(W_SIN)
            fetch_root()
            for k in range(KT):
                square(2, k)
            split_hi(W_SIN + 1)
            split_hi(W_SIN + 2)
            root(2)
            norm_hi(2, 3, 56)
            def lags_out():
                act.wait_ge(k_done, 1)
                act.wait_ge(kz, 1)
                for q in (1, 3):
                    rows = slice(32 * q, 32 * q + 32)
                    act.activation(kbd[rows, :, :, 32 * q:32 * q + 32],
                                   up[rows, :, :].rearrange("p b (m l n) -> p (b m) l n", m=4, l=LCH),
                                   ACT.Copy).then_inc(k_out, 1)

            def gelu(mt):
                act.wait_ge(yv_ready, mt + 1)
                act.activation(yg[:, mt, :], yv[:, mt % 2, :], ACT.Gelu_apprx_tanh).then_inc(yg_ready, 1)

            def hi(mt):
                act.wait_ge(yg_ready, mt + 1)
                act.activation(hh[:, mt, :], yg[:, mt, :], ACT.Copy).then_inc(act_hi, 1)

            for m in range(KT + 2):
                if m < KT:
                    act.wait_ge(slot_used, W_SIN + m + 1)
                    act.activation(ffn[:, m * T:(m + 1) * T], acc[:, m % 2, 0:T], ACT.Copy).then_inc(u_ready, 1)
                    split_hi(W_SIN + m + SPL)
                    act.wait_ge(bt_done, m + 1)
                    act.activation(bpow_r[:, 0, m * 512:(m + 1) * 512], gv[:], ACT.Copy).then_inc(bt_act, 1)
                    act.wait_ge(st_done, m + 1)
                    if m >= 2:
                        act.wait_ge(v_done, m - 1)
                    act.activation(ust[:, m % 2, :, :].rearrange("p q j -> p (q j)"), acc[:, m % 2, T:2 * T],
                                   ACT.Copy).then_inc(st_ready, 1)
                    if m == 0:
                        lags_out()
                if m >= 2:
                    gelu(m - 2)
                if m == KT - 1:
                    for mt in range(KT - 2):
                        hi(mt)
                if m >= KT:
                    hi(m - 2)

            for m in range(KT):
                split_hi(W_GLU + 2 * m + SPL)
                act.wait_ge(slot_used, W_GLU + 2 * m + 1)
                if m >= 2:
                    act.wait_ge(glu_s, m - 1)
                act.activation(sg[:, m % 2, :], acc[:, 2 * (m % 2), 0:T], ACT.Sigmoid).then_inc(sig_ready, 1)
                if m < KT - 1:
                    split_hi(W_GLU + 2 * m + 1 + SPL)
                if m:
                    square(3, m - 1)
            fetch_root()
            square(3, KT - 1)
            root(3)
            split_hi(W_FFN1 + 2)
            norm_hi(3, 5, 48 + 24)
            ffn_phase(1, W_FFN1)
            fetch_root()
            for k in range(KT):
                square(4, k)
            root(4)

        @block.vector
        def _(dve):
            def split_lo(n, i=0):
                dve.wait_ge(hi_ready, n + RAW * i + 1)
                dve.tensor_tensor(wlo[:, n % SPL, :], raw[:, n % RAW, :], whi[:, n % SPL, :].bitcast(F32),
                                  ALU.subtract).then_inc(lo_ready, 1)

            def col_out(pair, i=0):
                dve.wait_ge(cols_done, pair + i + 1)
                dve.tensor_tensor(modc[:, ds(8 * (pair + i), 8)].rearrange("p (e q) -> p q e", e=2),
                                  misc[:, 0:8].rearrange("p (q e) -> p q e", e=2),
                                  modb[:, ds(8 * (pair + i), 8)].rearrange("p (e q) -> p q e", e=2),
                                  ALU.add).then_inc(mod_col, 1)

            def scale_columns(norm, sc):
                dve.wait_ge(mod_col, (sc + 8) // 8)
                dve.scalar_tensor_tensor(amul[:, norm, :], modc[:, sc:sc + KT], 1.0, gains[:, norm, :],
                                         ALU.add, ALU.mult).then_inc(amul_ready, 1)

            def normalise(norm):
                dve.wait_ge(rt_ready, norm + 1)
                dve.reciprocal(rt[:], rt[:]).then_inc(ri_norm, 1)
                dve.wait_ge(ri_norm, norm + 1)
                for h in range(2):
                    dve.tensor_scalar(diag[:, h, :], ident[:], rt[:, h:h + 1], None, ALU.mult).then_inc(diag_ready, 1)

            def scaled(norm, k, spread=misc[:, T:2 * T]):
                dve.scalar_tensor_tensor(tmp[:, k, :], x[:, k, :], amul[:, norm, k:k + 1], spread,
                                         ALU.mult, ALU.mult).then_inc(hp_ready, 1)

            def low_in(k, phase, sh):
                dve.wait_ge(act_hi, KT * phase + k + 1)
                dve.scalar_tensor_tensor(hl[:, k, :], tmp[:, k, :], modc[:, sh + k:sh + k + 1],
                                         hh[:, k, :].bitcast(F32), ALU.add, ALU.subtract).then_inc(act_lo, 1)

            def norm_out(norm, phase, sh, third=None):
                dve.wait_ge(amul_ready, norm + 1)
                dve.wait_ge(rstd_ready, norm + 1)
                scaled(norm, 0)
                scaled(norm, 1)
                for k in range(KT):
                    low_in(k, phase, sh)
                    if k + 2 < KT:
                        scaled(norm, k + 2)
                    if k == 3 and third is not None:
                        split_lo(third)

            dve.memset(gv[:], 0.0).then_inc(set_up, 1)
            dve.memset(zrow[:], 0.0).then_inc(set_up, 1)
            dve.memset(cond[:, :, 0], 0.0).then_inc(set_up, 1)
            dve.memset(cond[:, :, 2], 0.0).then_inc(set_up, 1)
            np_ = [0]

            def step(ins):
                ins.then_inc(prm_v, 1)
                np_[0] += 1
                dve.wait_ge(prm_v, np_[0])

            dve.wait_ge(prm_a, 1)
            step(dve.tensor_tensor(pr("t0"), pr("lr"), pr("dt"), ALU.mult))
            step(dve.tensor_tensor(pr("th"), pr("li"), pr("dt"), ALU.mult))
            for dst, quarter in (("t2", 0.0), ("t3", 0.25)):
                step(dve.tensor_scalar(pr("t1"), pr("th"), 1.0 / TWO_PI, quarter, ALU.mult, ALU.add))
                step(dve.tensor_scalar(pr("t1"), pr("t1"), ROUND, -ROUND, ALU.add, ALU.add))
                step(dve.scalar_tensor_tensor(pr(dst), pr("t1"), -C1, pr("th"), ALU.mult, ALU.add))
                step(dve.scalar_tensor_tensor(pr(dst), pr("t1"), -C2, pr(dst), ALU.mult, ALU.add))
                if quarter:
                    step(dve.tensor_scalar(pr("t1"), pr("t1"), -C3, TWO_PI / 4, ALU.mult, ALU.add))
                    step(dve.tensor_tensor(pr(dst), pr(dst), pr("t1"), ALU.add))
                else:
                    step(dve.scalar_tensor_tensor(pr(dst), pr("t1"), -C3, pr(dst), ALU.mult, ALU.add))
            pi_f = 3.1415925
            step(dve.tensor_scalar(pr("frac"), pr("t2"), LCH / TWO_PI, None, ALU.mult))
            step(dve.tensor_scalar(pr("t1"), pr("frac"), ROUND, -ROUND, ALU.add, ALU.add))
            step(dve.tensor_tensor(pr("frac"), pr("frac"), pr("t1"), ALU.subtract))
            step(dve.tensor_scalar(pr("t2"), pr("t2"), pi_f, -pi_f, ALU.min, ALU.max))
            step(dve.tensor_scalar(pr("t3"), pr("t3"), pi_f, -pi_f, ALU.min, ALU.max))
            dve.wait_ge(prm_a, 4)
            step(dve.tensor_tensor(pr("are"), pr("mag"), pr("cos"), ALU.mult))
            step(dve.tensor_tensor(pr("aim"), pr("mag"), pr("sin"), ALU.mult))
            step(dve.tensor_tensor(pr("t0"), pr("mag"), pr("mag"), ALU.mult))
            step(dve.tensor_tensor(pr("rho"), pr("t0"), pr("t0"), ALU.mult))
            step(dve.tensor_tensor(pr("t0"), pr("lr"), pr("lr"), ALU.mult))
            step(dve.tensor_tensor(pr("t1"), pr("li"), pr("li"), ALU.mult))
            step(dve.tensor_tensor(pr("t0"), pr("t0"), pr("t1"), ALU.add))
            step(dve.reciprocal(pr("t3"), pr("t0")))
            step(dve.tensor_scalar(pr("t2"), pr("are"), -1.0, None, ALU.add))
            step(dve.tensor_tensor(pr("t0"), pr("t2"), pr("lr"), ALU.mult))
            step(dve.tensor_tensor(pr("t1"), pr("aim"), pr("li"), ALU.mult))
            step(dve.tensor_tensor(pr("t0"), pr("t0"), pr("t1"), ALU.add))
            step(dve.tensor_tensor(pr("cre"), pr("t0"), pr("t3"), ALU.mult))
            step(dve.tensor_tensor(pr("t0"), pr("aim"), pr("lr"), ALU.mult))
            step(dve.tensor_tensor(pr("t1"), pr("t2"), pr("li"), ALU.mult))
            step(dve.tensor_tensor(pr("t0"), pr("t0"), pr("t1"), ALU.subtract))
            step(dve.tensor_tensor(pr("cim"), pr("t0"), pr("t3"), ALU.mult))

            assert np_[0] == PRM_STEPS
            dve.wait_ge(early_in, 16 * N_EARLY)
            col_out(0)
            scale_columns(0, 0)
            normalise(0)
            dve.wait_ge(amul_ready, 1)
            dve.wait_ge(rstd_ready, 1)
            for k in range(KT):
                scaled(0, k, up[:, 0, 0:T])
            col_out(1)
            split_lo(0)
            split_lo(1)
            for k in range(KT):
                low_in(k, 0, 8)
                if k == 3:
                    split_lo(2)

            for n in range(RAW):
                split_lo(n + SPL)
            dve.wait_ge(idx_done, 1)
            dve.tensor_scalar(wit, misc[:, 0:T].rearrange("p (q n) -> p q n", q=2)[:, :, 0:IH], float(IH) ** -0.5, None,
                              ALU.mult).then_inc(wit_ready, 1)
            dve.wait_ge(wit_ready, 1)
            for step, (qt, keys, off) in enumerate(((1, T, 0), (0, P, T))):
                dve.wait_ge(idx_relu, step + 1)
                for h in range(IH):
                    r = rbuf[:, h % 4, h // 4, 0:keys]
                    out = scr[:, off:off + keys]
                    if h == 0:
                        dve.tensor_scalar(out, r, wit[:, qt, h:h + 1], None, ALU.mult).then_inc(idx_acc, 1)
                    else:
                        dve.wait_ge(idx_acc, step * 8 + h)
                        dve.scalar_tensor_tensor(out, r, wit[:, qt, h:h + 1], out, ALU.mult, ALU.add).then_inc(idx_acc, 1)
            col_out(C_PROJ // 2)
            dve.wait_ge(idx_acc, 16)
            dve.memset(scr[0:64, 192:256], NEG).then_inc(sel, 1)
            dve.memset(scr[0:64, T + 64:T + P], NEG).then_inc(sel, 1)
            dve.wait_ge(sel, 2)
            def top_k(i, slots):
                for n in slots:
                    if n < 4:
                        dve.wait_ge(sel, 2 + 8 * (i - 1) + 2 * n)
                    split_lo(n + SPL, i)
                    for qt, off, keys in ((0, 0, T), (1, T, P)):
                        sc = scr[:, off:off + keys]
                        if n in (0, 2):
                            dve.max(max8[:, qt, :], sc).then_inc(sel, 1)
                        if n in (1, 3):
                            dve.match_replace(sc, max8[:, qt, :], sc, TAKEN).then_inc(sel, 1)

            with dve.Fori(1, N_IN // RAW - 1) as i:
                top_k(i, range(RAW))
            top_k(N_IN // RAW - 1, range(RAW - 1))
            dve.wait_ge(sel, 34)
            dve.tensor_scalar(msk, scr, TAKEN, MASKED, ALU.not_equal, ALU.mult).then_inc(sel, 1)
            dve.wait_ge(sel, 35)

            dve.wait_ge(small_in, 16 * N_SMALL)
            def masked(p, a):
                for e in range(2):
                    dve.scalar_tensor_tensor(bm[:, a, e, :], ndist, slope[:, ds(2 * p + e, 1)], msk,
                                             ALU.mult, ALU.add).then_inc(bias_ready, 1)
                dve.wait_ge(s_done, p + 1)
                if not (isinstance(p, int) and p < 2):
                    dve.wait_ge(tr_done, p - 1)
                for e in range(2):
                    dve.wait_ge(bias_ready, 2 * p + e + 1)
                    dve.scalar_tensor_tensor(sp[:, a, e, :], acc[:, 2 * a + e, 0:384], HD ** -0.5, bm[:, a, e, :],
                                             ALU.mult, ALU.add).then_inc(sp_ready, 1)
                dve.wait_ge(sp_ready, 2 * p + 2)
                dve.tensor_reduce(nmx[:, a, 0:2], sp[:, a, :, 0:T], AX.X, ALU.max, negate=True).then_inc(mx_ready, 1)
                dve.tensor_reduce(nmx[:, a, 2:4], sp[:, a, :, T:T + P], AX.X, ALU.max, negate=True).then_inc(mx_ready, 1)

            def v_out(p, a):
                if not (isinstance(p, int) and p < 2):
                    dve.wait_ge(pv_done, p - 1)
                dve.tensor_copy(vsb[:, a, :, :], acc[:, 2 * a:2 * a + 2, 384:512]).then_inc(v_ready, 1)

            def normed(p, a):
                dve.wait_ge(exp_done, 4 * (p + 1))
                dve.reciprocal(ri[:, a, :], rs[:, a, :]).then_inc(ri_ready, 1)
                dve.wait_ge(ri_ready, p + 1)
                for e in range(2):
                    dve.tensor_scalar(sp[:, a, e, 0:T], sp[:, a, e, 0:T], ri[:, a, e:e + 1], None,
                                      ALU.mult).then_inc(p_ready, 1)
                    dve.tensor_scalar(sp[:, a, e, T:T + P], sp[:, a, e, T:T + P], ri[:, a, 2 + e:3 + e], None,
                                      ALU.mult).then_inc(p_ready, 1)

            def out_low(p):
                dve.wait_ge(act_hi, KT + p + 1)
                dve.tensor_tensor(hl_f[:, ds(p * T, T)].rearrange("p (b t) -> p b t", b=2), up[:, :, 384:512],
                                  hh_f[:, ds(p * T, T)].bitcast(F32).rearrange("p (b t) -> p b t", b=2),
                                  ALU.subtract).then_inc(act_lo, 1)

            masked(0, 0)
            v_out(0, 0)
            masked(1, 1)
            normed(0, 0)
            v_out(1, 1)
            split_lo(N_IN + SPL - 1)
            masked(2, 0)
            out_low(0)
            normed(1, 1)
            v_out(2, 0)
            col_out(C_ATT // 2)
            with dve.Fori(0, 2) as i:
                for h in range(2):
                    masked(2 * i + 3 + h, (1 + h) % 2)
                    out_low(2 * i + 1 + h)
                    normed(2 * i + 2 + h, h % 2)
                    v_out(2 * i + 3 + h, (1 + h) % 2)
                    if h:
                        col_out(C_ATT // 2 + 1, i)
            for p in range(6, PAIRS):
                if p + 1 < PAIRS:
                    masked(p + 1, (p + 1) % 2)
                out_low(p - 1)
                normed(p, p % 2)
                if p + 1 < PAIRS:
                    v_out(p + 1, (p + 1) % 2)
                if p == 7:
                    col_out((C_ATT + p - 1) // 2)
            out_low(PAIRS - 1)
            scale_columns(1, 32)
            dve.wait_ge(mod_col, CH // 2)

            def residual(psum, k, gate):
                dve.scalar_tensor_tensor(x[:, k, :], psum, modc[:, gate + k:gate + k + 1], x[:, k, :],
                                         ALU.mult, ALU.add).then_inc(x_upd, 1)

            for m in range(KT):
                dve.wait_ge(slot_used, W_OUT + m + 1)
                residual(acc[:, m % 4, 0:T], m, 16)
                if m < KT - 1:
                    split_lo(W_OUT + m + SPL)
            normalise(1)
            norm_out(1, 2, 24, W_FFN0 + 2)

            def ffn_phase(layer, base):
                def conv_rest(par, s, cnt):
                    dve.wait_ge(tap, 2 * (cnt + 1))
                    for back in range(2):
                        for e in range(2):
                            if back:
                                dve.wait_ge(conv_s, 4 * cnt + e + 1)
                            w = conv[:, layer, 1 - back, ds(s + e * FT, 1)]
                            dve.scalar_tensor_tensor(cb[:, par, e, 1 + back:T], up[:, par, e * T:e * T + T - 1 - back], w,
                                                     cb[:, par, e, 1 + back:T], ALU.mult, ALU.add).then_inc(conv_s, 1)

                def gate(par, cnt):
                    dve.wait_ge(sg_ready, cnt + 1)
                    dve.tensor_tensor(ab[:, par, :], sg[:, par, :], cb[:, par, 0, :], ALU.mult).then_inc(am, 1)

                def low(par, cnt):
                    dve.wait_ge(a_hi, cnt + 1)
                    dve.tensor_tensor(al[:, par, :], ab[:, par, :], ah[:, par, :].bitcast(F32),
                                      ALU.subtract).then_inc(a_lo, 1)

                off = FT * layer

                def step(h, s, c, i=0, extra=None):
                    conv_rest(h, s, off + s)
                    if c + 2 < N_SLOTS:
                        split_lo(c + 2, i)
                    gate(h, off + s)
                    low(h, off + s)
                    if extra is not None:
                        col_out(C_FFN // 2, extra)
                    if c + 4 < base + N_FFN:
                        split_lo(c + 3, i)
                        split_lo(c + 4, i)

                split_lo(base + 3)
                conv_rest(0, 0, off)
                split_lo(base + 4)
                gate(0, off)
                low(0, off)
                split_lo(base + 5)
                conv_rest(1, 1, off + 1)
                split_lo(base + 6)
                gate(1, off + 1)
                low(1, off + 1)
                split_lo(base + 7)
                def two_steps(i, extra=None):
                    for h in range(2):
                        step(h, 2 * i + 2 + h, base + 6 + 3 * h, i, extra if h else None)

                if layer == 0:
                    with dve.Fori(0, 4) as i:
                        two_steps(2 * i)
                        two_steps(2 * i + 1, i)
                    two_steps(8)
                else:
                    with dve.Fori(0, 9) as i:
                        two_steps(i)
                for h in range(2):
                    step(h, 20 + h, base + 60 + 3 * h, 0, 4 if layer == 0 and h else None)
                if layer == 0:
                    split_lo(W_SIN)
                for k in range(KT):
                    if k < KT - 2:
                        dve.wait_ge(fold_done, 3 * layer + k // 2 + 1)
                    else:
                        dve.wait_ge(slot_used, base + N_FFN)
                    residual(acc[:, k // 2, (k % 2) * T:(k % 2 + 1) * T], k, 48 * layer + 40)

            ffn_phase(0, W_FFN0)
            scale_columns(2, 48)
            scale_columns(3, 48 + 32)
            split_lo(W_SIN + 1)
            split_lo(W_SIN + 2)
            normalise(2)
            norm_out(2, 3, 56)
            def lags_out():
                dve.wait_ge(k_done, 1)
                dve.wait_ge(kz, 1)
                for q in (0, 2):
                    rows = slice(32 * q, 32 * q + 32)
                    dve.tensor_copy(kbd[rows, :, :, 32 * q:32 * q + 32],
                                    up[rows, :, :].rearrange("p b (m l n) -> p (b m) l n", m=4, l=LCH)).then_inc(k_out, 1)

            dve.wait_ge(tab_ready, 1)

            def turn_in(mt):
                dve.wait_ge(v_done, mt + 1)
                if mt:
                    dve.wait_ge(g2_ready, 8 * mt)
                pairs = slice(4 * mt, 4 * mt + 4)
                v = acc[:, 2 + mt % 2, :].rearrange("p (q r j) -> p q r j", q=4, r=2)
                shape = [P, 4, 2, NJ]
                dve.tensor_tensor(va, v, tcos_v[:, pairs, :].unsqueeze(2).broadcast_to(shape), ALU.mult).then_inc(v_read, 1)
                dve.tensor_tensor(vb, v, tsin_v[:, pairs, :].unsqueeze(2).broadcast_to(shape), ALU.mult).then_inc(v_read, 1)
                dve.wait_ge(v_read, 2 * mt + 2)
                dve.tensor_tensor(va[:, :, 0, :], va[:, :, 0, :], vb[:, :, 1, :], ALU.add).then_inc(g_ready, 1)
                dve.tensor_tensor(va[:, :, 1, :], va[:, :, 1, :], vb[:, :, 0, :], ALU.subtract).then_inc(g_ready, 1)
                dve.wait_ge(g_ready, 2 * mt + 2)
                if mt:
                    dve.wait_ge(rot_s, 2 * mt)
                for q in range(4):
                    for r in range(2):
                        p_ = 4 * mt + q
                        dve.tensor_tensor_scan(g2[:, r, q, :],
                                               prm[:, PRM.index("rho"), p_:p_ + 1].broadcast_to([P, NJ]),
                                               va[:, q, r, :], 0.0, ALU.mult, ALU.add).then_inc(g2_ready, 1)

            def skip(mt):
                dve.wait_ge(y_done, mt + 1)
                if mt >= 2:
                    dve.wait_ge(yg_ready, mt - 1)
                dve.scalar_tensor_tensor(yv[:, mt % 2, :], ffn[:, mt * T:(mt + 1) * T], dcol[:, mt:mt + 1],
                                         up[:, mt % 2, 0:T], ALU.mult, ALU.add).then_inc(yv_ready, 1)

            def low(mt):
                dve.wait_ge(act_hi, 4 * KT + mt + 1)
                dve.tensor_tensor(hl[:, mt, :], yg[:, mt, :], hh[:, mt, :].bitcast(F32),
                                  ALU.subtract).then_inc(act_lo, 1)

            for m in range(KT + 2):
                if m < KT:
                    if m:
                        split_lo(W_SIN + m + SPL)
                    dve.wait_ge(bt_done, m + 1)
                    dve.tensor_copy(bpow_r[:, 1, m * 512:(m + 1) * 512], misc[:]).then_inc(bt_dve, 1)
                    if m == 0:
                        split_lo(W_SIN + SPL)
                        lags_out()
                if m == KT:
                    low(0)
                    low(1)
                if 1 <= m <= KT:
                    turn_in(m - 1)
                if m == KT:
                    low(2)
                if m == KT + 1:
                    for mt in range(3, KT - 1):
                        low(mt)
                if m >= 2:
                    skip(m - 2)
            dve.wait_ge(bt_act, KT)
            dve.memset(gv[:], 0.0).then_inc(set_up, 1)
            low(KT - 1)

            for m in range(KT):
                split_lo(W_GLU + 2 * m + SPL)
                dve.wait_ge(sig_ready, m + 1)
                dve.wait_ge(slot_used, W_GLU + 2 * m + 2)
                dve.tensor_tensor(ab[:, m % 2, :], sg[:, m % 2, :], acc[:, 2 * (m % 2) + 1, 0:T], ALU.mult).then_inc(glu_s, 1)
                dve.wait_ge(glu_s, m + 1)
                dve.scalar_tensor_tensor(x[:, m, :], ab[:, m % 2, :], modc[:, 64 + m:65 + m], x[:, m, :],
                                         ALU.mult, ALU.add).then_inc(x_upd, 1)
                if m < KT - 1:
                    split_lo(W_GLU + 2 * m + 1 + SPL)
            normalise(3)
            norm_out(3, 5, 48 + 24, W_FFN1 + 2)
            ffn_phase(1, W_FFN1)
            normalise(4)
            dve.wait_ge(rstd_ready, 5)
            for k in range(KT):
                dve.scalar_tensor_tensor(tmp[:, k, :], x[:, k, :], gains[:, 4, k:k + 1], misc[:, T:2 * T],
                                         ALU.mult, ALU.mult).then_inc(fin_ready, 1)

        @block.gpsimd
        def _(pool):
            tabs = [0]

            def tab_step(ins):
                ins.then_inc(tab_arg, 1)
                tabs[0] += 1
                if tabs[0] < TAB_STEPS:
                    pool.wait_ge(tab_arg, tabs[0])

            turns = arena[:, 13 * 1024:15 * 1024]
            ang = turns.rearrange("p (n j) -> p n j", j=NJ)
            shape = [P, PR, NJ]
            pool.wait_ge(prm_v, PRM_SIN)
            tab_step(pool.tensor_tensor(ang, pr("frac").unsqueeze(2).broadcast_to(shape),
                                        jrow[:].unsqueeze(1).broadcast_to(shape), ALU.mult))
            tab_step(pool.tensor_scalar(tsin, turns, ROUND, -ROUND, ALU.add, ALU.add))
            tab_step(pool.tensor_tensor(tsin, turns, tsin, ALU.subtract))
            tab_step(pool.tensor_scalar(turns, turns, 0.25, None, ALU.add))
            tab_step(pool.tensor_scalar(tcos, turns, ROUND, -ROUND, ALU.add, ALU.add))
            tab_step(pool.tensor_tensor(tcos, turns, tcos, ALU.subtract))
            for j, s in enumerate((S_Q, S_K, S_V)):
                for a in range(2):
                    pool.wait_ge(qkv_ready, s + a + 1)
                    pool.tensor_copy(stage[:, a, j, :], qkv[:, s + a, :]).then_inc(stage_ready, 1)
            pool.wait_ge(qkv_ready, N_IN)
            with pool.Fori(1, PAIRS // 2) as i:
                for a in range(2):
                    pool.wait_ge(s_done, 2 * i + a - 1)
                    for j, s in enumerate((S_Q, S_K, S_V)):
                        pool.tensor_copy(stage[:, a, j, :], qkv_f[:, ds((s + a + 2 * i) * T, T)]).then_inc(stage_ready, 1)

            cnt = [0]

            def step(ins):
                ins.then_inc(pw, 1)
                cnt[0] += 1
                pool.wait_ge(pw, cnt[0])

            def wide(name):
                return pr(name).unsqueeze(2).broadcast_to([P, PR, 32])

            def w3(a):
                return a.rearrange("p (n c) -> p n c", c=32)

            def b_at(k):
                return bpow[:, :, :, LCH - 1 - k, :]

            def c_at(k):
                return cpow[:, k].rearrange("p r (n c) -> p r n c", c=32)

            def times(dst, src, re, im, minus_im):
                ops = (ALU.subtract, ALU.add) if not minus_im else (ALU.add, ALU.subtract)
                step(pool.tensor_tensor(w3(t1), src[:, 0], wide(re), ALU.mult))
                step(pool.tensor_tensor(w3(t2), src[:, 1], wide(im), ALU.mult))
                step(pool.tensor_tensor(dst[:, 0], w3(t1), w3(t2), ops[0]))
                step(pool.tensor_tensor(w3(t1), src[:, 1], wide(re), ALU.mult))
                step(pool.tensor_tensor(w3(t2), src[:, 0], wide(im), ALU.mult))
                step(pool.tensor_tensor(dst[:, 1], w3(t1), w3(t2), ops[1]))

            pool.wait_ge(act_lo, 16)
            for ri_, name in ((0, "b_re"), (1, "b_im")):
                pool.dma_start(cpow[:, 1, ri_, :], t[name]).then_inc(ssm_in, 16)
            for ri_, name in ((0, "c_re"), (1, "c_im")):
                pool.dma_start(cpow[:, 0, ri_, :], t[name]).then_inc(ssm_in, 16)
            pool.wait_ge(prm_v, PRM_STEPS)
            pool.wait_ge(ssm_in, 16 * N_SSM)
            times(b_at(0), c_at(1), "cre", "cim", False)
            for k in range(3):
                times(b_at(k + 1), b_at(k), "are", "aim", False)
            step(pool.tensor_scalar(cpow[:, 0, 1, :], cpow[:, 0, 1, :], -1.0, None, ALU.mult))
            for k in range(3):
                times(c_at(k + 1), c_at(k), "are", "aim", True)
            assert cnt[0] == PW_K
            pool.wait_ge(mod_used, 2 * CH * MS)
            pool.memset(mraw[:].rearrange("p a b -> p (a b)"), 0.0).then_inc(kz, 1)
            pool.wait_ge(k_done, 1)
            times(c_at(0), c_at(3), "are", "aim", True)
            assert cnt[0] == PW_ALL
            step(pool.memset(hst[:, :, :, 0:1], 0.0))
            pool.wait_ge(tab_ready, 1)
            for mt in range(KT):
                pool.wait_ge(g2_ready, 8 * (mt + 1))
                pairs = slice(4 * mt, 4 * mt + 4)
                sh4 = [P, 2, 4, NJ]
                pool.tensor_tensor(rot1, g2, tcos_v[:, pairs, :].unsqueeze(1).broadcast_to(sh4), ALU.mult).then_inc(rot_s, 1)
                pool.tensor_tensor(rot2, g2, tsin_v[:, pairs, :].unsqueeze(1).broadcast_to(sh4), ALU.mult).then_inc(rot_s, 1)
                pool.wait_ge(rot_s, 2 * mt + 2)
                if mt:
                    pool.wait_ge(y_done, mt)
                pool.tensor_tensor(hst[:, 0, :, 1:NJ], rot1[:, 0, :, 0:NJ - 1], rot2[:, 1, :, 0:NJ - 1],
                                   ALU.subtract).then_inc(h_ready, 1)
                pool.tensor_tensor(hst[:, 1, :, 1:NJ], rot1[:, 1, :, 0:NJ - 1], rot2[:, 0, :, 0:NJ - 1],
                                   ALU.add).then_inc(h_ready, 1)
                pool.wait_ge(h_ready, 2 * mt + 2)


PRM_SIN = 18
PRM_STEPS = 35
TAB_STEPS = 6
PW_K = 4 * 6 + 1 + 3 * 6
PW_ALL = PW_K + 6


def _weights(a):
    k, m = a.shape
    return a.reshape(k // P, P, m // P, P).transpose(2, 1, 0, 3).reshape(m // P, P, k * P // P)


def _ffn_weights(up, down):
    u, d = _weights(up), down.reshape(FT, P, D)
    order = [u[0], u[FT], u[1], u[FT + 1]]
    for s in range(2, FT):
        order += [u[s], u[FT + s], d[s - 2]]
    return order + [d[FT - 2], d[FT - 1]]


def _columns(a):
    a = a.reshape(*a.shape[:-1], a.shape[-1] // P, P)
    return np.moveaxis(a, -1, 0)


def _pairs(a):
    return a.reshape(PR, 2, 64).transpose(1, 2, 0).reshape(P, PR)


def _blocks(a):
    out = np.zeros((2, 64, PR, 2, 16), a.dtype)
    v = a.reshape(PR, 2, 64, 16)
    for g in range(2):
        out[g, :, :, g, :] = v[:, g].transpose(1, 0, 2)
    return out.reshape(P, 1024)


def layout(i):
    f = np.float32
    w_in = i["attn_w_in"][0]
    qi0 = 3 * D
    ki0 = qi0 + IH * HD
    ki, wi = w_in[:, ki0:ki0 + HD], w_in[:, ki0 + HD:]
    w_first = np.concatenate([ki, ki, wi, np.zeros((D, P - IH), f), w_in[:, qi0:ki0], w_in[:, 0:qi0]], axis=1)
    glu = _weights(i["ssm_w_glu"][0])
    glu = glu.reshape(2, KT, P, D)[::-1].transpose(1, 0, 2, 3).reshape(N_GLU, P, D)
    stream = [*_weights(w_first), *_weights(i["attn_w_out"][0]),
              *_ffn_weights(i["ffn_w_up"][0], i["ffn_w_down"][0]), *_weights(i["ssm_w_in"][0]), *glu,
              *_ffn_weights(i["ffn_w_up"][1], i["ffn_w_down"][1])]
    order = [1, 0, 2, 3, 4, 5]
    mod_w = i["mod_w"].reshape(2, D, 6, D)[:, :, order].reshape(2, D, 6 * D)
    mod_b = i["mod_b"].reshape(2, 6, D)[:, order].reshape(2, 6 * D)
    mw = mod_w.reshape(2, MS, 2, P, CH, 512).transpose(0, 4, 1, 3, 2, 5).reshape(2 * CH * MS, P, 1024)
    q = np.arange(P)[:, None]
    ndist = -np.abs(np.concatenate([q + P - np.arange(T)[None], q - np.arange(P)[None]], axis=1)).astype(f)
    conv = np.concatenate([i["ffn_conv_w"], i["ffn_conv_b"][:, None]], axis=1)
    slopes = (2.0 ** (-8.0 * np.arange(1, HEADS + 1, dtype=f) / HEADS)).astype(f)
    return {
        "w": np.stack(stream),
        "mw": mw,
        "x": i["x"][0].T.reshape(KT, P, T).transpose(1, 0, 2),
        "cond": _columns(i["c"][0]),
        "modb": _columns(mod_b).reshape(P, 96),
        "ident": np.eye(P, dtype=f),
        "ones": np.ones((P, P), f),
        "picks": np.stack([np.arange(P) % 32 == 0, np.arange(P) % 32 == 1], axis=1).astype(f),
        "prm": np.stack([_pairs(i["ssm_lam_re"][0]), _pairs(i["ssm_lam_im"][0]),
                         _pairs(np.repeat(i["ssm_log_dt"][0][:, None], 64, axis=1))], axis=1),
        "conv": _columns(conv),
        "gains": _columns(np.stack([i["norm_mix_g"][0], i["norm_ffn_g"][0], i["norm_mix_g"][1], i["norm_ffn_g"][1],
                                    i["final_g"]])),
        "dcol": _columns(i["ssm_d"][0].reshape(D)),
        "jrow": np.repeat(np.arange(NJ, dtype=f)[None], P, axis=0),
        "slope": np.repeat(slopes[None], P, axis=0),
        "epsc": np.full((P, 1), EPS, f),
        "ndist": ndist,
        "b_re": _blocks(i["ssm_b_re"][0]),
        "b_im": _blocks(i["ssm_b_im"][0]),
        "c_re": _blocks(i["ssm_c_re"][0].transpose(0, 2, 1)),
        "c_im": _blocks(i["ssm_c_im"][0].transpose(0, 2, 1)),
    }


def kernel(**inputs):
    import concourse.bacc as bacc
    from concourse.bass_utils import run_bass_kernel_spmd

    nc = bacc.Bacc("TRN2", target_bir_lowering=False, num_devices=1)
    given = {k: np.asarray(v) for k, v in inputs.items()}
    arrays, tensors = {}, {}
    for name, a in layout(given).items():
        a = np.ascontiguousarray(a)
        arrays[f"in_{name}"] = a
        tensors[name] = nc.dram_tensor(f"in_{name}", a.shape, mybir.dt.from_np(a.dtype), kind="ExternalInput").ap()
    tensors["out"] = nc.dram_tensor("out_0", (P, KT, T), F32, kind="ExternalOutput").ap()
    build(nc, tensors)
    r = run_bass_kernel_spmd(nc, [arrays], core_ids=[0])
    y = r.results[0]["out_0"]
    return np.ascontiguousarray(y.transpose(1, 0, 2).reshape(D, T).T).reshape(1, T, D)
```
